# Optimizing a Trainium2 kernel written in Bass

```python
import math
import jax
import jax.numpy as jnp
from jax import lax
import numpy as np

D_MODEL = 1024
BATCH = 1
SEQ = 1024
DEPTH = 1

CTX_LEN = 256
GRID_W = 64
N_BRANCH = 4
BRANCH_W = D_MODEL // N_BRANCH
NA_HEADS = 4
NA_DIM = BRANCH_W // NA_HEADS
NA_WIN_H = 8
NA_WIN_W = 16
NA_QB = 16
NA_KB = 32
DA_HEADS = 4
DA_QK_DIM = BRANCH_W // (2 * DA_HEADS)
DA_V_DIM = 2 * DA_QK_DIM
DA_QBLOCK = 128
ROPE_BASE = 10000.0
GDN_HEADS = 4
GDN_DIM = BRANCH_W // GDN_HEADS
GDN_CONV = 5
GDN_CHUNK = 64
FNET_GROUPS = 4
FNET_GROUP_W = BRANCH_W // FNET_GROUPS
N_EXPERTS = 16
N_GROUPS = 4
TOP_K = 2
D_FF = 512
MOE_BLOCK = 128
RMS_EPS = 1e-6
NEG_INF = -1e30
IN_SPLITS = (3 * BRANCH_W, 3 * BRANCH_W, 3 * BRANCH_W, BRANCH_W, 4 * GDN_HEADS, BRANCH_W, N_BRANCH * D_MODEL)
D_IN = sum(IN_SPLITS)

kernel_name = 'hybrid_diffusion_trunk'

def rmsnorm(x, g):
    xf = x.astype(jnp.float32)
    y = xf * lax.rsqrt(jnp.mean(xf * xf, axis=-1, keepdims=True) + RMS_EPS)
    return (y * g.astype(jnp.float32)).astype(x.dtype)

def l2norm(x):
    xf = x.astype(jnp.float32)
    return xf * lax.rsqrt(jnp.sum(xf * xf, axis=-1, keepdims=True) + RMS_EPS)

def modulate(h, shift, scale):
    return h * (1.0 + scale) + shift

def softmax_f32(s):
    return jax.nn.softmax(s.astype(jnp.float32), axis=-1)

def split_cols(p):
    outs, o = [], 0
    for w in IN_SPLITS:
        outs.append(p[..., o:o + w])
        o += w
    return outs

def rope_2d(x, rows, cols):
    nf = x.shape[-1] // 4
    freqs = ROPE_BASE ** (-jnp.arange(nf, dtype=jnp.float32) / nf)
    ang = jnp.stack([rows[:, None] * freqs, cols[:, None] * freqs], axis=1)
    cos = jnp.cos(ang)[None, :, None, None]
    sin = jnp.sin(ang)[None, :, None, None]
    xf = x.astype(jnp.float32).reshape(*x.shape[:-1], 2, 2, nf)
    x1, x2 = xf[..., 0, :], xf[..., 1, :]
    out = jnp.stack([x1 * cos - x2 * sin, x2 * cos + x1 * sin], axis=-2)
    return out.reshape(x.shape).astype(x.dtype)

def dense_ctx_attention(qc, kc, vc):
    p = softmax_f32(jnp.einsum('bqhd,bkhd->bhqk', qc, kc) * qc.shape[-1] ** -0.5)
    return jnp.einsum('bhqk,bkhd->bqhd', p.astype(vc.dtype), vc)

def neighbourhood_attention(q, k, v, qc, kc, vc, rpb, ctx_out):
    B, S, H, Dh = q.shape
    L = qc.shape[1]
    rows = S // GRID_W
    wh = min(NA_WIN_H, rows)
    ncb = GRID_W // NA_QB
    scale = Dh ** -0.5
    r = jnp.arange(rows)
    row_idx = jnp.clip(r - wh // 2, 0, rows - wh)[:, None] + jnp.arange(wh)[None, :]
    qcol = jnp.arange(GRID_W).reshape(ncb, NA_QB)
    col_idx = jnp.clip(qcol[:, 0] - NA_WIN_W // 2, 0, GRID_W - NA_KB)[:, None] + jnp.arange(NA_KB)[None, :]
    win_start = jnp.clip(qcol - NA_WIN_W // 2, 0, GRID_W - NA_WIN_W)
    rel = col_idx[:, None, :] - win_start[..., None]
    col_mask = (rel >= 0) & (rel < NA_WIN_W)
    rel_r = row_idx - r[:, None] + NA_WIN_H - 1
    rel_c = jnp.clip(col_idx[:, None, :] - qcol[..., None] + NA_WIN_W - 1, 0, 2 * NA_WIN_W - 2)
    bias = rpb.astype(jnp.float32)[:, rel_r[:, None, None, :, None], rel_c[None, :, :, None, :]]
    bias = jnp.where(col_mask[None, None, :, :, None, :], bias, NEG_INF)
    nk = wh * NA_KB
    bias = bias.reshape(H, rows, ncb, NA_QB, nk)
    kw = k.reshape(B, rows, GRID_W, H, Dh)[:, row_idx[:, None, :, None], col_idx[None, :, None, :]]
    vw = v.reshape(B, rows, GRID_W, H, Dh)[:, row_idx[:, None, :, None], col_idx[None, :, None, :]]
    kw = kw.reshape(B, rows, ncb, nk, H, Dh)
    vw = vw.reshape(B, rows, ncb, nk, H, Dh)
    qb = q.reshape(B, rows, ncb, NA_QB, H, Dh)
    s_loc = jnp.einsum('brjqhd,brjkhd->bhrjqk', qb, kw).astype(jnp.float32) * scale + bias[None]
    s_ctx = jnp.einsum('brjqhd,bchd->bhrjqc', qb, kc).astype(jnp.float32) * scale
    p = softmax_f32(jnp.concatenate([s_loc, s_ctx], axis=-1)).astype(v.dtype)
    o = (jnp.einsum('bhrjqk,brjkhd->brjqhd', p[..., :nk], vw)
         + jnp.einsum('bhrjqc,bchd->brjqhd', p[..., nk:], vc)).reshape(B, S, H * Dh)
    o_c = dense_ctx_attention(qc, kc, vc).reshape(B, L, H * Dh) if ctx_out else None
    return o, o_c

def diff_attention(q, k, v, qc, kc, vc, lam, ctx_out):
    B, S, H, _, dq = q.shape
    scale = dq ** -0.5
    k_all = jnp.concatenate([k, kc], axis=1)
    v_all = jnp.concatenate([v, vc], axis=1)
    nb = S // DA_QBLOCK
    qb = jnp.moveaxis(q.reshape(B, nb, DA_QBLOCK, H, 2, dq), 1, 0)

    def block(qblk):
        p = softmax_f32(jnp.einsum('bqhmd,bkhmd->bhmqk', qblk, k_all) * scale)
        a = p[:, :, 0] - lam * p[:, :, 1]
        return jnp.einsum('bhqk,bkhd->bqhd', a.astype(v_all.dtype), v_all)

    o = jnp.moveaxis(lax.map(block, qb), 0, 1).reshape(B, S, H, v.shape[-1])
    o_c = None
    if ctx_out:
        p = softmax_f32(jnp.einsum('bqhmd,bkhmd->bhmqk', qc, kc) * scale)
        a = p[:, :, 0] - lam * p[:, :, 1]
        o_c = jnp.einsum('bhqk,bkhd->bqhd', a.astype(vc.dtype), vc)
    return o, o_c

def short_conv(x, w):
    K = w.shape[0]
    pad = K // 2
    T = x.shape[1]
    xp = jnp.pad(x, ((0, 0), (pad, pad), (0, 0)))
    y = xp[:, 0:T] * w[0]
    for i in range(1, K):
        y = y + xp[:, i:i + T] * w[i]
    return jax.nn.silu(y)

def gdn_prepare(qkv, ab, conv_w, a_log, dt_bias):
    B, T, _ = qkv.shape
    q, k, v = jnp.split(short_conv(qkv, conv_w), 3, axis=-1)
    to_heads = lambda u: jnp.moveaxis(u.reshape(B, T, GDN_HEADS, GDN_DIM), 1, 2)
    q = l2norm(to_heads(q)) * GDN_DIM ** -0.5
    k = l2norm(to_heads(k))
    v = to_heads(v).astype(jnp.float32)
    abf = ab.astype(jnp.float32).reshape(B, T, 2, 2, GDN_HEADS)
    g = -jnp.exp(a_log.astype(jnp.float32)) * jax.nn.softplus(abf[:, :, 0] + dt_bias.astype(jnp.float32))
    beta = jax.nn.sigmoid(abf[:, :, 1])
    g = jnp.transpose(g, (2, 0, 3, 1))
    beta = jnp.transpose(beta, (2, 0, 3, 1))
    return q, k, v, g, beta

def gdn_chunked(q, k, v, g, beta, s0):
    B, H, T, dk = q.shape
    dv = v.shape[-1]
    C = GDN_CHUNK
    N = T // C
    q, k, v = (u.reshape(B, H, N, C, -1) for u in (q, k, v))
    g = g.reshape(B, H, N, C)
    beta = beta.reshape(B, H, N, C)
    G = jnp.cumsum(g, axis=-1)
    incl = jnp.tril(jnp.ones((C, C), dtype=bool))
    strict = jnp.tril(jnp.ones((C, C), dtype=bool), -1)
    decay = jnp.where(incl, jnp.exp(jnp.where(incl, G[..., :, None] - G[..., None, :], 0.0)), 0.0)
    kb = k * beta[..., None]
    a = jnp.where(strict, jnp.einsum('bhnid,bhnjd->bhnij', kb, k) * decay, 0.0)
    lhs = a + jnp.eye(C, dtype=a.dtype)
    u = lax.linalg.triangular_solve(lhs, v * beta[..., None], left_side=True, lower=True, unit_diagonal=True)
    w = lax.linalg.triangular_solve(lhs, kb * jnp.exp(G)[..., None], left_side=True, lower=True, unit_diagonal=True)
    qk = jnp.where(incl, jnp.einsum('bhnid,bhnjd->bhnij', q, k) * decay, 0.0)
    q_dec = q * jnp.exp(G)[..., None]
    k_dec = k * jnp.exp(G[..., -1:] - G)[..., None]
    g_last = jnp.exp(G[..., -1])

    def step(S, xs):
        qk_c, qd_c, kd_c, u_c, w_c, gl_c = xs
        v_new = u_c - jnp.einsum('bhcd,bhde->bhce', w_c, S)
        o = jnp.einsum('bhcd,bhde->bhce', qd_c, S) + jnp.einsum('bhij,bhje->bhie', qk_c, v_new)
        S = S * gl_c[..., None, None] + jnp.einsum('bhcd,bhce->bhde', kd_c, v_new)
        return S, o

    xs = tuple(jnp.moveaxis(t, 2, 0) for t in (qk, q_dec, k_dec, u, w, g_last))
    s_final, o = lax.scan(step, s0, xs)
    return jnp.moveaxis(o, 0, 2).reshape(B, H, T, dv), s_final

def gdn_mixer(qkv, ab, z, qkv_c, ab_c, z_c, conv_w, a_log, dt_bias, onorm_g, ctx_out):
    ql, kl, vl, gl, bl = gdn_prepare(qkv, ab, conv_w, a_log, dt_bias)
    qc, kc, vc, gc, bc = gdn_prepare(qkv_c, ab_c, conv_w, a_log, dt_bias)
    B = qkv.shape[0]
    s0 = jnp.zeros((B, GDN_HEADS, GDN_DIM, GDN_DIM), jnp.float32)
    o_lat, o_ctx = 0.0, 0.0
    for d in range(2):
        fl = (lambda u: jnp.flip(u, axis=2)) if d == 1 else (lambda u: u)
        oc, s_ctx = gdn_chunked(fl(qc), fl(kc), fl(vc), fl(gc[d]), fl(bc[d]), s0)
        ol, _ = gdn_chunked(fl(ql), fl(kl), fl(vl), fl(gl[d]), fl(bl[d]), s_ctx)
        o_lat = o_lat + fl(ol)
        if ctx_out:
            o_ctx = o_ctx + fl(oc)

    def gate_out(o, zz):
        Bq, H, T, dv = o.shape
        y = rmsnorm(jnp.moveaxis(o, 1, 2), onorm_g) * jax.nn.silu(zz.reshape(Bq, T, H, dv).astype(jnp.float32))
        return y.reshape(Bq, T, H * dv).astype(zz.dtype)

    return gate_out(o_lat, z), (gate_out(o_ctx, z_c) if ctx_out else None)

def fourier_mix(f):
    B, T, _ = f.shape
    fg = f.astype(jnp.float32).reshape(B, T, FNET_GROUPS, FNET_GROUP_W)
    y = jnp.real(jnp.fft.fft2(fg, axes=(1, 3), norm='ortho'))
    return y.reshape(B, T, BRANCH_W).astype(f.dtype)

def merge_branches(branches, gate_in, w_branch, w_out):
    br = jnp.stack(branches, axis=2)
    proj = jnp.einsum('btiw,iwd->btid', br, w_branch)
    gates = jax.nn.sigmoid(gate_in.reshape(*gate_in.shape[:2], N_BRANCH, D_MODEL))
    return jnp.sum(gates * proj, axis=2) @ w_out

def token_mixers(h, hc, w_in, na_qn_g, na_kn_g, na_rpb, da_qn_g, da_kn_g, da_lam_q1, da_lam_k1,
                 da_lam_q2, da_lam_k2, da_subln_g, gdn_conv_w, gdn_a_log, gdn_dt_bias, gdn_onorm_g,
                 w_branch, w_out, lam_init, ctx_out):
    B, S, _ = h.shape
    L = hc.shape[1]
    na_qkv, da_qkv, gdn_qkv, gdn_z, gdn_ab, fnet_in, gate_in = split_cols(h @ w_in)
    na_qkv_c, da_qkv_c, gdn_qkv_c, gdn_z_c, gdn_ab_c, fnet_in_c, gate_in_c = split_cols(hc @ w_in)

    def na_heads(u, n):
        q, k, v = (t.reshape(B, n, NA_HEADS, NA_DIM) for t in jnp.split(u, 3, axis=-1))
        return rmsnorm(q, na_qn_g), rmsnorm(k, na_kn_g), v
    ya, ya_c = neighbourhood_attention(*na_heads(na_qkv, S), *na_heads(na_qkv_c, L), na_rpb, ctx_out)

    t = jnp.arange(S)
    rows = (t // GRID_W).astype(jnp.float32)
    cols = (t % GRID_W).astype(jnp.float32)

    def da_heads(u, n):
        q, k, v = jnp.split(u, 3, axis=-1)
        q = rmsnorm(q.reshape(B, n, DA_HEADS, 2, DA_QK_DIM), da_qn_g)
        k = rmsnorm(k.reshape(B, n, DA_HEADS, 2, DA_QK_DIM), da_kn_g)
        return q, k, v.reshape(B, n, DA_HEADS, DA_V_DIM)

    qd, kd, vd = da_heads(da_qkv, S)
    qd, kd = rope_2d(qd, rows, cols), rope_2d(kd, rows, cols)
    lam = (jnp.exp(jnp.sum(da_lam_q1.astype(jnp.float32) * da_lam_k1.astype(jnp.float32)))
           - jnp.exp(jnp.sum(da_lam_q2.astype(jnp.float32) * da_lam_k2.astype(jnp.float32))) + lam_init)
    yd, yd_c = diff_attention(qd, kd, vd, *da_heads(da_qkv_c, L), lam, ctx_out)

    def da_out(o):
        return (rmsnorm(o, da_subln_g) * (1.0 - lam_init)).reshape(*o.shape[:2], BRANCH_W)

    yg, yg_c = gdn_mixer(gdn_qkv, gdn_ab, gdn_z, gdn_qkv_c, gdn_ab_c, gdn_z_c, gdn_conv_w, gdn_a_log,
                         gdn_dt_bias, gdn_onorm_g, ctx_out)

    y = merge_branches((ya, da_out(yd), yg, fourier_mix(fnet_in)), gate_in, w_branch, w_out)
    y_c = None
    if ctx_out:
        y_c = merge_branches((ya_c, da_out(yd_c), yg_c, fourier_mix(fnet_in_c)), gate_in_c, w_branch, w_out)
    return y, y_c

def moe_ffn(h, w_router, router_bias, w_g, w_u, w_d):
    N, D = h.shape
    per_group = N_EXPERTS // N_GROUPS
    scores = jax.nn.sigmoid((h @ w_router).astype(jnp.float32))
    sel = scores + router_bias.astype(jnp.float32)
    group_score = lax.top_k(sel.reshape(N, N_GROUPS, per_group), 2)[0].sum(-1)
    best = jnp.argmax(group_score, axis=-1)
    in_group = (jnp.arange(N_EXPERTS) // per_group)[None, :] == best[:, None]
    _, idx = lax.top_k(jnp.where(in_group, sel, NEG_INF), TOP_K)
    wts = jnp.take_along_axis(scores, idx, axis=-1)
    wts = wts / jnp.sum(wts, axis=-1, keepdims=True)
    A = N * TOP_K
    expert = idx.reshape(A)
    token = jnp.repeat(jnp.arange(N, dtype=jnp.int32), TOP_K)
    weight = wts.reshape(A)
    order = jnp.argsort(expert)
    e_sorted = expert[order]
    counts = jnp.bincount(expert, length=N_EXPERTS)
    padded = (counts + MOE_BLOCK - 1) // MOE_BLOCK * MOE_BLOCK
    pad_end = jnp.cumsum(padded)
    pad_start = pad_end - padded
    start = jnp.cumsum(counts) - counts
    dest = pad_start[e_sorted] + jnp.arange(A) - start[e_sorted]
    n_blocks = -(-A // MOE_BLOCK) + N_EXPERTS
    P = n_blocks * MOE_BLOCK
    row_token = jnp.full((P,), N, jnp.int32).at[dest].set(token[order])
    row_weight = jnp.zeros((P,), h.dtype).at[dest].set(weight[order].astype(h.dtype))
    block_expert = jnp.minimum(jnp.searchsorted(pad_end, jnp.arange(n_blocks) * MOE_BLOCK, side='right'), N_EXPERTS - 1)
    h_pad = jnp.concatenate([h, jnp.zeros((1, D), h.dtype)], axis=0)
    xs = h_pad[row_token].reshape(n_blocks, MOE_BLOCK, D)

    def expert_block(args):
        xb, e = args
        return (jax.nn.silu(xb @ w_g[e]) * (xb @ w_u[e])) @ w_d[e]

    y = lax.map(expert_block, (xs, block_expert)).reshape(P, D) * row_weight[:, None]
    return jnp.zeros((N + 1, D), h.dtype).at[row_token].add(y)[:N]

def setup_inputs(seed: int = 0) -> dict:
    key = jax.random.key(seed)
    ks = (jax.random.fold_in(key, i) for i in range(100))
    nrm = lambda shape, s: jax.random.normal(next(ks), shape, jnp.float32) * s
    gain = lambda shape: 1.0 + nrm(shape, 0.01)
    dt = jnp.exp(jax.random.uniform(next(ks), (DEPTH, 2, GDN_HEADS), jnp.float32,
                                    minval=math.log(1e-3), maxval=math.log(1e-1)))
    a_log = jnp.log(jax.random.uniform(next(ks), (DEPTH, 2, GDN_HEADS), jnp.float32, minval=1.0, maxval=16.0))
    return {
        'x': nrm((BATCH, SEQ, D_MODEL), 1.0),
        'c': nrm((BATCH, D_MODEL), 1.0),
        'ctx': nrm((BATCH, CTX_LEN, D_MODEL), 1.0),
        'c_ctx': nrm((D_MODEL,), 1.0),
        'w_mod': nrm((DEPTH, D_MODEL, 6 * D_MODEL), 0.5 * D_MODEL ** -0.5),
        'b_mod': nrm((DEPTH, 6 * D_MODEL), 0.02),
        'norm1_g': gain((DEPTH, D_MODEL)),
        'norm2_g': gain((DEPTH, D_MODEL)),
        'w_in': nrm((DEPTH, D_MODEL, D_IN), D_MODEL ** -0.5),
        'na_qn_g': gain((DEPTH, NA_DIM)),
        'na_kn_g': gain((DEPTH, NA_DIM)),
        'na_rpb': nrm((DEPTH, NA_HEADS, 2 * NA_WIN_H - 1, 2 * NA_WIN_W - 1), 0.1),
        'da_qn_g': gain((DEPTH, DA_QK_DIM)),
        'da_kn_g': gain((DEPTH, DA_QK_DIM)),
        'da_lam_q1': nrm((DEPTH, DA_QK_DIM), 0.1),
        'da_lam_k1': nrm((DEPTH, DA_QK_DIM), 0.1),
        'da_lam_q2': nrm((DEPTH, DA_QK_DIM), 0.1),
        'da_lam_k2': nrm((DEPTH, DA_QK_DIM), 0.1),
        'da_subln_g': gain((DEPTH, DA_V_DIM)),
        'gdn_conv_w': nrm((DEPTH, GDN_CONV, 3 * BRANCH_W), GDN_CONV ** -0.5),
        'gdn_a_log': a_log,
        'gdn_dt_bias': dt + jnp.log(-jnp.expm1(-dt)),
        'gdn_onorm_g': gain((DEPTH, GDN_DIM)),
        'w_branch': nrm((DEPTH, N_BRANCH, BRANCH_W, D_MODEL), BRANCH_W ** -0.5),
        'w_out': nrm((DEPTH, D_MODEL, D_MODEL), D_MODEL ** -0.5),
        'w_router': nrm((D_MODEL, N_EXPERTS), D_MODEL ** -0.5),
        'router_bias': nrm((N_EXPERTS,), 0.01),
        'moe_w_gate': nrm((DEPTH, N_EXPERTS, D_MODEL, D_FF), D_MODEL ** -0.5),
        'moe_w_up': nrm((DEPTH, N_EXPERTS, D_MODEL, D_FF), D_MODEL ** -0.5),
        'moe_w_down': nrm((DEPTH, N_EXPERTS, D_FF, D_MODEL), D_FF ** -0.5),
    }

def reference(x, c, ctx, c_ctx, w_mod, b_mod, norm1_g, norm2_g, w_in, na_qn_g, na_kn_g, na_rpb,
              da_qn_g, da_kn_g, da_lam_q1, da_lam_k1, da_lam_q2, da_lam_k2, da_subln_g, gdn_conv_w,
              gdn_a_log, gdn_dt_bias, gdn_onorm_g, w_branch, w_out, w_router, router_bias,
              moe_w_gate, moe_w_up, moe_w_down):
    B, S, _ = x.shape
    L = ctx.shape[1]
    for l in range(DEPTH):
        last = l == DEPTH - 1
        lam_init = 0.8 - 0.6 * math.exp(-0.3 * l)
        mod = jax.nn.silu(c) @ w_mod[l] + b_mod[l]
        mod_c = jax.nn.silu(c_ctx) @ w_mod[l] + b_mod[l]
        sh1, sc1, g1, sh2, sc2, g2 = jnp.split(mod[:, None, :], 6, axis=-1)
        sh1c, sc1c, g1c, sh2c, sc2c, g2c = jnp.split(mod_c, 6)
        h = modulate(rmsnorm(x, norm1_g[l]), sh1, sc1)
        hc = modulate(rmsnorm(ctx, norm1_g[l]), sh1c, sc1c)
        y, y_c = token_mixers(h, hc, w_in[l], na_qn_g[l], na_kn_g[l], na_rpb[l], da_qn_g[l], da_kn_g[l],
                              da_lam_q1[l], da_lam_k1[l], da_lam_q2[l], da_lam_k2[l], da_subln_g[l],
                              gdn_conv_w[l], gdn_a_log[l], gdn_dt_bias[l], gdn_onorm_g[l],
                              w_branch[l], w_out[l], lam_init, not last)
        x = x + g1 * y
        h2 = modulate(rmsnorm(x, norm2_g[l]), sh2, sc2).reshape(B * S, D_MODEL)
        if last:
            f = moe_ffn(h2, w_router, router_bias, moe_w_gate[l], moe_w_up[l], moe_w_down[l])
            x = x + g2 * f.reshape(B, S, D_MODEL)
        else:
            ctx = ctx + g1c * y_c
            h2c = modulate(rmsnorm(ctx, norm2_g[l]), sh2c, sc2c).reshape(B * L, D_MODEL)
            f = moe_ffn(jnp.concatenate([h2, h2c], axis=0), w_router, router_bias,
                        moe_w_gate[l], moe_w_up[l], moe_w_down[l])
            x = x + g2 * f[:B * S].reshape(B, S, D_MODEL)
            ctx = ctx + g2c * f[B * S:].reshape(B, L, D_MODEL)
    return x


_drawn_inputs = setup_inputs


def setup_inputs(seed=0):
    import zlib

    import numpy as np

    out = dict(_drawn_inputs(seed))
    spreads = {}
    factors = {'norm1_g': 6.289,
     'norm2_g': 3.459,
     'na_qn_g': 8.0,
     'na_kn_g': 8.0,
     'na_rpb': 8.0,
     'da_qn_g': 8.0,
     'da_kn_g': 8.0,
     'da_lam_q1': 8.0,
     'da_lam_k1': 8.0,
     'da_lam_q2': 8.0,
     'da_lam_k2': 8.0,
     'da_subln_g': 8.0,
     'gdn_onorm_g': 8.0}
    for name, (base, spread) in spreads.items():
        noise = np.random.default_rng([zlib.crc32(name.encode()), seed]).standard_normal(out[name].shape)
        drawn = base * np.exp(spread * noise) if base else spread * noise
        out[name] = jnp.asarray(drawn.astype(out[name].dtype))
    for name, factor in factors.items():
        out[name] = (out[name] * factor).astype(out[name].dtype)
    return out
```

```python
import math
from contextlib import ExitStack

import numpy as np

import concourse.bass as bass
from concourse import mybir

F32 = mybir.dt.float32
I32 = mybir.dt.int32
U32 = mybir.dt.uint32
ALU = mybir.AluOpType
ACT = mybir.ActivationFunctionType
AX = mybir.AxisListType

P = 128
D = 1024
KD = D // P
S = 1024
L = 256
T = S + L
NT = T // P
NL = S // P
GRID_W = 64
BW = 256
H = 4
HD = 64
DQ = 32
WIN_H, WIN_W = 8, 16
NEXP, NGRP, PERG, FF = 16, 4, 4, 512
NBLK = (2 * S) // P + NEXP - 1
EPS = 1e-6
NEG = -1e30
COL_NA, COL_DA, COL_GDN, COL_Z = 0, 3 * BW, 6 * BW, 9 * BW
COL_AB, COL_F, COL_G = 10 * BW, 10 * BW + 16, 11 * BW + 16
D_IN = COL_G + 4 * D
CONV = 5


class Chain:

    def __init__(self, eng, sem):
        self.eng, self.sem, self.n = eng, sem, 0

    def __call__(self, ins):
        self.n += 1
        ins.then_inc(self.sem, 1)
        self.eng.wait_ge(self.sem, self.n)


def named(**things):
    return type("Named", (), things)()


def bc(ap, n):
    return ap.unsqueeze(len(ap.shape)).broadcast_to(list(ap.shape) + [n])


def phase_modulation(nc, g, ctx):
    sb = lambda n, s, d=F32: ctx.enter_context(nc.sbuf_tensor(n, s, d))
    NCH, ROWCH, W = 12, 4, 512
    wm = g.attmem[:, 0:3 * KD * W].rearrange("p (j k n) -> p j k n", j=3, k=KD)
    ccol = sb("ccol", [P, KD, 2])
    scol = sb("scol", [P, KD, 2])
    sbig = sb("sbig", [P, KD, P])
    brow = sb("brow", [2, 2 * D])
    mrow = sb("mrow", [2, 2 * D])
    n1col = sb("n1col", [P, KD])
    junk = sb("junk_sq", [P, D])
    ss = sb("ss", [P, NT])
    block = ctx.enter_context(nc.Block())
    link, e = g.link, g.mo

    @block.sync
    def _(sp):
        sp.dma_start(ccol[:, :, :], g.c_cols).then_inc(e.c_loaded, 16)
        for j in range(3):
            sp.dma_start(wm[:, j], g.w_mod.rearrange("(k p) n -> p k n", p=P)[:, :, j * W:(j + 1) * W]).then_inc(e.wmod_loaded[j], 16)
        for a, src in ((0, g.x), (1, g.ctx)):
            n = (NL, NT - NL)[a]
            for t in range(n):
                sp.dma_start(g.xall[:, a * NL + t], src[0, t * P:(t + 1) * P, :]).then_inc(e.x_loaded, 16)
        for j in range(3, NCH):
            sp.wait_ge(e.mod_done, j - 2)
            sp.dma_start(wm[:, j % 3], g.w_mod.rearrange("(k p) n -> p k n", p=P)[:, :, j * W:(j + 1) * W]).then_inc(e.wmod_loaded[j % 3], 16)

    @block.gpsimd
    def _(pool):
        for a in range(2):
            pool.dma_start(brow[a:a + 1, :], g.b_mod[0:2 * D].unsqueeze(0)).then_inc(e.small_loaded, 16)
        pool.dma_start(n1col[:, :], g.norm1_cols).then_inc(e.small_loaded, 16)
        pool.dma_start(g.modb[:, :], g.b_mod[2 * D:6 * D].partition_broadcast(P)).then_inc(e.bmod_loaded, 16)
        for t, src in ((g.ident, g.k_ident),):
            pool.dma_start(t[:, :], src).then_inc(e.ident_loaded, 16)

    @block.scalar
    def _(act):
        act.wait_ge(e.c_loaded, 16)
        act.activation(scol[:, :, :], ccol[:, :, :], ACT.Silu).then_inc(e.silu_done, 1)
        act.wait_ge(e.x_loaded, 16 * NT)
        for t in range(NT):
            if t:
                act.wait_ge(e.sums_done, t)
            act.activation(junk[:, :], g.xall[:, t], ACT.Square, accum_out=ss[:, t:t + 1]).then_inc(e.sums_done, 1)
        act.wait_ge(e.meansq_done, 1)
        act.activation(ss[:, :], ss[:, :], ACT.Sqrt).then_inc(e.rms_done, 1)
        act.wait_ge(e.rstd_done, 1)
        for t in range(NT):
            i = act.activation(g.xall[:, t], g.xall[:, t], ACT.Copy, scale=ss[:, t:t + 1])
        i.then_inc(e.xn_done, 1)

    @block.vector
    def _(dve):
        dve.wait_ge(e.silu_done, 1)
        dve.tensor_copy(sbig[:, :, :], bc(scol[:, :, 0], P)).then_inc(e.sbig_done, 1)
        dve.wait_ge(e.sums_done, NT)
        dve.tensor_scalar(ss[:, :], ss[:, :], 1.0 / D, EPS, ALU.mult, ALU.add).then_inc(e.meansq_done, 1)
        dve.wait_ge(e.rms_done, 1)
        dve.reciprocal(ss[:, :], ss[:, :]).then_inc(e.rstd_done, 1)
        dve.wait_ge(e.small_loaded, 48)
        for j in range(NCH):
            dve.wait_ge(e.mod_done, j + 1)
            if j < ROWCH:
                c = slice(j * W, (j + 1) * W)
                i = dve.tensor_tensor(mrow[:, c], g.ps[0:2, j % 2, :], brow[:, c], ALU.add)
            else:
                if j == ROWCH:
                    dve.wait_ge(e.bmod_loaded, 16)
                c = slice((j - ROWCH) * W, (j - ROWCH + 1) * W)
                i = dve.tensor_tensor(g.modb[:, c], g.ps[:, j % 2, :], g.modb[:, c], ALU.add)
            i.then_inc(e.mod_kept, 1)
            if j == ROWCH:
                dve.wait_ge(e.modT_done, 1)
                v = g.ps[:, 2, 0:32].rearrange("p (k a) -> p k a", a=2)
                link(dve.tensor_copy(g.bcol[:, :, :], v[:, 0:KD, :]))
                link(dve.tensor_scalar(g.acol[:, :, :], v[:, KD:2 * KD, :], 1.0, None, ALU.add))
                link(dve.tensor_tensor(g.acol[:, :, :], g.acol[:, :, :], bc(n1col[:, :], 2), ALU.mult))

    @block.tensor
    def _(pe):
        pe.wait_ge(e.silu_done, 1)
        pe.wait_ge(e.sbig_done, 1)
        for j in range(NCH):
            pe.wait_ge(e.wmod_loaded[j % 3], 16 * (j // 3 + 1))
            if j >= 2:
                pe.wait_ge(e.mod_kept, j - 1)
            for k in range(KD):
                out = g.ps[0:2, j % 2, :] if j < ROWCH else g.ps[:, j % 2, :]
                lhs = scol[:, k, :] if j < ROWCH else sbig[:, k, :]
                i = pe.matmul(out, lhs, wm[:, j % 3, k, :], start=(k == 0), stop=(k == KD - 1))
            i.then_inc(e.mod_done, 1)
            if j == ROWCH:
                pe.wait_ge(e.mod_kept, ROWCH)
                pe.wait_ge(e.ident_loaded, 16)
                for k in range(2 * KD):
                    i = pe.transpose(g.ps[:, 2, 2 * k:2 * k + 2], mrow[:, k * P:(k + 1) * P], g.ident[0:2, 0:2])
                i.then_inc(e.modT_done, 1)


def phase_qkv(nc, g, ctx, which):
    sb = lambda n, s, d=F32: ctx.enter_context(nc.sbuf_tensor(f"{n}{which}", s, d))
    first = which == 0
    nz = BW + 16 if first else 0
    hw, ng = (HD, 8) if first else (DQ, 16)
    wq = sb("wq", [P, KD, 3 * BW + nz])
    sq = sb("sq", [P, 2 * BW])
    qn = sb("qn", [P, 2, 2 * BW])
    r = sb("r", [P, 2, ng])
    QT, KT, V = ((g.naQ, g.naK, g.naV), (g.daQ, g.daK, g.daV))[which]
    if first:
        gcol = sb("gcol", [P, 2])
    else:
        gb = sb("gb", [P, 2, 8, DQ])
        cos = sb("cos", [P, NT, DQ])
        sin = sb("sin", [P, NT, DQ])
        xr = sb("xr", [P, 2 * BW])
        xs = sb("xs", [P, 2 * BW])
    qn_g, kn_g = ((g.na_qn_g, g.na_kn_g), (g.da_qn_g, g.da_kn_g))[which]
    c0 = (COL_NA, COL_DA)[which]
    link, e = g.link, g.qkv
    w_in = g.w_in.rearrange("(k p) n -> p k n", p=P)
    block = ctx.enter_context(nc.Block())

    @block.sync
    def _(sp):
        sp.dma_start(wq[:, :, 0:3 * BW], w_in[:, :, c0:c0 + 3 * BW]).then_inc(e.w_loaded, 16)
        if first:
            sp.dma_start(wq[:, :, 3 * BW:], w_in[:, :, COL_Z:COL_Z + nz]).then_inc(e.w_loaded, 16)
            for a, src in ((0, qn_g), (1, kn_g)):
                for b in range(2):
                    sp.dma_start(gcol[b * HD:(b + 1) * HD, a:a + 1], src.unsqueeze(1)).then_inc(e.w_loaded, 16)
        else:
            for a, src in ((0, qn_g), (1, kn_g)):
                sp.dma_start(gb[:, a], bass.AP(src.tensor, src.offset, [[0, P], [0, 8], [1, DQ]])).then_inc(e.w_loaded, 16)
            sp.dma_start(cos[:, :, :], g.k_cos.rearrange("(t p) f -> p t f", p=P)).then_inc(e.w_loaded, 16)
            sp.dma_start(sin[:, :, :], g.k_sin.rearrange("(t p) f -> p t f", p=P)).then_inc(e.w_loaded, 16)

    loads = 6 if first else 5

    @block.scalar
    def _(act):
        for t in range(NT):
            s = t % 2
            if first:
                act.wait_ge(e.hT_turned, t + 1)
                for k in range(KD // 2, KD):
                    a = 0 if t < NL else 1
                    i = act.activation(g.hT[:, k, t * P:(t + 1) * P], g.ps[:, k // 4, (k % 4) * P:(k % 4 + 1) * P],
                                       ACT.Identity, bias=g.bcol[:, k, a:a + 1], scale=g.acol[:, k, a:a + 1])
                i.then_inc(e.hT_act, 1)
            act.wait_ge(e.qk_done, t + 1)
            if t:
                act.wait_ge(e.ss_done, t)
            act.activation(sq[:, :], g.ps[:, 2 + s, :], ACT.Square).then_inc(e.sq_done, 1)
            act.wait_ge(e.v_done, t + 1)
            act.activation(V[:, t, :], g.ps[:, 4 + s, 0:BW], ACT.Copy).then_inc(e.v_kept, 1)
            if first:
                if t < NL:
                    act.activation(g.z[:, t, :], g.ps[:, 4 + s, BW:2 * BW], ACT.Copy)
                act.activation(g.ab[:, t, :], g.ps[:, 6, 0:16], ACT.Copy).then_inc(e.v_kept, 1)
            act.wait_ge(e.ms_done, t + 1)
            act.activation(r[:, s, :], r[:, s, :], ACT.Sqrt).then_inc(e.rms_done, 1)

    @block.vector
    def _(dve):
        dve.wait_ge(e.w_loaded, 16 * loads)
        if first:
            link(dve.tensor_scalar(gcol[:, 0:1], gcol[:, 0:1], HD ** -0.5, None, ALU.mult))

        def keep_turned(t):
            dve.wait_ge(e.qT_turned, t + 1)
            for c in range(4):
                if c < 2 and t >= NL:
                    continue
                dst = (QT if c < 2 else KT)[:, c % 2, t * P:(t + 1) * P]
                src = g.ps[:, 7, c * P:(c + 1) * P]
                if first:
                    i = dve.tensor_scalar(dst, src, gcol[:, c // 2:c // 2 + 1], None, ALU.mult)
                else:
                    i = dve.tensor_copy(dst, src)
            i.then_inc(e.qT_kept, 1)

        for t in range(NT):
            s = t % 2
            if first:
                dve.wait_ge(e.hT_turned, t + 1)
                for k in range(KD // 2):
                    a = 0 if t < NL else 1
                    i = dve.tensor_scalar(g.hT[:, k, t * P:(t + 1) * P], g.ps[:, k // 4, (k % 4) * P:(k % 4 + 1) * P],
                                          g.acol[:, k, a:a + 1], g.bcol[:, k, a:a + 1], ALU.mult, ALU.add)
                i.then_inc(e.hT_dve, 1)
            dve.wait_ge(e.sq_done, t + 1)
            dve.tensor_reduce(r[:, s, :], sq[:, :].rearrange("p (g f) -> p g f", f=hw), AX.X, ALU.add).then_inc(e.ss_done, 1)
            dve.wait_ge(e.ss_done, t + 1)
            dve.tensor_scalar(r[:, s, :], r[:, s, :], 1.0 / hw, EPS, ALU.mult, ALU.add).then_inc(e.ms_done, 1)
            dve.wait_ge(e.rms_done, t + 1)
            link(dve.reciprocal(r[:, s, :], r[:, s, :]))
            if t >= 2:
                dve.wait_ge(e.qT_turned, t - 1)
            q3 = qn[:, s, :].rearrange("p (g f) -> p g f", f=hw)
            i = dve.tensor_tensor(q3, g.ps[:, 2 + s, :].rearrange("p (g f) -> p g f", f=hw), bc(r[:, s, :], hw), ALU.mult)
            i.then_inc(e.qk_kept, 1)
            if not first:
                dve.wait_ge(e.qk_kept, t + 1)
                flat = qn[:, s, :]
                link(dve.tensor_tensor(xr[:, :], flat, gb[:, :, :, :].rearrange("p a g f -> p (a g f)"), ALU.mult))
                x4 = xr[:, :].rearrange("p (g a f) -> p g a f", g=32, a=2)
                o4 = xs[:, :].rearrange("p (g a f) -> p g a f", g=32, a=2)
                for b in range(2):
                    sn = sin[:, t, :].rearrange("p (x a f) -> p x a f", x=2, a=2)[:, :, b, :]
                    sn = sn.unsqueeze(1).broadcast_to([P, 16, 2, 8])
                    link(dve.tensor_tensor(o4[:, :, b, :].rearrange("p (g x) f -> p g x f", x=2),
                                           x4[:, :, 1 - b, :].rearrange("p (g x) f -> p g x f", x=2), sn, ALU.mult))
                cs = cos[:, t, :].unsqueeze(1).broadcast_to([P, 16, DQ])
                link(dve.tensor_tensor(q3, xr[:, :].rearrange("p (g f) -> p g f", f=DQ), cs, ALU.mult))
                dve.tensor_tensor(flat, flat, xs[:, :], ALU.add).then_inc(e.rope_done, 1)
            if t:
                keep_turned(t - 1)
        keep_turned(NT - 1)

    @block.tensor
    def _(pe):

        def turn_h(t):
            if t:
                pe.wait_ge(e.hT_act, t)
                pe.wait_ge(e.hT_dve, t)
            for k in range(KD):
                i = pe.transpose(g.ps[:, k // 4, (k % 4) * P:(k % 4 + 1) * P], g.xall[:, t, k * P:(k + 1) * P], g.ident[:, :])
            i.then_inc(e.hT_turned, 1)

        def turn_q(t):
            pe.wait_ge(e.rope_done if not first else e.qk_kept, t + 1)
            if t:
                pe.wait_ge(e.qT_kept, t)
            for c in range(4):
                i = pe.transpose(g.ps[:, 7, c * P:(c + 1) * P], qn[:, t % 2, c * P:(c + 1) * P], g.ident[:, :])
            i.then_inc(e.qT_turned, 1)

        if first:
            turn_h(0)
        pe.wait_ge(e.w_loaded, 16 * loads)
        per_v = 2 if first else 1
        for t in range(NT):
            s = t % 2
            if first:
                if t + 1 < NT:
                    turn_h(t + 1)
                pe.wait_ge(e.hT_act, t + 1)
                pe.wait_ge(e.hT_dve, t + 1)
            if t >= 2:
                pe.wait_ge(e.qk_kept, t - 1)
            for k in range(KD):
                i = pe.matmul(g.ps[:, 2 + s, :], g.hT[:, k, t * P:(t + 1) * P], wq[:, k, 0:2 * BW], start=(k == 0), stop=(k == KD - 1))
            i.then_inc(e.qk_done, 1)
            if t >= 1:
                turn_q(t - 1)
                pe.wait_ge(e.v_kept, per_v * t)
            for k in range(KD):
                i = pe.matmul(g.ps[:, 4 + s, 0:BW], g.hT[:, k, t * P:(t + 1) * P], wq[:, k, 2 * BW:3 * BW], start=(k == 0), stop=(k == KD - 1))
            if first:
                for k in range(KD):
                    pe.matmul(g.ps[:, 4 + s, BW:2 * BW], g.hT[:, k, t * P:(t + 1) * P], wq[:, k, 3 * BW:4 * BW], start=(k == 0), stop=(k == KD - 1))
                for k in range(KD):
                    i = pe.matmul(g.ps[:, 6, 0:16], g.hT[:, k, t * P:(t + 1) * P], wq[:, k, 4 * BW:4 * BW + 16], start=(k == 0), stop=(k == KD - 1))
            i.then_inc(e.v_done, 1)
        turn_q(NT - 1)


def turn_branch(nc, g, e, pe, src):
    for j in range(4):
        for q in range(4):
            i = pe.transpose(g.ps[:, j, q * P:(q + 1) * P], src[:, 4 * (j % 2) + q, (j // 2) * P:(j // 2 + 1) * P], g.ident[:, :])
    i.then_inc(e.br_turned, 1)


def keep_branch(nc, g, e, dve, branch):
    dve.wait_ge(e.br_turned, 1)
    for j in range(4):
        dve.tensor_copy(g.brT[:, 2 * branch + j // 2, (j % 2) * 512:(j % 2 + 1) * 512], g.ps[:, j, :])


def na_first_tile(i):
    return min(max(i - 2, 0), 3)


def phase_na(nc, g, ctx):
    sb = lambda n, s, d=F32: ctx.enter_context(nc.sbuf_tensor("na_" + n, s, d))
    NKL, NK = 640, 896
    bm = sb("bm", [P, 2, H, NKL])
    mask = sb("mask", [P, 2, NKL])
    pr = sb("pr", [P, 2, NK])
    pT = sb("pT", [P, 2, 7, P])
    ya = g.stage
    mx = sb("mx", [P, 2])
    nmx = sb("nmx", [P, 2])
    l = sb("l", [P, NL * H])
    e, link = g.na, g.link
    OFF = 9
    U = [(i, h) for i in range(NL) for h in range(H)]
    block = ctx.enter_context(nc.Block())

    @block.sync
    def _(sp):
        sp.dma_start(g.rpb_pad.rearrange("h r c -> h (r c)"), g.k_zeros[:, 0:20 * P]).then_inc(e.pad_done, 16)
        sp.wait_ge(e.pad_done, 16)
        sp.dma_start(g.rpb_pad[:, OFF - WIN_H + 1:OFF + WIN_H, 48:48 + 2 * WIN_W - 1], g.na_rpb).then_inc(e.pad_done, 16)
        sp.wait_ge(e.pad_done, 32)
        for h in range(H):
            sp.dma_start(g.rpb_rep[h], g.rpb_pad[h].unsqueeze(1).broadcast_to([20, GRID_W, P])).then_inc(e.rep_done, 16)
        sp.wait_ge(e.rep_done, 16 * H)
        for i in range(NL):
            if i >= 2:
                sp.wait_ge(e.bm_used, H * (i - 1))
            for a in range(2):
                for h in range(H):
                    row = 2 * na_first_tile(i) - (2 * i + a) + OFF
                    src = bass.AP(g.rpb_rep.tensor, (h * 20 + row) * GRID_W * P + GRID_W - 1, [[P - 1, GRID_W], [GRID_W * P, 10], [1, GRID_W]])
                    sp.dma_start(bm[a * 64:(a + 1) * 64, i % 2, h, :].rearrange("p (r c) -> p r c", r=10), src).then_inc(e.bm_loaded[i % 2], 16)
            sp.dma_start(mask[:, i % 2], g.k_namask[[0, 1, 2, 2, 2, 2, 3, 4][i]]).then_inc(e.bm_loaded[i % 2], 16)

    @block.gpsimd
    def _(pool):
        for i in range(NL):
            pool.wait_ge(e.bm_loaded[i % 2], 16 * 9 * (i // 2 + 1))
            for h in range(H):
                pool.tensor_tensor(bm[:, i % 2, h], bm[:, i % 2, h], mask[:, i % 2], ALU.add).then_inc(e.bm_ready, 1)

    @block.tensor
    def _(pe):
        def scores(u):
            i, h = U[u]
            if u >= 2:
                pe.wait_ge(e.exp_done, u - 1)
            b, s = 64 * (h % 2), 2 * (u % 2)
            k0 = na_first_tile(i) * P
            q = g.naQ[b:b + 64, h // 2, i * P:(i + 1) * P]
            for off, src, n in ((0, k0, 512), (512, k0 + 512, 128), (640, S, L)):
                mm = pe.matmul(g.ps[:, s + off // 512, off % 512:off % 512 + n], q, g.naK[b:b + 64, h // 2, src:src + n], start=True, stop=True)
            mm.then_inc(e.s_done, 1)

        def turn(u):
            pe.wait_ge(e.exp_done, u + 1)
            if u:
                pe.wait_ge(e.pt_act, u)
                pe.wait_ge(e.pt_dve, u)
            for k in range(7):
                mm = pe.transpose(g.ps[:, 4 + k // 4, (k % 4) * P:(k % 4 + 1) * P], pr[:, u % 2, k * P:(k + 1) * P], g.ident[:, :])
            mm.then_inc(e.pt_turned, 1)

        def values(u):
            i, h = U[u]
            pe.wait_ge(e.pt_act, u + 1)
            pe.wait_ge(e.pt_dve, u + 1)
            if u >= 2:
                pe.wait_ge(e.o_kept, u - 1)
            for k in range(7):
                kt = na_first_tile(i) + k if k < 5 else NL + k - 5
                mm = pe.matmul(g.ps[:, 6 + u % 2, 0:HD], pT[:, u % 2, k, :], g.naV[:, kt, h * HD:(h + 1) * HD], start=(k == 0), stop=(k == 6))
            mm.then_inc(e.o_done, 1)

        for u in range(len(U) + 2):
            if u < len(U):
                scores(u)
            if 1 <= u <= len(U):
                turn(u - 1)
            if u >= 2:
                values(u - 2)
        pe.wait_ge(e.o_kept, len(U))
        turn_branch(nc, g, e, pe, ya)

    @block.scalar
    def _(act):
        for u in range(len(U) + 1):
            if u < len(U):
                act.wait_ge(e.max_done, u + 1)
                if u >= 2:
                    act.wait_ge(e.pt_turned, u - 1)
                s = g.ps[:, 2 * (u % 2):2 * (u % 2) + 2, :].rearrange("p a b -> p (a b)")
                act.activation(pr[:, u % 2, :], s[:, 0:NK], ACT.Exp, bias=nmx[:, u % 2:u % 2 + 1], accum_out=l[:, u:u + 1]).then_inc(e.exp_done, 1)
            if u:
                act.wait_ge(e.pt_turned, u)
                if u >= 3:
                    act.wait_ge(e.o_done, u - 2)
                act.activation(pT[:, (u - 1) % 2, 0:4, :], g.ps[:, 4, :].rearrange("p (a b) -> p a b", a=4), ACT.Copy).then_inc(e.pt_act, 1)

    @block.vector
    def _(dve):
        for u in range(len(U) + 2):
            if u < len(U):
                i, h = U[u]
                s = g.ps[:, 2 * (u % 2):2 * (u % 2) + 2, :].rearrange("p a b -> p (a b)")
                dve.wait_ge(e.s_done, u + 1)
                dve.wait_ge(e.bm_ready, u + 1)
                dve.tensor_tensor(s[:, 0:NKL], s[:, 0:NKL], bm[:, i % 2, h], ALU.add).then_inc(e.bm_used, 1)
                dve.wait_ge(e.bm_used, u + 1)
                link(dve.tensor_reduce(mx[:, u % 2:u % 2 + 1], s[:, 0:NK], AX.X, ALU.max))
                if u >= 2:
                    dve.wait_ge(e.exp_done, u - 1)
                dve.tensor_scalar(nmx[:, u % 2:u % 2 + 1], mx[:, u % 2:u % 2 + 1], -1.0, None, ALU.mult).then_inc(e.max_done, 1)
            if 1 <= u <= len(U):
                dve.wait_ge(e.pt_turned, u)
                if u >= 3:
                    dve.wait_ge(e.o_done, u - 2)
                dve.tensor_copy(pT[:, (u - 1) % 2, 4:7, :], g.ps[:, 5, 0:384].rearrange("p (a b) -> p a b", a=3)).then_inc(e.pt_dve, 1)
                link(dve.reciprocal(l[:, u - 1:u], l[:, u - 1:u]))
            if u >= 2:
                i, h = U[u - 2]
                dve.wait_ge(e.o_done, u - 1)
                dve.tensor_scalar(ya[:, i, h * HD:(h + 1) * HD], g.ps[:, 6 + u % 2, 0:HD], l[:, u - 2:u - 1], None, ALU.mult).then_inc(e.o_kept, 1)
        keep_branch(nc, g, e, dve, 0)


def phase_da(nc, g, ctx):
    sb = lambda n, s, d=F32: ctx.enter_context(nc.sbuf_tensor("da_" + n, s, d))
    LAM0 = 0.8 - 0.6 * math.exp(0.0)
    p0 = sb("p0", [P, 2, T])
    p1 = sb("p1", [P, 2, T])
    pT = sb("pT", [P, 2, NT, P])
    yd = g.stage
    sq = sb("sq", [P, NL, BW])
    gb = sb("gb", [P, HD])
    rr = sb("rr", [P, NL * H])
    lv = sb("lv", [P, 4, DQ])
    lam = sb("lam", [P, 4])
    mx = sb("mx", [P, 2, 2])
    nmx = sb("nmx", [P, 2, 2])
    l = sb("l", [P, 2, 2])
    e, link = g.da, g.link
    U = [(i, h) for i in range(NL) for h in range(H)]
    NU = len(U)
    block = ctx.enter_context(nc.Block())

    def score_banks(m):
        return g.ps[:, 3 * m:3 * m + 3, :].rearrange("p a b -> p (a b)")[:, 0:T]

    @block.sync
    def _(sp):
        for a, v in enumerate((g.da_lam_q1, g.da_lam_q2, g.da_lam_k1, g.da_lam_k2)):
            sp.dma_start(lv[:, a, :], v.partition_broadcast(P)).then_inc(e.small_loaded, 16)
        sp.dma_start(gb[:, :], g.da_subln_g.partition_broadcast(P)).then_inc(e.small_loaded, 16)

    @block.tensor
    def _(pe):
        def scores(u, m):
            i, h = U[u]
            c = 2 * h + m
            b = DQ * (c % 4)
            if u:
                pe.wait_ge(e.exp_done, 2 * (u - 1) + m + 1)
            q = g.daQ[b:b + DQ, c // 4, i * P:(i + 1) * P]
            for k in range(3):
                n = min(512, T - 512 * k)
                mm = pe.matmul(g.ps[:, 3 * m + k, 0:n], q, g.daK[b:b + DQ, c // 4, 512 * k:512 * k + n], start=True, stop=True, tile_position=(b, 0))
            mm.then_inc(e.s_done, 1)

        def turn(u, j):
            if j == 0:
                pe.wait_ge(e.a_done, u + 1)
            if 3 * u + j:
                pe.wait_ge(e.pt_kept, 3 * u + j)
            for k in range(4 * j, min(4 * j + 4, NT)):
                mm = pe.transpose(g.ps[:, 6, (k % 4) * P:(k % 4 + 1) * P], p1[:, u % 2, k * P:(k + 1) * P], g.ident[:, :])
            mm.then_inc(e.pt_turned, 1)

        def values(u, j):
            i, h = U[u]
            pe.wait_ge(e.pt_kept, 3 * u + j + 1)
            if j == 0 and u:
                pe.wait_ge(e.o_kept, u)
            for k in range(4 * j, min(4 * j + 4, NT)):
                mm = pe.matmul(g.ps[:, 7, 0:HD], pT[:, u % 2, k, :], g.daV[:, k, h * HD:(h + 1) * HD], start=(k == 0), stop=(k == NT - 1))
            if j == 2:
                mm.then_inc(e.o_done, 1)

        for u in range(NU + 1):
            if u < NU:
                scores(u, 0)
            if u:
                turn(u - 1, 0)
            if u < NU:
                scores(u, 1)
            if u:
                turn(u - 1, 1)
                values(u - 1, 0)
                turn(u - 1, 2)
                values(u - 1, 1)
                values(u - 1, 2)
        pe.wait_ge(e.y_done, 1)
        turn_branch(nc, g, e, pe, yd)

    @block.scalar
    def _(act):
        act.wait_ge(e.dots_done, 1)
        act.activation(lam[:, 0:2], lam[:, 0:2], ACT.Exp).then_inc(e.lam_exp, 1)
        for u in range(NU + 1):
            if u < NU:
                for m, p in ((0, p0), (1, p1)):
                    act.wait_ge(e.max_done, 2 * u + m + 1)
                    if u >= 2:
                        act.wait_ge(e.pt_turned, 3 * (u - 1))
                    act.activation(p[:, u % 2, :], score_banks(m), ACT.Exp, scale=DQ ** -0.5, bias=nmx[:, u % 2, m:m + 1],
                                   accum_out=l[:, u % 2, m:m + 1]).then_inc(e.exp_done, 1)
            if u:
                for j in range(3):
                    k = min(4, NT - 4 * j)
                    act.wait_ge(e.pt_turned, 3 * (u - 1) + j + 1)
                    if u >= 3:
                        act.wait_ge(e.o_done, u - 2)
                    act.activation(pT[:, (u - 1) % 2, 4 * j:4 * j + k, :], g.ps[:, 6, 0:k * P].rearrange("p (a b) -> p a b", a=k), ACT.Copy).then_inc(e.pt_kept, 1)
        act.wait_ge(e.ms_done, 1)
        act.activation(rr[:, :], rr[:, :], ACT.Sqrt).then_inc(e.rms_done, 1)

    @block.gpsimd
    def _(pool):
        for u in range(NU):
            pool.wait_ge(e.r_done, u + 1)
            pool.tensor_scalar(p0[:, u % 2, :], p0[:, u % 2, :], l[:, u % 2, 0:1], None, ALU.mult).then_inc(e.p0_done, 1)

    @block.vector
    def _(dve):
        dve.wait_ge(e.small_loaded, 80)
        link(dve.tensor_tensor(lv[:, 0:2, :], lv[:, 0:2, :], lv[:, 2:4, :], ALU.mult))
        dve.tensor_reduce(lam[:, 0:2], lv[:, 0:2, :], AX.X, ALU.add).then_inc(e.dots_done, 1)
        dve.wait_ge(e.lam_exp, 1)
        link(dve.tensor_tensor(lam[:, 2:3], lam[:, 1:2], lam[:, 0:1], ALU.subtract))
        link(dve.tensor_scalar(lam[:, 2:3], lam[:, 2:3], LAM0, None, ALU.subtract))

        def largest(u, m):
            dve.wait_ge(e.s_done, 2 * u + m + 1)
            link(dve.tensor_reduce(mx[:, u % 2, m:m + 1], score_banks(m), AX.X, ALU.max))
            dve.tensor_scalar(nmx[:, u % 2, m:m + 1], mx[:, u % 2, m:m + 1], -DQ ** -0.5, None, ALU.mult).then_inc(e.max_done, 1)

        for u in range(NU + 1):
            if u:
                w = (u - 1) % 2
                dve.wait_ge(e.exp_done, 2 * u)
                link(dve.reciprocal(l[:, w, :], l[:, w, :]))
                dve.tensor_scalar(l[:, w, 1:2], l[:, w, 1:2], lam[:, 2:3], None, ALU.mult).then_inc(e.r_done, 1)
                dve.wait_ge(e.r_done, u)
            if u < NU:
                largest(u, 0)
            if u:
                dve.wait_ge(e.p0_done, u)
                dve.scalar_tensor_tensor(p1[:, w, :], p1[:, w, :], l[:, w, 1:2], p0[:, w, :], ALU.mult, ALU.add).then_inc(e.a_done, 1)
            if u < NU:
                largest(u, 1)
            if u >= 2:
                i, h = U[u - 2]
                dve.wait_ge(e.o_done, u - 1)
                dve.tensor_copy(yd[:, i, h * HD:(h + 1) * HD], g.ps[:, 7, 0:HD]).then_inc(e.o_kept, 1)
        dve.wait_ge(e.o_done, NU)
        link(dve.tensor_copy(yd[:, NL - 1, 3 * HD:], g.ps[:, 7, 0:HD]))
        y3 = yd[:, :, :].rearrange("p t (h f) -> p (t h) f", f=HD)
        link(dve.tensor_tensor(sq[:, :, :], yd[:, :, :], yd[:, :, :], ALU.mult))
        link(dve.tensor_reduce(rr[:, :], sq[:, :, :].rearrange("p t (h f) -> p (t h) f", f=HD), AX.X, ALU.add))
        dve.tensor_scalar(rr[:, :], rr[:, :], 1.0 / HD, EPS, ALU.mult, ALU.add).then_inc(e.ms_done, 1)
        dve.wait_ge(e.rms_done, 1)
        link(dve.reciprocal(rr[:, :], rr[:, :]))
        link(dve.tensor_scalar(gb[:, :], gb[:, :], 1.0 - LAM0, None, ALU.mult))
        link(dve.tensor_tensor(y3, y3, bc(rr[:, :], HD), ALU.mult))
        dve.tensor_tensor(y3, y3, gb[:, :].unsqueeze(1).broadcast_to([P, NL * H, HD]), ALU.mult).then_inc(e.y_done, 1)
        keep_branch(nc, g, e, dve, 1)


def phase_gdn_inputs(nc, g, ctx):
    sb = lambda n, s, d=F32: ctx.enter_context(nc.sbuf_tensor("gi_" + n, s, d))
    HALF = CONV // 2
    SEG = S + 2 * HALF
    W = S + L + 2 * HALF
    NS = 6
    wg = sb("wg", [P, 2, KD, P])
    cp = sb("cp", [P, 2, W + 2 * HALF])
    acc = sb("acc", [P, W])
    cw = sb("cw", [P, NS, CONV])
    qkvc = sb("qkvc", [P, NS, T])
    sq = sb("sq", [P, 2 * BW])
    r = sb("r", [P, 2 * H])
    qn = sb("qn", [P, 2, BW])
    e, link = g.gi, g.link
    w_in = g.w_in.rearrange("(k p) n -> p k n", p=P)
    block = ctx.enter_context(nc.Block())

    @block.sync
    def _(sp):
        sp.dma_start(cw[:, :, :], g.conv_cols).then_inc(e.cw_loaded, 16)
        for s in range(NS):
            if s >= 2:
                sp.wait_ge(e.proj_done, s - 1)
            c = COL_GDN + s * P
            sp.dma_start(wg[:, s % 2], w_in[:, :, c:c + P]).then_inc(e.w_loaded[s % 2], 16)

    @block.tensor
    def _(pe):
        for s in range(NS):
            pe.wait_ge(e.w_loaded[s % 2], 16 * (s // 2 + 1))
            if s >= 2:
                pe.wait_ge(e.padded, 3 * (s - 1))
            for j in range(3):
                n = min(512, T - 512 * j)
                for k in range(KD):
                    i = pe.matmul(g.ps[:, 3 * (s % 2) + j, 0:n], wg[:, s % 2, k, :], g.hT[:, k, 512 * j:512 * j + n], start=(k == 0), stop=(k == KD - 1))
            i.then_inc(e.proj_done, 1)

        def turn_back(t):
            pe.wait_ge(e.qk_normed, t + 1)
            if t >= 2:
                pe.wait_ge(e.qkT_kept, t - 1)
            for c in range(2):
                pe.transpose(g.ps[:, t % 2, c * P:(c + 1) * P], qn[:, t % 2, c * P:(c + 1) * P], g.ident[:, :])
            for c in range(2):
                i = pe.transpose(g.ps[:, t % 2, (2 + c) * P:(3 + c) * P], g.gk[:, t, c * P:(c + 1) * P], g.ident[:, :])
            i.then_inc(e.qkT_turned, 1)

        pe.wait_ge(e.silu_done, 2 * NS)
        for t in range(NT):
            if t:
                pe.wait_ge(e.qk_normed, t)
                pe.wait_ge(e.v_kept, t)
            for c in range(NS):
                i = pe.transpose(g.ps[:, 6 + c // 4, (c % 4) * P:(c % 4 + 1) * P], qkvc[:, c, t * P:(t + 1) * P], g.ident[:, :])
            i.then_inc(e.turned, 1)
            if t:
                turn_back(t - 1)
        turn_back(NT - 1)

    @block.scalar
    def _(act):
        act.wait_ge(e.pads_zero, 1)
        for s in range(NS):
            act.wait_ge(e.proj_done, s + 1)
            if s >= 2:
                act.wait_ge(e.conv_done, s - 1)
            for j in range(3):
                n = min(512, T - 512 * j)
                o = HALF + 512 * j if j < 2 else SEG + HALF
                act.activation(cp[:, s % 2, o:o + n], g.ps[:, 3 * (s % 2) + j, 0:n], ACT.Copy).then_inc(e.padded, 1)
            act.wait_ge(e.conv_done, s + 1)
            act.activation(qkvc[:, s, 0:S], acc[:, 0:S], ACT.Silu).then_inc(e.silu_done, 1)
            act.activation(qkvc[:, s, S:T], acc[:, SEG:SEG + L], ACT.Silu).then_inc(e.silu_done, 1)
        for t in range(NT):
            act.wait_ge(e.turned, t + 1)
            if t:
                act.wait_ge(e.ss_done, t)
            act.activation(sq[:, :], g.ps[:, 6, :], ACT.Square).then_inc(e.sq_done, 1)
            act.activation(g.gv[:, t, :], g.ps[:, 7, 0:BW], ACT.Copy).then_inc(e.v_kept, 1)
            act.wait_ge(e.eps_added, t + 1)
            act.activation(r[:, :], r[:, :], ACT.Sqrt).then_inc(e.rms_done, 1)

    @block.gpsimd
    def _(pool):
        pool.memset(g.gkT[:, :, :, :], 0.0).then_inc(e.gkT_zero, 1)

    @block.vector
    def _(dve):
        dve.memset(cp[:, :, :], 0.0).then_inc(e.pads_zero, 1)
        dve.wait_ge(e.gkT_zero, 1)
        dve.wait_ge(e.cw_loaded, 16)
        for s in range(NS):
            dve.wait_ge(e.padded, 3 * (s + 1))
            if s:
                dve.wait_ge(e.silu_done, 2 * s)
            link(dve.tensor_scalar(acc[:, :], cp[:, s % 2, 0:W], cw[:, s, 0:1], None, ALU.mult))
            for i in range(1, CONV):
                ins = dve.scalar_tensor_tensor(acc[:, :], cp[:, s % 2, i:i + W], cw[:, s, i:i + 1], acc[:, :], ALU.mult, ALU.add)
                if i < CONV - 1:
                    link(ins)
            ins.then_inc(e.conv_done, 1)

        def keep_back(t):
            dve.wait_ge(e.qkT_turned, t + 1)
            for c in range(2):
                if t < NL:
                    dve.tensor_copy(g.gqT[:, c, t * P:(t + 1) * P], g.ps[:, t % 2, c * P:(c + 1) * P])
                for b in range(2):
                    q = slice(64 * b, 64 * b + 64)
                    i = dve.tensor_copy(g.gkT[q, b, c, t * P:(t + 1) * P], g.ps[q, t % 2, (2 + c) * P:(3 + c) * P])
            i.then_inc(e.qkT_kept, 1)

        for t in range(NT):
            dve.wait_ge(e.sq_done, t + 1)
            dve.tensor_reduce(r[:, :], sq[:, :].rearrange("p (g f) -> p g f", f=HD), AX.X, ALU.add).then_inc(e.ss_done, 1)
            dve.wait_ge(e.ss_done, t + 1)
            dve.tensor_scalar(r[:, :], r[:, :], EPS, None, ALU.add).then_inc(e.eps_added, 1)
            dve.wait_ge(e.rms_done, t + 1)
            link(dve.reciprocal(r[:, :], r[:, :]))
            link(dve.tensor_scalar(r[:, 0:H], r[:, 0:H], HD ** -0.5, None, ALU.mult))
            if t >= 2:
                dve.wait_ge(e.qkT_turned, t - 1)
            src = g.ps[:, 6, :].rearrange("p (g f) -> p g f", f=HD)
            dve.tensor_tensor(qn[:, t % 2, :].rearrange("p (g f) -> p g f", f=HD), src[:, 0:H], bc(r[:, 0:H], HD), ALU.mult)
            dve.tensor_tensor(g.gk[:, t, :].rearrange("p (g f) -> p g f", f=HD), src[:, H:], bc(r[:, H:], HD), ALU.mult).then_inc(e.qk_normed, 1)
            if t:
                keep_back(t - 1)
        keep_back(NT - 1)


def phase_gdn(nc, g, ctx):
    sb = lambda n, s, d=F32: ctx.enter_context(nc.sbuf_tensor("gd_" + n, s, d))
    lev = sb("lev", [P, 14, P])
    cum = sb("cum", [P, 2, P])
    ones = sb("ones", [P, P])
    two = lambda n, s: [sb(f"{n}{d}", s) for d in range(2)]
    E, ET, AT, Dm, DT, PS_ = (two(n, [P, H, P]) for n in ("E", "ET", "AT", "D", "DT", "P"))
    LT = two("LT", [P, 2, H, P])
    gbig = two("gbig", [P, H, P])
    vb, kbg, kd, vn = (two(n, [P, H, HD]) for n in ("vb", "kbg", "kd", "vn"))
    nwT = two("nwT", [P, 2, P])
    St = two("S", [P, H, HD])
    ot = two("ot", [P, BW])
    al = sb("al", [P, 8])
    dtb = sb("dtb", [P, 8])
    gx = sb("gx", [P, NT, 8])
    g8 = sb("g8", [P, NT, 8])
    be = sb("be", [P, NT, 8])
    G = sb("G", [P, NT, 8])
    eG = sb("eG", [P, NT, 8])
    eL = sb("eL", [P, NT, 8])
    eK = sb("eK", [P, NT, 8])
    beG = sb("beG", [P, NT, 8])
    onb = sb("onb", [P, HD])
    rr = sb("rr", [P, NL * H])
    sq = gbig[0]
    e, link, plink, alink = g.gd, g.link, g.plink, g.alink
    og = g.stage
    order = [[8, 9] + list(range(NL)), [9, 8] + list(range(NL))[::-1]]
    NSTEP, NLEV = NT, 7
    block = ctx.enter_context(nc.Block())

    def heads(ap, t, d):
        return ap[:, t, 4 * d:4 * d + 4]

    @block.sync
    def _(sp):
        sp.dma_start(lev[:, :, :], g.k_lev.rearrange("s p i -> p s i")).then_inc(e.loaded, 16)
        sp.dma_start(cum[:, :, :], g.k_cum.rearrange("s p i -> p s i")).then_inc(e.loaded, 16)
        sp.dma_start(al[:, :], g.gdn_a_log.rearrange("a h -> (a h)").partition_broadcast(P)).then_inc(e.loaded, 16)
        sp.dma_start(dtb[:, :], g.gdn_dt_bias.rearrange("a h -> (a h)").partition_broadcast(P)).then_inc(e.loaded, 16)
        sp.dma_start(onb[:, :], g.gdn_onorm_g.partition_broadcast(P)).then_inc(e.loaded, 16)

    @block.tensor
    def _(pe):
        pe.wait_ge(e.g_ready, 1)
        for d in range(2):
            pe.matmul(g.ps[:, 0, 40 * d:40 * d + 40].rearrange("p (t h) -> p t h", h=4), cum[:, d, :], g8[:, :, 4 * d:4 * d + 4], start=True, stop=True)
        pe.matmul(g.ps[:, 0, 80:160], ones[:, :], g8[:, :, :].rearrange("p t h -> p (t h)"), start=True, stop=True).then_inc(e.cum_done, 1)
        pe.wait_ge(e.decays_ready, 1)
        for n in range(NSTEP):
            for d in range(2):
                t = order[d][n]
                B = 3 * d
                pe.wait_ge(e.gbig_ready, 2 * n + d + 1)
                if n:
                    pe.wait_ge(e.s_kept[d], n)
                    if n > 2:
                        pe.wait_ge(e.o_kept[d], n - 2)
                for h in range(H):
                    pe.matmul(g.ps[:, B, h * P:(h + 1) * P], gbig[d][:, h, :], cum[:, d, :], start=True, stop=True)
                for h in range(H):
                    k = g.gkT[:, h % 2, h // 2, t * P:(t + 1) * P]
                    i = pe.matmul(g.ps[:, B + 1, h * P:(h + 1) * P], k, k, start=True, stop=True)
                if t < NL:
                    for h in range(H):
                        i = pe.matmul(g.ps[:, B + 2, h * P:(h + 1) * P], g.gkT[:, h % 2, h // 2, t * P:(t + 1) * P],
                                      g.gqT[:, h // 2, t * P:(t + 1) * P], start=True, stop=True)
                i.then_inc(e.prods[d], 1)
            for d in range(2):
                pe.wait_ge(e.a_ready[d], n + 1)
                for h in range(H):
                    i = pe.transpose(g.ps[:, 3 * d, h * P:(h + 1) * P], E[d][:, h, :], g.ident[:, :])
                i.then_inc(e.a_turned[d], 1)
            for s in range(1, NLEV):
                m = n * (NLEV - 1) + s
                for d in range(2):
                    pe.wait_ge(e.lt_ready[d], m)
                    pe.wait_ge(e.d_ready[d], m)
                    for h in range(H):
                        i = pe.matmul(g.ps[:, 3 * d, h * P:(h + 1) * P], LT[d][:, s % 2, h, :], Dm[d][:, h, :], start=True, stop=True)
                    i.then_inc(e.p_done[d], 1)
                for d in range(2):
                    pe.wait_ge(e.p_kept[d], m)
                    pe.wait_ge(e.dt_ready[d], m)
                    if s < NLEV - 1:
                        for h in range(H):
                            i = pe.matmul(g.ps[:, 3 * d + 1, h * P:(h + 1) * P], DT[d][:, h, :], PS_[d][:, h, :], start=True, stop=True)
                    for h in range(H):
                        i = pe.matmul(g.ps[:, 3 * d + 2, h * P:(h + 1) * P], PS_[d][:, h, :], DT[d][:, h, :], start=True, stop=True)
                    i.then_inc(e.e_done[d], 1)
            for d in range(2):
                pe.wait_ge(e.dt_last[d], n + 1)
                for h in range(H):
                    b = 64 * (h % 2)
                    i = pe.matmul(g.ps[b:b + 64, 3 * d + 1, (h // 2) * P:(h // 2 + 1) * P], kbg[d][:, h, :], DT[d][:, h, :], start=True, stop=True)
                i.then_inc(e.w_done[d], 1)
            for d in range(2):
                t = order[d][n]
                pe.wait_ge(e.w_kept[d], n + 1)
                for h in range(H):
                    o = g.ps[:, 6 + d, h * HD:(h + 1) * HD]
                    pe.matmul(o, DT[d][:, h, :], vb[d][:, h, :], start=True, stop=False)
                    i = pe.matmul(o, nwT[d][:, h // 2, :], St[d][:, h, :], start=False, stop=True)
                i.then_inc(e.v_done[d], 1)
            for d in range(2):
                t = order[d][n]
                if t < NL:
                    for h in range(H):
                        pe.matmul(g.ps[:, 3 * d, h * HD:(h + 1) * HD], g.gqT[:, h // 2, t * P:(t + 1) * P], St[d][:, h, :], start=True, stop=True)
                pe.wait_ge(e.v_kept[d], n + 1)
                if t < NL:
                    for h in range(H):
                        i = pe.matmul(g.ps[:, 3 * d, BW + h * HD:BW + (h + 1) * HD], ET[d][:, h, :], vn[d][:, h, :], start=True, stop=True)
                    i.then_inc(e.o_done[d], 1)
                for h in range(H):
                    b = 64 * (h % 2)
                    i = pe.matmul(g.ps[b:b + 64, 3 * d + 1, (h // 2) * HD:(h // 2 + 1) * HD], kd[d][:, h, :], vn[d][:, h, :], start=True, stop=True)
                i.then_inc(e.s_done[d], 1)
        pe.wait_ge(e.y_done, 1)
        turn_branch(nc, g, e, pe, og)

    @block.scalar
    def _(act):
        act.wait_ge(e.loaded, 80)
        act.wait_ge(e.sp_in, 1)
        alink(act.activation(eG[:, :, :], eG[:, :, :], ACT.Exp))
        alink(act.activation(al[:, :], al[:, :], ACT.Exp))
        act.activation(eG[:, :, :], eG[:, :, :], ACT.Ln, bias=1.0).then_inc(e.ln_done, 1)
        act.activation(be[:, :, :], g.ab[:, :, 8:16], ACT.Sigmoid).then_inc(e.beta_done, 1)
        act.activation(g.z[:, :, :], g.z[:, :, :], ACT.Silu).then_inc(e.z_done, 1)
        act.wait_ge(e.G_kept, 1)
        act.activation(eG[:, :, :], G[:, :, :], ACT.Exp).then_inc(e.exps_done, 1)
        act.activation(eL[:, :, :], eL[:, :, :], ACT.Exp).then_inc(e.exps_done, 1)
        act.activation(eK[:, :, :], eK[:, :, :], ACT.Exp).then_inc(e.exps_done, 1)
        for n in range(NSTEP):
            for d in range(2):
                act.wait_ge(e.x_ready[d], n + 1)
                act.activation(E[d][:, :, :], E[d][:, :, :], ACT.Exp).then_inc(e.exp_done[d], 1)
                act.activation(ET[d][:, :, :], ET[d][:, :, :], ACT.Exp).then_inc(e.exp_done[d], 1)
            for d in range(2):
                act.wait_ge(e.a_turned[d], n + 1)
                act.activation(AT[d][:, :, :].rearrange("p h i -> p (h i)"), g.ps[:, 3 * d, :], ACT.Copy).then_inc(e.at_kept[d], 1)
            for s in range(1, NLEV):
                m = n * (NLEV - 1) + s
                for d in range(2):
                    act.wait_ge(e.p_done[d], m)
                    act.activation(PS_[d][:, :, :].rearrange("p h i -> p (h i)"), g.ps[:, 3 * d, :], ACT.Copy).then_inc(e.p_kept[d], 1)
            for d in range(2):
                act.wait_ge(e.w_done[d], n + 1)
                act.activation(nwT[d][:, :, :].rearrange("p h i -> p (h i)"), g.ps[:, 3 * d + 1, 0:2 * P], ACT.Copy, scale=-1.0).then_inc(e.w_kept[d], 1)
        act.wait_ge(e.ms_done, 1)
        act.activation(rr[:, :], rr[:, :], ACT.Sqrt).then_inc(e.rms_done, 1)

    @block.gpsimd
    def _(pool):
        pool.wait_ge(e.decays_ready, 1)
        for n in range(NSTEP):
            for d in range(2):
                t = order[d][n]
                if n:
                    pool.wait_ge(e.prods[d], n)
                pool.tensor_copy(gbig[d][:, :, :], bc(heads(g8, t, d), P)).then_inc(e.gbig_ready, 1)
            for d in range(2):
                t = order[d][n]
                if n:
                    pool.wait_ge(e.s_done[d], n)
                k3 = g.gk[:, t, :].rearrange("p (h f) -> p h f", f=HD)
                pool.tensor_tensor(vb[d][:, :, :], g.gv[:, t, :].rearrange("p (h f) -> p h f", f=HD), bc(heads(be, t, d), HD), ALU.mult).then_inc(e.ops_ready[d], 1)
                pool.tensor_tensor(kbg[d][:, :, :], k3, bc(heads(beG, t, d), HD), ALU.mult).then_inc(e.ops_ready[d], 1)
                pool.tensor_tensor(kd[d][:, :, :], k3, bc(heads(eK, t, d), HD), ALU.mult).then_inc(e.ops_ready[d], 1)
            for d in range(2):
                pool.wait_ge(e.at_kept[d], n + 1)
                msk = lambda s: lev[:, 7 * (1 - d) + s, :].unsqueeze(1).broadcast_to([P, H, P])
                plink(pool.tensor_tensor(DT[d][:, :, :], AT[d][:, :, :], msk(0), ALU.mult))
                pool.tensor_tensor(DT[d][:, :, :], g.ident[:, :].unsqueeze(1).broadcast_to([P, H, P]), DT[d][:, :, :], ALU.subtract).then_inc(e.dt_first[d], 1)
            for s in range(1, NLEV):
                m = n * (NLEV - 1) + s
                for d in range(2):
                    if m > 2:
                        pool.wait_ge(e.p_done[d], m - 2)
                    pool.tensor_tensor(LT[d][:, s % 2, :, :], AT[d][:, :, :], lev[:, 7 * (1 - d) + s, :].unsqueeze(1).broadcast_to([P, H, P]), ALU.mult).then_inc(e.lt_ready[d], 1)

    @block.vector
    def _(dve):
        dve.memset(ones[:, :], 1.0)
        for d in range(2):
            link(dve.memset(St[d][:, :, :], 0.0))
        dve.wait_ge(e.loaded, 80)
        link(dve.tensor_tensor(gx[:, :, :], g.ab[:, :, 0:8], dtb[:, :].unsqueeze(1).broadcast_to([P, NT, 8]), ALU.add))
        link(dve.tensor_scalar(eG[:, :, :], gx[:, :, :], -1.0, None, ALU.mult))
        dve.tensor_tensor(eG[:, :, :], eG[:, :, :], gx[:, :, :], ALU.min).then_inc(e.sp_in, 1)
        dve.wait_ge(e.ln_done, 1)
        link(dve.scalar_tensor_tensor(gx[:, :, :], gx[:, :, :], 0.0, eG[:, :, :], ALU.max, ALU.add))
        link(dve.tensor_scalar(gx[:, :, :], gx[:, :, :], -1.0, None, ALU.mult))
        dve.tensor_tensor(g8[:, :, :], gx[:, :, :], al[:, :].unsqueeze(1).broadcast_to([P, NT, 8]), ALU.mult).then_inc(e.g_ready, 1)
        dve.wait_ge(e.cum_done, 1)
        for d in range(2):
            link(dve.tensor_copy(G[:, :, 4 * d:4 * d + 4], g.ps[:, 0, 40 * d:40 * d + 40].rearrange("p (t h) -> p t h", h=4)))
        link(dve.tensor_copy(eL[:, :, :], g.ps[:, 0, 80:160].rearrange("p (t h) -> p t h", h=8)))
        dve.tensor_tensor(eK[:, :, :], eL[:, :, :], G[:, :, :], ALU.subtract).then_inc(e.G_kept, 1)
        dve.wait_ge(e.exps_done, 3)
        dve.wait_ge(e.beta_done, 1)
        dve.tensor_tensor(beG[:, :, :], be[:, :, :], eG[:, :, :], ALU.mult).then_inc(e.decays_ready, 1)
        hh = lambda ap: ap[:, :, :].rearrange("p h i -> p (h i)")
        idb = g.ident[:, :].unsqueeze(1).broadcast_to([P, H, P])
        for n in range(NSTEP):
            for d in range(2):
                t = order[d][n]
                B = 3 * d
                dve.wait_ge(e.prods[d], n + 1)
                link(dve.tensor_tensor(E[d][:, :, :], bc(heads(G, t, d), P), g.ps[:, B, :].rearrange("p (h i) -> p h i", h=H), ALU.subtract))
                link(dve.tensor_scalar(ET[d][:, :, :], E[d][:, :, :], -1.0, 0.0, ALU.mult, ALU.min))
                dve.tensor_scalar(E[d][:, :, :], E[d][:, :, :], 0.0, None, ALU.min).then_inc(e.x_ready[d], 1)
            for d in range(2):
                t = order[d][n]
                B = 3 * d
                dve.wait_ge(e.exp_done[d], 2 * n + 2)
                link(dve.tensor_tensor(E[d][:, :, :], E[d][:, :, :], bc(heads(be, t, d), P), ALU.mult))
                dve.tensor_tensor(hh(E[d]), g.ps[:, B + 1, :], hh(E[d]), ALU.mult).then_inc(e.a_ready[d], 1)
                if t < NL:
                    link(dve.tensor_tensor(hh(ET[d]), g.ps[:, B + 2, :], hh(ET[d]), ALU.mult))
                    link(dve.tensor_tensor(ET[d][:, :, :], ET[d][:, :, :], cum[:, d, :].unsqueeze(1).broadcast_to([P, H, P]), ALU.mult))
                dve.wait_ge(e.a_ready[d], n + 1)
                link(dve.tensor_tensor(Dm[d][:, :, :], E[d][:, :, :], lev[:, 7 * d, :].unsqueeze(1).broadcast_to([P, H, P]), ALU.mult))
                dve.tensor_tensor(Dm[d][:, :, :], idb, Dm[d][:, :, :], ALU.subtract).then_inc(e.d_ready[d], 1)
            for d in range(2):
                dve.wait_ge(e.dt_first[d], n + 1)
                dve.tensor_copy(DT[d][0:1, 0, 0:1], DT[d][0:1, 0, 0:1]).then_inc(e.dt_ready[d], 1)
            for s in range(1, NLEV):
                m = n * (NLEV - 1) + s
                for d in range(2):
                    dve.wait_ge(e.e_done[d], m)
                    if s < NLEV - 1:
                        dve.tensor_tensor(hh(Dm[d]), hh(Dm[d]), g.ps[:, 3 * d + 1, :], ALU.subtract).then_inc(e.d_ready[d], 1)
                    dve.tensor_tensor(hh(DT[d]), hh(DT[d]), g.ps[:, 3 * d + 2, :], ALU.subtract).then_inc(e.dt_ready[d] if s < NLEV - 1 else e.dt_last[d], 1)
            for d in range(2):
                dve.wait_ge(e.v_done[d], n + 1)
                dve.tensor_copy(vn[d][:, :, :].rearrange("p h f -> p (h f)"), g.ps[:, 6 + d, 0:BW]).then_inc(e.v_kept[d], 1)
            for d in range(2):
                t = order[d][n]
                if t < NL:
                    dve.wait_ge(e.o_done[d], n - 1)
                    link(dve.tensor_tensor(ot[d][:, :].rearrange("p (h f) -> p h f", f=HD), g.ps[:, 3 * d, 0:BW].rearrange("p (h f) -> p h f", f=HD),
                                           bc(heads(eG, t, d), HD), ALU.mult))
                    if n - 2 < NL // 2:
                        i = dve.tensor_tensor(og[:, t, :], ot[d][:, :], g.ps[:, 3 * d, BW:2 * BW], ALU.add)
                    else:
                        link(dve.tensor_tensor(ot[d][:, :], ot[d][:, :], g.ps[:, 3 * d, BW:2 * BW], ALU.add))
                        i = dve.tensor_tensor(og[:, t, :], og[:, t, :], ot[d][:, :], ALU.add)
                    i.then_inc(e.o_kept[d], 1)
                dve.wait_ge(e.s_done[d], n + 1)
                for b in range(2):
                    q = slice(64 * b, 64 * b + 64)
                    link(dve.tensor_tensor(St[d][q, b:H:2, :], St[d][q, b:H:2, :], bc(eL[q, t, 4 * d + b:4 * d + 4:2], HD), ALU.mult))
                for b in range(2):
                    q = slice(64 * b, 64 * b + 64)
                    i = dve.tensor_tensor(St[d][q, b:H:2, :], St[d][q, b:H:2, :], g.ps[q, 3 * d + 1, 0:2 * HD].rearrange("p (a f) -> p a f", f=HD), ALU.add)
                i.then_inc(e.s_kept[d], 1)
        for d in range(2):
            dve.wait_ge(e.o_kept[d], NL)
        y3 = og[:, :, :].rearrange("p t (h f) -> p (t h) f", f=HD)
        for half in range(4):
            v = og[:, 2 * half:2 * half + 2, :].rearrange("p t c -> p (t c)")
            link(dve.tensor_tensor(hh(sq), v, v, ALU.mult))
            link(dve.tensor_reduce(rr[:, 8 * half:8 * half + 8], hh(sq).rearrange("p (a f) -> p a f", f=HD), AX.X, ALU.add))
        dve.tensor_scalar(rr[:, :], rr[:, :], 1.0 / HD, EPS, ALU.mult, ALU.add).then_inc(e.ms_done, 1)
        dve.wait_ge(e.rms_done, 1)
        link(dve.reciprocal(rr[:, :], rr[:, :]))
        link(dve.tensor_tensor(y3, y3, bc(rr[:, :], HD), ALU.mult))
        link(dve.tensor_tensor(y3, y3, onb[:, :].unsqueeze(1).broadcast_to([P, NL * H, HD]), ALU.mult))
        dve.wait_ge(e.z_done, 1)
        dve.tensor_tensor(og[:, :, :], og[:, :, :], g.z[:, :, :], ALU.mult).then_inc(e.y_done, 1)
        keep_branch(nc, g, e, dve, 2)


def phase_fourier(nc, g, ctx):
    sb = lambda n, s, d=F32: ctx.enter_context(nc.sbuf_tensor("fo_" + n, s, d))
    wf = sb("wf", [P, KD, BW])
    fT = sb("fT", [P, 2, S])
    bd = sb("bd", [P, 2, P])
    Z = sb("Z", [P, NL, 2, 2, P])
    dft = sb("dft", [P, 2, 2, S])
    e = g.fo
    block = ctx.enter_context(nc.Block())

    @block.sync
    def _(sp):
        sp.dma_start(wf[:, :, :], g.w_in.rearrange("(k p) n -> p k n", p=P)[:, :, COL_F:COL_F + BW]).then_inc(e.w_loaded, 16)
        sp.dma_start(bd[:, :, :], g.k_bdft.rearrange("a p i -> p a i")).then_inc(e.w_loaded, 16)
        for t in range(NL):
            if t >= 2:
                sp.wait_ge(e.dft_used, t - 1)
            sp.dma_start(dft[:, t % 2], g.k_dft[:, t * P:(t + 1) * P, :].rearrange("a p i -> p a i")).then_inc(e.dft_loaded[t % 2], 16)

    @block.tensor
    def _(pe):
        pe.wait_ge(e.w_loaded, 32)
        for c in range(2):
            for j in range(2):
                for k in range(KD):
                    i = pe.matmul(g.ps[:, 2 * c + j, :], wf[:, k, c * P:(c + 1) * P], g.hT[:, k, 512 * j:512 * j + 512], start=(k == 0), stop=(k == KD - 1))
                i.then_inc(e.f_done, 1)
        pe.wait_ge(e.f_kept, 4)
        for t in range(NL):
            if t >= 2:
                pe.wait_ge(e.z_kept, t - 1)
            for a in range(2):
                for c in range(2):
                    i = pe.matmul(g.ps[:, t % 2, (2 * a + c) * P:(2 * a + c + 1) * P], fT[:, c, t * P:(t + 1) * P], bd[:, a, :], start=True, stop=True)
            i.then_inc(e.z_done, 1)
        for t in range(NL):
            pe.wait_ge(e.z_kept, t + 1)
            pe.wait_ge(e.dft_loaded[t % 2], 16 * (t // 2 + 1))
            for a in range(2):
                for c in range(2):
                    for j in range(2):
                        i = pe.matmul(g.ps[:, 4 + 2 * c + j, :], Z[:, t, a, c, :], dft[:, t % 2, a, 512 * j:512 * j + 512],
                                      start=(t == 0 and a == 0), stop=(t == NL - 1 and a == 1))
            i.then_inc(e.dft_used, 1)

    @block.scalar
    def _(act):
        for c in range(4):
            act.wait_ge(e.f_done, c + 1)
            act.activation(fT[:, c // 2, 512 * (c % 2):512 * (c % 2) + 512], g.ps[:, c, :], ACT.Copy).then_inc(e.f_kept, 1)

    @block.vector
    def _(dve):
        for t in range(NL):
            dve.wait_ge(e.z_done, t + 1)
            dve.tensor_copy(Z[:, t].rearrange("p a c i -> p (a c i)"), g.ps[:, t % 2, :]).then_inc(e.z_kept, 1)
        dve.wait_ge(e.dft_used, NL)
        for c in range(2):
            for j in range(2):
                dve.tensor_copy(g.brT[:, 6 + c, 512 * j:512 * j + 512], g.ps[:, 4 + 2 * c + j, :])


def phase_merge(nc, g, ctx):
    sb = lambda n, s, d=F32: ctx.enter_context(nc.sbuf_tensor("me_" + n, s, d))
    wg = sb("wg", [P, 4, KD, P])
    wb = sb("wb", [P, 4, 2, P])
    gs = sb("gs", [P, 2, S])
    pt = sb("pt", [P, 2, S])
    e = g.me
    w_in = g.w_in.rearrange("(k p) n -> p k n", p=P)
    U = [(c, b) for c in range(KD) for b in range(4)]
    block = ctx.enter_context(nc.Block())

    @block.sync
    def _(sp):
        for u, (c, b) in enumerate(U):
            if u >= 4:
                sp.wait_ge(e.proj_done, u - 3)
            o = COL_G + b * D + c * P
            sp.dma_start(wg[:, u % 4], w_in[:, :, o:o + P]).then_inc(e.w_loaded[u % 4], 16)
            sp.dma_start(wb[:, u % 4], g.w_branch[b].rearrange("(k p) n -> p k n", p=P)[:, :, c * P:(c + 1) * P]).then_inc(e.w_loaded[u % 4], 16)

    @block.tensor
    def _(pe):
        for u, (c, b) in enumerate(U):
            s = 2 * (u % 2)
            pe.wait_ge(e.w_loaded[u % 4], 32 * (u // 4 + 1))
            if u >= 2:
                pe.wait_ge(e.gate_done, u - 1)
            for j in range(2):
                for k in range(KD):
                    i = pe.matmul(g.ps[:, s + j, :], wg[:, u % 4, k, :], g.hT[:, k, 512 * j:512 * j + 512], start=(k == 0), stop=(k == KD - 1))
            i.then_inc(e.gate_in, 1)
            if u >= 2:
                pe.wait_ge(e.mult_done, u - 1)
            for j in range(2):
                for k in range(2):
                    i = pe.matmul(g.ps[:, 4 + s + j, :], wb[:, u % 4, k, :], g.brT[:, 2 * b + k, 512 * j:512 * j + 512], start=(k == 0), stop=(k == 1))
            i.then_inc(e.proj_done, 1)

    @block.scalar
    def _(act):
        for u in range(len(U)):
            act.wait_ge(e.gate_in, u + 1)
            if u >= 2:
                act.wait_ge(e.mult_done, u - 1)
            act.activation(gs[:, u % 2, :], g.ps[:, 2 * (u % 2):2 * (u % 2) + 2, :].rearrange("p a b -> p (a b)"), ACT.Sigmoid).then_inc(e.gate_done, 1)

    @block.vector
    def _(dve):
        for u, (c, b) in enumerate(U):
            dve.wait_ge(e.gate_done, u + 1)
            dve.wait_ge(e.proj_done, u + 1)
            if u >= 2:
                dve.wait_ge(e.added, u - 1)
            dst = g.yT[:, c, :] if b == 0 else pt[:, u % 2, :]
            dve.tensor_tensor(dst, gs[:, u % 2, :], g.ps[:, 4 + 2 * (u % 2):6 + 2 * (u % 2), :].rearrange("p a b -> p (a b)"), ALU.mult).then_inc(e.mult_done, 1)

    @block.gpsimd
    def _(pool):
        for u, (c, b) in enumerate(U):
            pool.wait_ge(e.mult_done, u + 1)
            if u:
                pool.wait_ge(e.added, u)
            if b == 0:
                pool.sem_inc(e.added, 1)
            else:
                pool.tensor_tensor(g.yT[:, c, :], g.yT[:, c, :], pt[:, u % 2, :], ALU.add).then_inc(e.added, 1)


def phase_out(nc, g, ctx):
    sb = lambda n, s, d=F32: ctx.enter_context(nc.sbuf_tensor("ou_" + n, s, d))
    wo = sb("wo", [P, KD, D])
    xt = sb("xt", [P, 2, D])
    junk = sb("junk", [P, D])
    ss = sb("ss", [P, NL])
    a2 = sb("a2", [P, D])
    wr = sb("wr", [P, KD, NEXP])
    hTt = sb("hTt", [P, KD, P])
    e, link = g.ou, g.link
    g1, sh2, sc2 = g.modb[:, 0:D], g.modb[:, D:2 * D], g.modb[:, 2 * D:3 * D]
    h2 = g.h2
    block = ctx.enter_context(nc.Block())

    @block.sync
    def _(sp):
        sp.dma_start(wo[:, :, :], g.w_out.rearrange("(k p) n -> p k n", p=P)).then_inc(e.w_loaded, 16)
        sp.dma_start(a2[:, :], g.norm2_g.partition_broadcast(P)).then_inc(e.w_loaded, 16)
        sp.dma_start(wr[:, :, :], g.w_router.rearrange("(k p) n -> p k n", p=P)).then_inc(e.w_loaded, 16)
        for t in range(NL):
            if t >= 2:
                sp.wait_ge(e.x1_done, t - 1)
            sp.dma_start(xt[:, t % 2], g.x[0, t * P:(t + 1) * P, :]).then_inc(e.x_loaded[t % 2], 16)
        for t in range(NL):
            sp.wait_ge(e.x1_done, t + 1)
            sp.dma_start(g.x1_dram[t * P:(t + 1) * P, :], g.x1[:, t, :]).then_inc(e.x1_stored, 16)
        sp.wait_ge(e.x1_stored, 16 * NL)

    @block.tensor
    def _(pe):
        pe.wait_ge(e.w_loaded, 48)

        def route(t):
            pe.wait_ge(e.h2_done, t + 1)
            if t:
                pe.wait_ge(e.hT_act, t)
                pe.wait_ge(e.hT_dve, t)
            for k in range(KD):
                i = pe.transpose(g.ps[:, 4 + k // 4, (k % 4) * P:(k % 4 + 1) * P], h2[:, t, k * P:(k + 1) * P], g.ident[:, :])
            i.then_inc(e.turned, 1)
            pe.wait_ge(e.hT_act, t + 1)
            pe.wait_ge(e.hT_dve, t + 1)
            if t:
                pe.wait_ge(e.scored, t)
            for k in range(KD):
                i = pe.matmul(g.ps[:, 6, 0:NEXP], hTt[:, k, :], wr[:, k, :], start=(k == 0), stop=(k == KD - 1))
            i.then_inc(e.logits, 1)

        for t in range(NL):
            if t >= 2:
                pe.wait_ge(e.y_read, t - 1)
            for j in range(2):
                for k in range(KD):
                    i = pe.matmul(g.ps[:, 2 * (t % 2) + j, :], g.yT[:, k, t * P:(t + 1) * P], wo[:, k, 512 * j:512 * j + 512], start=(k == 0), stop=(k == KD - 1))
            i.then_inc(e.y_done, 1)
            if t:
                route(t - 1)
        route(NL - 1)

    @block.scalar
    def _(act):
        def keep(t):
            act.wait_ge(e.turned, t + 1)
            if t:
                act.wait_ge(e.logits, t)
            act.activation(hTt[:, 4:8, :].rearrange("p k i -> p (k i)"), g.ps[:, 5, :], ACT.Copy).then_inc(e.hT_act, 1)
            act.wait_ge(e.logits, t + 1)
            act.activation(g.scores[:, t, :], g.ps[:, 6, 0:NEXP], ACT.Sigmoid).then_inc(e.scored, 1)

        for t in range(NL):
            act.wait_ge(e.x1_done, t + 1)
            if t:
                act.wait_ge(e.sq_done, t)
            act.activation(junk[:, :], g.x1[:, t, :], ACT.Square, accum_out=ss[:, t:t + 1]).then_inc(e.sq_done, 1)
            act.wait_ge(e.ms_done, t + 1)
            act.activation(ss[:, t:t + 1], ss[:, t:t + 1], ACT.Sqrt).then_inc(e.rms_done, 1)
            if t:
                keep(t - 1)
        keep(NL - 1)

    @block.vector
    def _(dve):
        dve.wait_ge(e.w_loaded, 48)
        link(dve.scalar_tensor_tensor(a2[:, :], sc2, 1.0, a2[:, :], ALU.add, ALU.mult))

        def keep(t):
            dve.wait_ge(e.turned, t + 1)
            if t:
                dve.wait_ge(e.logits, t)
            dve.tensor_copy(hTt[:, 0:4, :].rearrange("p k i -> p (k i)"), g.ps[:, 4, :]).then_inc(e.hT_dve, 1)

        for t in range(NL):
            dve.wait_ge(e.y_done, t + 1)
            x1 = g.x1[:, t, :]
            dve.tensor_tensor(x1, g.ps[:, 2 * (t % 2):2 * (t % 2) + 2, :].rearrange("p a b -> p (a b)"), g1, ALU.mult).then_inc(e.y_read, 1)
            dve.wait_ge(e.y_read, t + 1)
            dve.wait_ge(e.x_loaded[t % 2], 16 * (t // 2 + 1))
            dve.tensor_tensor(x1, x1, xt[:, t % 2], ALU.add).then_inc(e.x1_done, 1)
            if t:
                keep(t - 1)
            dve.wait_ge(e.sq_done, t + 1)
            dve.tensor_scalar(ss[:, t:t + 1], ss[:, t:t + 1], 1.0 / D, EPS, ALU.mult, ALU.add).then_inc(e.ms_done, 1)
            dve.wait_ge(e.rms_done, t + 1)
            link(dve.reciprocal(ss[:, t:t + 1], ss[:, t:t + 1]))
            link(dve.scalar_tensor_tensor(h2[:, t, :], x1, ss[:, t:t + 1], a2[:, :], ALU.mult, ALU.mult))
            dve.tensor_tensor(h2[:, t, :], h2[:, t, :], sh2, ALU.add).then_inc(e.h2_done, 1)
        keep(NL - 1)


def phase_route(nc, g, ctx):
    sb = lambda n, s, d=F32: ctx.enter_context(nc.sbuf_tensor("ro_" + n, s, d))
    sel = sb("sel", [P, NL, NEXP])
    rb = sb("rb", [P, NEXP])
    pair = sb("pair", [P, 6, NL * NGRP])
    gsc = sb("gsc", [P, NL, NGRP])
    gm = sb("gm", [P, NL])
    one4 = sb("one4", [P, NL, NGRP])
    idx = sb("idx", [P, 2, NEXP])
    t4 = sb("t4", [P, NL, NGRP])
    tE = sb("tE", [P, NL, NEXP])
    m1 = sb("m1", [P, NL])
    oh = sb("oh", [P, 2, NL, NEXP])
    A = sb("A", [P, NL, NEXP])
    tri = sb("tri", [P, 2, P])
    pos = sb("pos", [P, NL, NEXP])
    tot = sb("tot", [P, NL + 1, NEXP])
    nb = sb("nb", [P, NEXP])
    nb2 = sb("nb2", [P, NEXP])
    pe_ = sb("pend", [P, NEXP])
    ps_ = sb("pstart", [P, NEXP])
    cmp3 = sb("cmp3", [P, 8, NEXP])
    blk = sb("blk", [P, 32])
    bcmp = sb("bcmp", [P, 32, NEXP])
    bexp = sb("bexp", [P, 32])
    dst = sb("dst", [P, 2, NL])
    ws = sb("ws", [P, 3, NL])
    zt = sb("zt", [P, 2 * D])
    e, link = g.ro, g.link
    block = ctx.enter_context(nc.Block())
    NEGB = 1e30

    @block.sync
    def _(sp):
        sp.dma_start(rb[:, :], g.router_bias.partition_broadcast(P)).then_inc(e.loaded, 16)
        sp.dma_start(blk[:, :], g.k_blk).then_inc(e.loaded, 16)
        sp.dma_start(tri[:, 0, :], g.k_cum[0]).then_inc(e.loaded, 16)
        sp.wait_ge(e.zero_made, 1)
        rows = g.xs.rearrange("(n p r) d -> n p (r d)", p=P, r=2)
        for n in range(NBLK_RUN // 2):
            sp.dma_start(rows[n], zt[:, :]).then_inc(e.zeroed, 16)
        sp.wait_ge(e.zeroed, 16 * (NBLK_RUN // 2))

    @block.gpsimd
    def _(pool):
        pool.memset(zt[:, :], 0.0).then_inc(e.zero_made, 1)
        pool.wait_ge(e.zeroed, 16 * (NBLK_RUN // 2))
        pool.wait_ge(e.dst_done, 1)
        for k in range(2):
            for t in range(NL):
                pool.indirect_dma_start(g.xs[:, :], bass.IndirectOffsetOnAxis(ap=g.dsti[:, k * NL + t:k * NL + t + 1], axis=0), g.h2[:, t, :], None).then_inc(e.scattered, 16)
        pool.wait_ge(e.scattered, 32 * NL)

    @block.tensor
    def _(pe):
        pe.wait_ge(e.a_done, 1)
        v = A[:, :, :].rearrange("p t e -> p (t e)")
        pe.matmul(g.ps[:, 0, 0:P], tri[:, 0, :], v, start=True, stop=True)
        pe.matmul(g.ps[:, 0, P:2 * P], tri[:, 1, :], v, start=True, stop=True).then_inc(e.counted, 1)

    @block.vector
    def _(dve):
        tt, ts, tr = dve.tensor_tensor, dve.tensor_scalar, dve.tensor_reduce
        sc = g.scores
        for i in range(NEXP):
            dve.memset(idx[:, 0, i:i + 1], float(i))
            link(dve.memset(idx[:, 1, i:i + 1], float(NEXP - i)))
        link(dve.memset(tri[:, 1, :], 1.0))
        dve.wait_ge(e.loaded, 48)
        link(tt(sel[:, :, :], sc[:, :, :], rb[:, :].unsqueeze(1).broadcast_to([P, NL, NEXP]), ALU.add))
        s4 = sel[:, :, :].rearrange("p t (g m) -> p (t g) m", m=PERG)
        for n, (a, b) in enumerate(((0, 1), (0, 2), (0, 3), (1, 2), (1, 3), (2, 3))):
            link(tt(pair[:, n, :], s4[:, :, a], s4[:, :, b], ALU.add))
        gf = gsc[:, :, :].rearrange("p t g -> p (t g)")
        link(tr(gf, pair[:, :, :].rearrange("p n x -> p x n"), AX.X, ALU.max))
        link(tr(gm[:, :], gsc[:, :, :], AX.X, ALU.max))

        def first_of(out, val, m, n, tmp):
            w = idx[:, 1, 0:n].unsqueeze(1).broadcast_to([P, NL, n])
            link(tt(tmp, val, bc(m, n), ALU.is_equal))
            link(tt(tmp, tmp, w, ALU.mult))
            link(tr(m, tmp, AX.X, ALU.max))
            link(tt(out, w, bc(m, n), ALU.is_equal))

        first_of(one4[:, :, :], gsc[:, :, :], gm[:, :], NGRP, t4[:, :, :])
        ig = bc(one4[:, :, :].rearrange("p t g -> p (t g)"), PERG)
        link(tt(s4, s4, ig, ALU.mult))
        link(ts(t4[:, :, :], one4[:, :, :], 1.0, NEGB, ALU.subtract, ALU.mult))
        link(tt(s4, s4, bc(t4[:, :, :].rearrange("p t g -> p (t g)"), PERG), ALU.add))
        for k in range(2):
            link(tr(m1[:, :], sel[:, :, :], AX.X, ALU.max))
            first_of(oh[:, k], sel[:, :, :], m1[:, :], NEXP, tE[:, :, :])
            if k == 0:
                link(ts(tE[:, :, :], oh[:, 0], -3.0 * NEGB, None, ALU.mult))
                link(tt(sel[:, :, :], sel[:, :, :], tE[:, :, :], ALU.add))
        link(tt(A[:, :, :], oh[:, 0], oh[:, 1], ALU.add))
        link(tt(tri[:, 0, :], tri[:, 0, :], g.ident[:, :], ALU.subtract))
        dve.tensor_copy(A[:, :, :], A[:, :, :]).then_inc(e.a_done, 1)
        for k in range(2):
            link(tt(tE[:, :, :], oh[:, k], sc[:, :, :], ALU.mult))
            link(tr(ws[:, k, :], tE[:, :, :], AX.X, ALU.add))
        link(tt(ws[:, 2, :], ws[:, 0, :], ws[:, 1, :], ALU.add))
        link(dve.reciprocal(ws[:, 2, :], ws[:, 2, :]))
        for k in range(2):
            link(tt(g.wts[:, k, :], ws[:, k, :], ws[:, 2, :], ALU.mult))
        dve.wait_ge(e.counted, 1)
        link(dve.tensor_copy(pos[:, :, :].rearrange("p t e -> p (t e)"), g.ps[:, 0, 0:P]))
        link(dve.memset(tot[:, 0, :], 0.0))
        for t in range(NL):
            link(tt(tot[:, t + 1, :], g.ps[:, 0, P + t * NEXP:P + (t + 1) * NEXP], tot[:, t, :], ALU.add))
        link(tt(pos[:, :, :], pos[:, :, :], tot[:, 0:NL, :], ALU.add))
        link(tt(cmp3[:, :, :], tot[:, NL, :].unsqueeze(1).broadcast_to([P, 8, NEXP]), bc(g_mult128(g, dve, link, blk), NEXP), ALU.is_gt))
        link(tr(nb[:, :], cmp3[:, :, :].rearrange("p j e -> p e j"), AX.X, ALU.add))
        link(dve.tensor_copy(pe_[:, :], nb[:, :]))
        a, b = pe_, nb2
        for s in (1, 2, 4, 8):
            link(dve.tensor_copy(b[:, 0:s], a[:, 0:s]))
            link(tt(b[:, s:], a[:, s:], a[:, 0:NEXP - s], ALU.add))
            a, b = b, a
        link(tt(ps_[:, :], a[:, :], nb[:, :], ALU.subtract))
        link(ts(ps_[:, :], ps_[:, :], float(P), None, ALU.mult))
        link(ts(a[:, :], a[:, :], float(P), None, ALU.mult))
        link(tt(bcmp[:, :, :], bc(blk[:, :], NEXP), a[:, :].unsqueeze(1).broadcast_to([P, 32, NEXP]), ALU.is_ge))
        link(tr(bexp[:, :], bcmp[:, :, :], AX.X, ALU.add))
        link(ts(bexp[:, :], bexp[:, :], float(NEXP - 1), None, ALU.min))
        link(dve.tensor_copy(g.bexpi[:, :], bexp[0:1, :]))
        link(tt(pos[:, :, :], pos[:, :, :], ps_[:, :].unsqueeze(1).broadcast_to([P, NL, NEXP]), ALU.add))
        for k in range(2):
            link(tt(tE[:, :, :], oh[:, k], pos[:, :, :], ALU.mult))
            link(tr(dst[:, k, :], tE[:, :, :], AX.X, ALU.add))
        dve.tensor_copy(g.dsti[:, :], dst[:, :, :].rearrange("p k t -> p (k t)")).then_inc(e.dst_done, 1)


def g_mult128(g, dve, link, blk):
    link(dve.tensor_scalar(blk[:, :], blk[:, :], float(P), None, ALU.mult))
    return blk[:, 0:8]


NBLK_RUN = NBLK + NBLK % 2


def phase_experts(nc, g, ctx):
    sb = lambda n, s, d=F32: ctx.enter_context(nc.sbuf_tensor("ex_" + n, s, d))
    Wg = [sb(f"Wg{s}", [P, KD, FF]) for s in range(2)]
    Wu = [sb(f"Wu{s}", [P, KD, FF]) for s in range(2)]
    Wd = [sb(f"Wd{s}", [P, FF // P, D]) for s in range(2)]
    xt = [sb(f"xt{s}", [P, D]) for s in range(2)]
    xT = sb("xT", [P, KD, P])
    gs = sb("gs", [P, FF])
    hh = sb("hh", [P, FF])
    hT = sb("hT", [P, FF // P, P])
    yo = sb("yo", [P, 2, D])
    e = g.ex
    xs = g.xs.rearrange("(n p) d -> n p d", p=P)
    ys = g.ys.rearrange("(n p) d -> n p d", p=P)
    wgv = g.moe_w_gate.rearrange("e (k p) f -> e p k f", p=P)
    wuv = g.moe_w_up.rearrange("e (k p) f -> e p k f", p=P)
    wdv = g.moe_w_down.rearrange("e (k p) f -> e p k f", p=P)
    block = ctx.enter_context(nc.Block())
    N2 = NBLK_RUN // 2

    def load(sp, i, s):
        ex = sp.value_load(g.bexpi[0:1, bass.ds(i, 1)], min_val=0, max_val=NEXP - 1)
        one = lambda v, j: v[bass.ds(j, 1)].rearrange("o p a -> (o p) a") if len(v.shape) == 3 else v[bass.ds(j, 1)].rearrange("o p k f -> (o p) k f")
        sp.dma_start(xt[s][:, :], one(xs, i)).then_inc(e.x_loaded[s], 16)
        sp.dma_start(Wg[s][:, :, :], one(wgv, ex)).then_inc(e.g_loaded[s], 16)
        sp.dma_start(Wu[s][:, :, :], one(wuv, ex)).then_inc(e.u_loaded[s], 16)
        sp.dma_start(Wd[s][:, :, :], one(wdv, ex)).then_inc(e.d_loaded[s], 16)

    @block.sync
    def _(sp):
        for s in range(2):
            load(sp, s, s)
        with sp.Fori(1, N2) as j:
            for s in range(2):
                sp.wait_ge(e.down_done, 2 * j + s - 1)
                load(sp, 2 * j + s, s)

    @block.tensor
    def _(pe):
        with pe.Fori(0, N2) as j:
            for s in range(2):
                b = 2 * j + s
                pe.wait_ge(e.x_loaded[s], 16 * j + 16)
                for k in range(KD):
                    i = pe.transpose(g.ps[:, k // 4, (k % 4) * P:(k % 4 + 1) * P], xt[s][:, k * P:(k + 1) * P], g.ident[:, :])
                i.then_inc(e.x_turned, 1)
                pe.wait_ge(e.xT_act, b + 1)
                pe.wait_ge(e.xT_dve, b + 1)
                pe.wait_ge(e.g_loaded[s], 16 * j + 16)
                for k in range(KD):
                    i = pe.matmul(g.ps[:, 2, :], xT[:, k, :], Wg[s][:, k, :], start=(k == 0), stop=(k == KD - 1))
                i.then_inc(e.gate_done, 1)
                pe.wait_ge(e.u_loaded[s], 16 * j + 16)
                for k in range(KD):
                    i = pe.matmul(g.ps[:, 3, :], xT[:, k, :], Wu[s][:, k, :], start=(k == 0), stop=(k == KD - 1))
                i.then_inc(e.up_done, 1)
                pe.wait_ge(e.h_done, b + 1)
                for k in range(FF // P):
                    i = pe.transpose(g.ps[:, 4, k * P:(k + 1) * P], hh[:, k * P:(k + 1) * P], g.ident[:, :])
                i.then_inc(e.h_turned, 1)
                pe.wait_ge(e.hT_kept, b + 1)
                pe.wait_ge(e.d_loaded[s], 16 * j + 16)
                for n in range(2):
                    for k in range(FF // P):
                        i = pe.matmul(g.ps[:, 5 + n, :], hT[:, k, :], Wd[s][:, k, 512 * n:512 * n + 512], start=(k == 0), stop=(k == FF // P - 1))
                i.then_inc(e.down_done, 1)

    @block.scalar
    def _(act):
        for s in range(2):
            act.sem_inc(e.y_free[s], 16)
        with act.Fori(0, N2) as j:
            for s in range(2):
                b = 2 * j + s
                act.wait_ge(e.x_turned, b + 1)
                act.activation(xT[:, 4:8, :].rearrange("p k i -> p (k i)"), g.ps[:, 1, :], ACT.Copy).then_inc(e.xT_act, 1)
                act.wait_ge(e.gate_done, b + 1)
                act.activation(gs[:, :], g.ps[:, 2, :], ACT.Silu).then_inc(e.silu_done, 1)
                act.wait_ge(e.h_turned, b + 1)
                act.activation(hT[:, :, :].rearrange("p k i -> p (k i)"), g.ps[:, 4, :], ACT.Copy).then_inc(e.hT_kept, 1)
                act.wait_ge(e.down_done, b + 1)
                act.wait_ge(e.y_free[s], 16 * j + 16)
                act.activation(yo[:, s, 0:512], g.ps[:, 5, :], ACT.Copy).then_inc(e.y_act, 1)
                act.wait_ge(e.y_act, b + 1)
                act.wait_ge(e.y_dve, b + 1)
                act.dma_start(ys[bass.ds(b, 1)].rearrange("o p a -> (o p) a"), yo[:, s, :]).then_inc(e.y_free[s], 16)
        for s in range(2):
            act.wait_ge(e.y_free[s], 16 * (N2 + 1))

    @block.vector
    def _(dve):
        with dve.Fori(0, N2) as j:
            for s in range(2):
                b = 2 * j + s
                dve.wait_ge(e.x_turned, b + 1)
                dve.tensor_copy(xT[:, 0:4, :].rearrange("p k i -> p (k i)"), g.ps[:, 0, :]).then_inc(e.xT_dve, 1)
                dve.wait_ge(e.silu_done, b + 1)
                dve.wait_ge(e.up_done, b + 1)
                dve.tensor_tensor(hh[:, :], gs[:, :], g.ps[:, 3, :], ALU.mult).then_inc(e.h_done, 1)
                dve.wait_ge(e.down_done, b + 1)
                dve.wait_ge(e.y_free[s], 16 * j + 16)
                dve.tensor_copy(yo[:, s, 512:1024], g.ps[:, 6, :]).then_inc(e.y_dve, 1)


def phase_combine(nc, g, ctx):
    sb = lambda n, s, d=F32: ctx.enter_context(nc.sbuf_tensor("co_" + n, s, d))
    ya = sb("ya", [P, 2, 4, D])
    x1 = sb("x1", [P, 4, D])
    g2 = g.modb[:, 3 * D:4 * D]
    e, link = g.co, g.link
    block = ctx.enter_context(nc.Block())

    @block.gpsimd
    def _(pool):
        for t in range(NL):
            if t >= 4:
                pool.wait_ge(e.out_done, t - 3)
            for k in range(2):
                pool.indirect_dma_start(ya[:, k, t % 4, :], None, g.ys[:, :], bass.IndirectOffsetOnAxis(ap=g.dsti[:, k * NL + t:k * NL + t + 1], axis=0)).then_inc(e.y_loaded[t % 4], 16)

    @block.sync
    def _(sp):
        for t in range(NL):
            if t >= 4:
                sp.wait_ge(e.stored[t % 4], 16)
            sp.dma_start(x1[:, t % 4], g.x1_dram[t * P:(t + 1) * P, :]).then_inc(e.x_loaded[t % 4], 16)

    @block.vector
    def _(dve):
        for t in range(NL):
            s = t % 4
            dve.wait_ge(e.y_loaded[s], 32 * (t // 4 + 1))
            link(dve.tensor_scalar(ya[:, 0, s, :], ya[:, 0, s, :], g.wts[:, 0, t:t + 1], None, ALU.mult))
            link(dve.scalar_tensor_tensor(ya[:, 1, s, :], ya[:, 1, s, :], g.wts[:, 1, t:t + 1], ya[:, 0, s, :], ALU.mult, ALU.add))
            link(dve.tensor_tensor(ya[:, 1, s, :], ya[:, 1, s, :], g2, ALU.mult))
            dve.wait_ge(e.x_loaded[s], 16 * (t // 4 + 1))
            dve.tensor_tensor(x1[:, s, :], x1[:, s, :], ya[:, 1, s, :], ALU.add).then_inc(e.out_done, 1)

    @block.scalar
    def _(act):
        for t in range(NL):
            act.wait_ge(e.out_done, t + 1)
            act.dma_start(g.out[0, t * P:(t + 1) * P, :], x1[:, t % 4]).then_inc(e.stored[t % 4], 16)
        for s in range(4):
            act.wait_ge(e.stored[s], 32)


def phase_events(nc, prefix, names):
    made = {}
    for word in names.split():
        name, _, count = word.partition("*")
        sems = [nc.alloc_semaphore(name=f"{prefix}_{name}{j}") for j in range(int(count or 1))]
        made[name] = sems if count else sems[0]
    return named(**made, every=[s for v in made.values() for s in (v if isinstance(v, list) else [v])])


def phase_end(nc, events):
    nc.clear_and_free_semaphores(events.every)
    nc.all_engine_barrier()


def trunk(nc, g):
    top = ExitStack()
    with top:
        sem = lambda n: top.enter_context(nc.semaphore(n))
        g.link = Chain(nc.vector, sem("dve_order"))
        g.alink = Chain(nc.scalar, sem("act_order"))
        g.plink = Chain(nc.gpsimd, sem("pool_order"))
        g.rpb_rep = nc.dram_tensor("rpb_rep", (H, 20, GRID_W, P), F32).ap()
        g.rpb_pad = nc.dram_tensor("rpb_pad", (H, 20, P), F32).ap()
        g.ps = top.enter_context(nc.psum_tensor("ps", [P, 8, 512], F32))
        keep = lambda n, s, d=F32: top.enter_context(nc.sbuf_tensor(n, s, d))
        g.ident = keep("ident", [P, P])
        g.acol = keep("acol", [P, KD, 2])
        g.bcol = keep("bcol", [P, KD, 2])
        g.modb = keep("modb", [P, 4 * D])
        g.scores = keep("scores", [P, NL, NEXP])
        g.wts = keep("wts", [P, 2, NL])
        g.dsti = keep("dsti", [P, 2 * NL], U32)
        g.bexpi = keep("bexpi", [1, 32], I32)
        g.xs = nc.dram_tensor("xs", (NBLK_RUN * P, D), F32).ap()
        g.ys = nc.dram_tensor("ys", (NBLK_RUN * P, D), F32).ap()
        g.x1_dram = nc.dram_tensor("x1_dram", (S, D), F32).ap()
        mid = ExitStack()
        keep = lambda n, s, d=F32: mid.enter_context(nc.sbuf_tensor(n, s, d))
        g.z = keep("z", [P, NL, BW])
        g.ab = keep("ab", [P, NT, 16])
        g.hT = keep("hT", [P, KD, T])
        region = keep("region", [P, NT * D])
        g.xall = region[:, :].rearrange("p (t d) -> p t d", t=NT)
        g.stage = region[:, 8 * S:].rearrange("p (t c) -> p t c", t=NL)
        g.brT = region[:, 0:8 * S].rearrange("p (b t) -> p b t", b=8)
        with ExitStack() as att:
            a = lambda n, s, d=F32: att.enter_context(nc.sbuf_tensor(n, s, d))
            g.attmem = a("attmem", [P, 4 * S + 8 * T])
            turned = lambda at, n: g.attmem[:, at:at + 2 * n].rearrange("p (a t) -> p a t", a=2)
            tokens = lambda at: g.attmem[:, at:at + NT * BW].rearrange("p (t c) -> p t c", t=NT)
            g.naQ, g.naK = turned(0, S), turned(2 * S, T)
            g.daQ, g.daK = turned(2 * (S + T), S), turned(4 * S + 2 * T, T)
            g.naV, g.daV = tokens(4 * (S + T)), tokens(4 * (S + T) + NT * BW)
            g.mo = phase_events(nc, "mo", "c_loaded x_loaded small_loaded bmod_loaded ident_loaded silu_done sums_done meansq_done rms_done "
                                          "rstd_done xn_done sbig_done mod_done mod_kept modT_done wmod_loaded*3")
            with ExitStack() as ctx:
                phase_modulation(nc, g, ctx)
            phase_end(nc, g.mo)
            for which in range(2):
                g.qkv = phase_events(nc, f"qkv{which}", "w_loaded hT_turned hT_act hT_dve qk_done ss_done sq_done v_done v_kept ms_done rms_done "
                                                  "qk_kept qT_turned qT_kept rope_done")
                with ExitStack() as ctx:
                    phase_qkv(nc, g, ctx, which)
                phase_end(nc, g.qkv)
            g.na = phase_events(nc, "na", "pad_done rep_done bm_ready bm_used s_done exp_done max_done pt_turned pt_act pt_dve o_done o_kept br_turned bm_loaded*2")
            with ExitStack() as ctx:
                phase_na(nc, g, ctx)
            phase_end(nc, g.na)
            g.da = phase_events(nc, "da", "small_loaded dots_done lam_exp s_done exp_done max_done pt_turned pt_kept p0_done r_done a_done o_done o_kept "
                              "ms_done rms_done y_done br_turned")
            with ExitStack() as ctx:
                phase_da(nc, g, ctx)
            phase_end(nc, g.da)
        with ExitStack() as delta:
            a = lambda n, s, d=F32: delta.enter_context(nc.sbuf_tensor(n, s, d))
            g.gqT = g.brT[:, 6:8, :]
            g.gkT = a("gkT", [P, 2, 2, T])
            g.gk, g.gv = a("gk", [P, NT, BW]), a("gv", [P, NT, BW])
            g.gi = phase_events(nc, "gi", "cw_loaded proj_done padded conv_done pads_zero gkT_zero silu_done turned ss_done sq_done v_kept eps_added rms_done "
                              "qk_normed qkT_turned qkT_kept w_loaded*2")
            with ExitStack() as ctx:
                phase_gdn_inputs(nc, g, ctx)
            phase_end(nc, g.gi)
            g.gd = phase_events(nc, "gd", "loaded g_ready cum_done decays_ready gbig_ready sp_in ln_done beta_done z_done G_kept exps_done ms_done "
                              "rms_done y_done br_turned s_kept*2 o_kept*2 prods*2 a_ready*2 a_turned*2 lt_ready*2 d_ready*2 p_done*2 "
                              "p_kept*2 dt_ready*2 dt_first*2 dt_last*2 e_done*2 w_done*2 w_kept*2 v_done*2 v_kept*2 o_done*2 s_done*2 "
                              "x_ready*2 exp_done*2 at_kept*2 ops_ready*2")
            with ExitStack() as ctx:
                phase_gdn(nc, g, ctx)
            phase_end(nc, g.gd)
        g.fo = phase_events(nc, "fo", "w_loaded dft_used f_done f_kept z_done z_kept dft_loaded*2")
        with ExitStack() as ctx:
            phase_fourier(nc, g, ctx)
        phase_end(nc, g.fo)
        with ExitStack() as merged:
            g.yT = merged.enter_context(nc.sbuf_tensor("yT", [P, KD, S], F32))
            g.me = phase_events(nc, "me", "proj_done gate_in gate_done mult_done added w_loaded*4")
            with ExitStack() as ctx:
                phase_merge(nc, g, ctx)
            phase_end(nc, g.me)
            g.x1 = region[:, 0:NL * D].rearrange("p (t d) -> p t d", t=NL)
            g.h2 = g.hT[:, :, :].rearrange("p k t -> p (k t)")[:, 0:NL * D].rearrange("p (t d) -> p t d", t=NL)
            g.ou = phase_events(nc, "ou", "w_loaded x1_done x1_stored h2_done hT_act hT_dve turned logits scored y_read y_done sq_done ms_done "
                                    "rms_done x_loaded*2")
            with ExitStack() as ctx:
                phase_out(nc, g, ctx)
            phase_end(nc, g.ou)
        g.ro = phase_events(nc, "ro", "loaded zero_made zeroed dst_done scattered a_done counted")
        with ExitStack() as ctx:
            phase_route(nc, g, ctx)
        phase_end(nc, g.ro)
        mid.close()
        g.ex = phase_events(nc, "ex", "down_done x_turned xT_act xT_dve gate_done up_done h_done h_turned hT_kept silu_done y_act y_dve "
                                "x_loaded*2 g_loaded*2 u_loaded*2 d_loaded*2 y_free*2")
        with ExitStack() as ctx:
            phase_experts(nc, g, ctx)
        phase_end(nc, g.ex)
        g.co = phase_events(nc, "co", "out_done y_loaded*4 x_loaded*4 stored*4")
        with ExitStack() as ctx:
            phase_combine(nc, g, ctx)


_INS = ["x", "c", "ctx", "c_ctx", "w_mod", "b_mod", "norm1_g", "norm2_g", "w_in", "na_qn_g", "na_kn_g", "na_rpb", "da_qn_g",
        "da_kn_g", "da_lam_q1", "da_lam_k1", "da_lam_q2", "da_lam_k2", "da_subln_g", "gdn_conv_w", "gdn_a_log",
        "gdn_dt_bias", "gdn_onorm_g", "w_branch", "w_out", "w_router", "router_bias", "moe_w_gate", "moe_w_up", "moe_w_down"]
_DEPTH = {"w_mod", "b_mod", "norm1_g", "norm2_g", "w_in", "na_qn_g", "na_kn_g", "na_rpb", "da_qn_g", "da_kn_g", "da_lam_q1",
          "da_lam_k1", "da_lam_q2", "da_lam_k2", "da_subln_g", "gdn_conv_w", "gdn_a_log", "gdn_dt_bias", "gdn_onorm_g",
          "w_branch", "w_out", "moe_w_gate", "moe_w_up", "moe_w_down"}


def shape_constants():
    f = np.float32
    i = np.arange(P)
    t = np.arange(S)
    k = {"ident": np.eye(P, dtype=f)}
    nf = DQ // 4
    freqs = (10000.0 ** (-np.arange(nf, dtype=f) / f(nf))).astype(f)
    ang = np.stack([(t // GRID_W).astype(f)[:, None] * freqs, (t % GRID_W).astype(f)[:, None] * freqs], axis=1)
    cos, sin = np.cos(ang), np.sin(ang)
    kc, ks = np.ones((T, 2, 2, nf), f), np.zeros((T, 2, 2, nf), f)
    kc[:S] = cos[:, :, None, :]
    ks[:S, :, 0], ks[:S, :, 1] = -sin, sin
    k["cos"], k["sin"] = kc.reshape(T, DQ), ks.reshape(T, DQ)
    m = np.full((NL, P, 10, GRID_W), NEG, f)
    for a in range(NL):
        kt = min(max(a - 2, 0), 3)
        for p in range(P):
            qr, qc = 2 * a + p // GRID_W, p % GRID_W
            r0 = min(max(qr - WIN_H // 2, 0), S // GRID_W - WIN_H)
            w0 = min(max(qc - WIN_W // 2, 0), GRID_W - WIN_W)
            m[a, p, r0 - 2 * kt:r0 - 2 * kt + WIN_H, w0:w0 + WIN_W] = 0
    k["namask"] = m[[0, 1, 2, 6, 7]].reshape(5, P, 640)
    k["cum"] = np.stack([(i[:, None] <= i[None, :]), (i[:, None] >= i[None, :])]).astype(f)
    lev = np.zeros((2, 7, P, P), f)
    for s in range(7):
        b = 1 << s
        same = (i[:, None] // (2 * b)) == (i[None, :] // (2 * b))
        low = (i[:, None] // b) > (i[None, :] // b)
        lev[0, s] = same & low
        lev[1, s] = (same & low).T
    k["lev"] = lev.reshape(14, P, P)
    tk = (t[:, None] * t[None, :]) % S
    k["dft"] = np.stack([np.cos(2 * np.pi * tk / S), np.sin(2 * np.pi * tk / S)]).astype(f)
    w = np.arange(HD)
    wk = (w[:, None] * w[None, :]) % HD
    bd = np.zeros((2, P, P), f)
    for b in range(2):
        q = slice(b * HD, (b + 1) * HD)
        bd[0, q, q] = np.cos(2 * np.pi * wk / HD) / 256
        bd[1, q, q] = -np.sin(2 * np.pi * wk / HD) / 256
    k["bdft"] = bd
    k["blk"] = np.arange(32, dtype=f)[None, :].repeat(P, 0)
    k["zeros"] = np.zeros((4, 24 * 128), f)
    return k


def kernel(**inputs):
    import concourse.bacc as bacc
    from concourse.bass_utils import run_bass_kernel_spmd as run

    nc = bacc.Bacc("TRN2", target_bir_lowering=False, num_devices=1)
    arrays, names = {}, {}
    for name in _INS:
        a = np.ascontiguousarray(inputs[name])
        if name in _DEPTH:
            a = a.reshape(a.shape[1:])
        arrays[name] = a
        names[name] = nc.dram_tensor(name, a.shape, F32, kind="ExternalInput").ap()
    cols = {"c_cols": np.stack([inputs["c"][0], inputs["c_ctx"]]).reshape(2, KD, P).transpose(2, 1, 0),
            "conv_cols": np.asarray(inputs["gdn_conv_w"]).reshape(CONV, 6, P).transpose(2, 1, 0),
            "norm1_cols": np.asarray(inputs["norm1_g"]).reshape(KD, P).T}
    for name, a in cols.items():
        arrays[name] = np.ascontiguousarray(a)
        names[name] = nc.dram_tensor(name, a.shape, F32, kind="ExternalInput").ap()
    for name, a in shape_constants().items():
        arrays["k_" + name] = a
        names["k_" + name] = nc.dram_tensor("k_" + name, a.shape, F32, kind="ExternalInput").ap()
    g = named(**names)
    g.out = nc.dram_tensor("out", (1, S, D), F32, kind="ExternalOutput").ap()
    trunk(nc, g)
    r = run(nc, [arrays], core_ids=[0])
    return r.results[0]["out"]
```

```python
import math
from contextlib import ExitStack

import numpy as np

import concourse.bass as bass
from concourse import mybir

F32 = mybir.dt.float32
F32R = mybir.dt.float32r
I32 = mybir.dt.int32
U32 = mybir.dt.uint32
ALU = mybir.AluOpType
ACT = mybir.ActivationFunctionType
AX = mybir.AxisListType

P = 128
D = 1024
KD = D // P
S = 1024
L = 256
T = S + L
NT = T // P
NL = S // P
GRID_W = 64
BW = 256
H = 4
HD = 64
DQ = 32
WIN_H, WIN_W = 8, 16
NEXP, NGRP, PERG, FF = 16, 4, 4, 512
NBLK = (2 * S) // P + NEXP - 1
NBLK_RUN = NBLK + NBLK % 2
EXPERT, FRESH, SETS16, SLOT, PAIRS = range(5)
EPS = 1e-6
NEG = -1e30
COL_NA, COL_DA, COL_GDN, COL_Z = 0, 3 * BW, 6 * BW, 9 * BW
COL_AB, COL_F, COL_G = 10 * BW, 10 * BW + 16, 11 * BW + 16
D_IN = COL_G + 4 * D
CONV = 5
RPB_ROW0 = 9
MCH = 512
MROW = 2 * D // MCH


class Chain:

    def __init__(self, eng, sem):
        self.eng, self.sem, self.n = eng, sem, 0

    def __call__(self, ins):
        self.n += 1
        ins.then_inc(self.sem, 1)
        self.eng.wait_ge(self.sem, self.n)


def named(**things):
    return type("Named", (), things)()


def bc(ap, n):
    return ap.unsqueeze(len(ap.shape)).broadcast_to(list(ap.shape) + [n])


def phase_modulation(nc, g, ctx):
    sb = lambda n, s, d=F32: ctx.enter_context(nc.sbuf_tensor(n, s, d))
    ROWCH, W = MROW, MCH
    wm = g.attmem[:, 0:3 * KD * W].rearrange("p (j k n) -> p j k n", j=3, k=KD)
    ccol = sb("ccol", [P, KD, 2])
    scol = g.scol
    brow = sb("brow", [2, 2 * D])
    mrow = sb("mrow", [2, 2 * D])
    n1col = sb("n1col", [P, KD])
    junk = sb("junk_sq", [P, D])
    ss = sb("ss", [P, NT])
    block = ctx.enter_context(nc.Block())
    link, e = g.link, g.mo

    @block.sync
    def _(sp):
        sp.dma_start(ccol[:, :, :], g.c_cols).then_inc(e.c_loaded, 16)
        for a, src in ((0, g.x), (1, g.ctx)):
            n = (NL, NT - NL)[a]
            for t in range(n):
                sp.dma_start(g.xall[:, a * NL + t], src[0, t * P:(t + 1) * P, :]).then_inc(e.x_loaded, 16)
        for j in range(3):
            sp.dma_start(wm[:, j], g.w_mod.rearrange("(k p) n -> p k n", p=P)[:, :, j * W:(j + 1) * W]).then_inc(e.wmod_loaded[j], 16)
        for j in range(3, ROWCH):
            sp.wait_ge(e.mod_done, j - 2)
            sp.dma_start(wm[:, j % 3], g.w_mod.rearrange("(k p) n -> p k n", p=P)[:, :, j * W:(j + 1) * W]).then_inc(e.wmod_loaded[j % 3], 16)

    @block.gpsimd
    def _(pool):
        for a in range(2):
            pool.dma_start(brow[a:a + 1, :], g.b_mod[0:2 * D].unsqueeze(0)).then_inc(e.small_loaded, 16)
        pool.dma_start(n1col[:, :], g.norm1_cols).then_inc(e.small_loaded, 16)
        pool.dma_start(g.modb[:, :], g.b_mod[2 * D:6 * D].partition_broadcast(P)).then_inc(e.bmod_loaded, 16)
        for t, src in ((g.ident, g.k_ident),):
            pool.dma_start(t[:, :], src).then_inc(e.ident_loaded, 16)

    @block.scalar
    def _(act):
        act.wait_ge(e.c_loaded, 16)
        act.activation(scol[:, :, :], ccol[:, :, :], ACT.Silu).then_inc(e.silu_done, 1)
        act.wait_ge(e.x_loaded, 16 * NT)
        for t in range(NT):
            if t:
                act.wait_ge(e.sums_done, t)
            act.activation(junk[:, :], g.xall[:, t], ACT.Square, accum_out=ss[:, t:t + 1]).then_inc(e.sums_done, 1)
        act.wait_ge(e.meansq_done, 1)
        act.activation(ss[:, :], ss[:, :], ACT.Sqrt).then_inc(e.rms_done, 1)
        act.wait_ge(e.rstd_done, 1)
        for t in range(NT):
            i = act.activation(g.xall[:, t], g.xall[:, t], ACT.Copy, scale=ss[:, t:t + 1])
        i.then_inc(e.xn_done, 1)

    @block.vector
    def _(dve):
        dve.wait_ge(e.silu_done, 1)
        dve.wait_ge(e.sums_done, NT)
        dve.tensor_scalar(ss[:, :], ss[:, :], 1.0 / D, EPS, ALU.mult, ALU.add).then_inc(e.meansq_done, 1)
        dve.wait_ge(e.rms_done, 1)
        dve.reciprocal(ss[:, :], ss[:, :]).then_inc(e.rstd_done, 1)
        dve.wait_ge(e.small_loaded, 48)
        for j in range(ROWCH):
            dve.wait_ge(e.mod_done, j + 1)
            c = slice(j * W, (j + 1) * W)
            dve.tensor_tensor(mrow[:, c], g.ps[0:2, j % 2, :], brow[:, c], ALU.add).then_inc(e.mod_kept, 1)
        dve.wait_ge(e.modT_done, 1)
        v = g.ps[:, 2, 0:32].rearrange("p (k a) -> p k a", a=2)
        link(dve.tensor_copy(g.bcol[:, :, :], v[:, 0:KD, :]))
        link(dve.tensor_scalar(g.acol[:, :, :], v[:, KD:2 * KD, :], 1.0, None, ALU.add))
        link(dve.tensor_tensor(g.acol[:, :, :], g.acol[:, :, :], bc(n1col[:, :], 2), ALU.mult))
        dve.wait_ge(e.bmod_loaded, 16)

    @block.tensor
    def _(pe):
        pe.wait_ge(e.silu_done, 1)
        for j in range(ROWCH):
            pe.wait_ge(e.wmod_loaded[j % 3], 16 * (j // 3 + 1))
            if j >= 2:
                pe.wait_ge(e.mod_kept, j - 1)
            for k in range(KD):
                i = pe.matmul(g.ps[0:2, j % 2, :], scol[:, k, :], wm[:, j % 3, k, :], start=(k == 0), stop=(k == KD - 1))
            i.then_inc(e.mod_done, 1)
        pe.wait_ge(e.mod_kept, ROWCH)
        pe.wait_ge(e.ident_loaded, 16)
        for k in range(2 * KD):
            i = pe.transpose(g.ps[:, 2, 2 * k:2 * k + 2], mrow[:, k * P:(k + 1) * P], g.ident[0:2, 0:2])
        i.then_inc(e.modT_done, 1)


def mod_chunk_source(g, j):
    return g.w_mod.rearrange("(k p) n -> p k n", p=P)[:, :, j * MCH:(j + 1) * MCH]


def mod_chunk_product(g, pe, bank, spread, wm):
    for k in range(KD):
        i = pe.matmul(g.ps[:, bank, :], spread[:, k, :], wm[:, k, :], start=(k == 0), stop=(k == KD - 1))
    return i


def mod_chunk_keep(g, dve, j, bank):
    c = slice((j - MROW) * MCH, (j - MROW + 1) * MCH)
    return dve.tensor_tensor(g.modb[:, c], g.ps[:, bank, :], g.modb[:, c], ALU.add)


def phase_qkv(nc, g, ctx, which):
    sb = lambda n, s, d=F32: ctx.enter_context(nc.sbuf_tensor(f"{n}{which}", s, d))
    first = which == 0
    nz = BW + 16 if first else 0
    hw, ng = (HD, 8) if first else (DQ, 16)
    wq = sb("wq", [P, KD, 3 * BW + nz])
    sq = sb("sq", [P, 2 * BW])
    qn = sb("qn", [P, 2, 2 * BW])
    r = sb("r", [P, 2, ng])
    QT, KT, V = ((g.naQ, g.naK, g.naV), (g.daQ, g.daK, g.daV))[which]
    if first:
        gcol = sb("gcol", [P, 2])
    else:
        gb = sb("gb", [P, 2, 8, DQ])
        cos = sb("cos", [P, NT, DQ])
        sin = sb("sin", [P, NT, DQ])
        xr = sb("xr", [P, 2 * BW])
        xs = sb("xs", [P, 2 * BW])
    qn_g, kn_g = ((g.na_qn_g, g.na_kn_g), (g.da_qn_g, g.da_kn_g))[which]
    c0 = (COL_NA, COL_DA)[which]
    link, e = g.link, g.qkv
    w_in = g.w_in.rearrange("(k p) n -> p k n", p=P)
    block = ctx.enter_context(nc.Block())

    @block.sync
    def _(sp):
        sp.dma_start(wq[:, :, 0:3 * BW], w_in[:, :, c0:c0 + 3 * BW]).then_inc(e.w_loaded, 16)
        if first:
            sp.dma_start(wq[:, :, 3 * BW:], w_in[:, :, COL_Z:COL_Z + nz]).then_inc(e.w_loaded, 16)
            for a, src in ((0, qn_g), (1, kn_g)):
                for b in range(2):
                    sp.dma_start(gcol[b * HD:(b + 1) * HD, a:a + 1], src.unsqueeze(1)).then_inc(e.w_loaded, 16)
            sp.dma_start(g.rpb_pad.rearrange("h r c -> h (r c)"), g.k_zeros[:, 0:20 * P]).then_inc(e.pad_done, 16)
            sp.wait_ge(e.pad_done, 16)
            sp.dma_start(g.rpb_pad[:, RPB_ROW0 - WIN_H + 1:RPB_ROW0 + WIN_H, 48:48 + 2 * WIN_W - 1], g.na_rpb).then_inc(e.pad_done, 16)
            sp.wait_ge(e.pad_done, 32)
            for h in range(H):
                sp.dma_start(g.rpb_rep[h], g.rpb_pad[h].unsqueeze(1).broadcast_to([20, GRID_W, P])).then_inc(e.rep_done, 16)
            sp.wait_ge(e.rep_done, 16 * H)
        else:
            for a, src in ((0, qn_g), (1, kn_g)):
                sp.dma_start(gb[:, a], bass.AP(src.tensor, src.offset, [[0, P], [0, 8], [1, DQ]])).then_inc(e.w_loaded, 16)
            sp.dma_start(cos[:, :, :], g.k_cos.rearrange("(t p) f -> p t f", p=P)).then_inc(e.w_loaded, 16)
            sp.dma_start(sin[:, :, :], g.k_sin.rearrange("(t p) f -> p t f", p=P)).then_inc(e.w_loaded, 16)

    loads = 6 if first else 5

    def c0(t):
        return 0 if t < NL else BW

    @block.scalar
    def _(act):
        for t in range(NT):
            s = t % 2
            if first:
                act.wait_ge(e.hT_turned, t + 1)
                for k in range(KD // 2, KD):
                    a = 0 if t < NL else 1
                    i = act.activation(g.hT[:, k, t * P:(t + 1) * P], g.ps[:, k // 4, (k % 4) * P:(k % 4 + 1) * P],
                                       ACT.Identity, bias=g.bcol[:, k, a:a + 1], scale=g.acol[:, k, a:a + 1])
                i.then_inc(e.hT_act, 1)
            act.wait_ge(e.qk_done, t + 1)
            if t:
                act.wait_ge(e.ss_done, t)
            act.activation(sq[:, c0(t):], g.ps[:, 2 + s, c0(t):], ACT.Square).then_inc(e.sq_done, 1)
            act.wait_ge(e.v_done, t + 1)
            act.activation(V[:, t, :], g.ps[:, 4 + s, 0:BW], ACT.Copy).then_inc(e.v_kept, 1)
            if first:
                if t < NL:
                    act.activation(g.z[:, t, :], g.ps[:, 4 + s, BW:2 * BW], ACT.Copy)
                act.activation(g.ab[:, t, :], g.ps[:, 6, 0:16], ACT.Copy).then_inc(e.v_kept, 1)
            act.wait_ge(e.ms_done, t + 1)
            act.activation(r[:, s, c0(t) // hw:], r[:, s, c0(t) // hw:], ACT.Sqrt).then_inc(e.rms_done, 1)

    @block.vector
    def _(dve):
        dve.wait_ge(e.w_loaded, 16 * loads)
        if first:
            link(dve.tensor_scalar(gcol[:, 0:1], gcol[:, 0:1], HD ** -0.5, None, ALU.mult))

        def keep_turned(t):
            dve.wait_ge(e.qT_turned, t + 1)
            for c in range(c0(t) // P, 4):
                dst = (QT if c < 2 else KT)[:, c % 2, t * P:(t + 1) * P]
                src = g.ps[:, 7, c * P:(c + 1) * P]
                if first:
                    i = dve.tensor_scalar(dst, src, gcol[:, c // 2:c // 2 + 1], None, ALU.mult)
                else:
                    i = dve.tensor_copy(dst, src)
            i.then_inc(e.qT_kept, 1)

        for t in range(NT):
            s = t % 2
            if first:
                dve.wait_ge(e.hT_turned, t + 1)
                for k in range(KD // 2):
                    a = 0 if t < NL else 1
                    i = dve.tensor_scalar(g.hT[:, k, t * P:(t + 1) * P], g.ps[:, k // 4, (k % 4) * P:(k % 4 + 1) * P],
                                          g.acol[:, k, a:a + 1], g.bcol[:, k, a:a + 1], ALU.mult, ALU.add)
                i.then_inc(e.hT_dve, 1)
            dve.wait_ge(e.sq_done, t + 1)
            rt = r[:, s, c0(t) // hw:]
            dve.tensor_reduce(rt, sq[:, c0(t):].rearrange("p (g f) -> p g f", f=hw), AX.X, ALU.add).then_inc(e.ss_done, 1)
            dve.wait_ge(e.ss_done, t + 1)
            dve.tensor_scalar(rt, rt, 1.0 / hw, EPS, ALU.mult, ALU.add).then_inc(e.ms_done, 1)
            dve.wait_ge(e.rms_done, t + 1)
            link(dve.reciprocal(rt, rt))
            if t >= 2:
                dve.wait_ge(e.qT_turned, t - 1)
            q3 = qn[:, s, c0(t):].rearrange("p (g f) -> p g f", f=hw)
            i = dve.tensor_tensor(q3, g.ps[:, 2 + s, c0(t):].rearrange("p (g f) -> p g f", f=hw), bc(rt, hw), ALU.mult)
            i.then_inc(e.qk_kept, 1)
            if not first:
                dve.wait_ge(e.qk_kept, t + 1)
                flat, rot, swapped = qn[:, s, c0(t):], xr[:, c0(t):], xs[:, c0(t):]
                nh = (2 * BW - c0(t)) // DQ
                link(dve.tensor_tensor(rot, flat, gb[:, :, :, :].rearrange("p a g f -> p (a g f)")[:, c0(t):], ALU.mult))
                x4 = rot.rearrange("p (g a f) -> p g a f", g=2 * nh, a=2)
                o4 = swapped.rearrange("p (g a f) -> p g a f", g=2 * nh, a=2)
                for b in range(2):
                    sn = sin[:, t, :].rearrange("p (x a f) -> p x a f", x=2, a=2)[:, :, b, :]
                    sn = sn.unsqueeze(1).broadcast_to([P, nh, 2, 8])
                    link(dve.tensor_tensor(o4[:, :, b, :].rearrange("p (g x) f -> p g x f", x=2),
                                           x4[:, :, 1 - b, :].rearrange("p (g x) f -> p g x f", x=2), sn, ALU.mult))
                cs = cos[:, t, :].unsqueeze(1).broadcast_to([P, nh, DQ])
                link(dve.tensor_tensor(q3, rot.rearrange("p (g f) -> p g f", f=DQ), cs, ALU.mult))
                dve.tensor_tensor(flat, flat, swapped, ALU.add).then_inc(e.rope_done, 1)
            if t:
                keep_turned(t - 1)
        keep_turned(NT - 1)

    @block.tensor
    def _(pe):

        def turn_h(t):
            if t:
                pe.wait_ge(e.hT_act, t)
                pe.wait_ge(e.hT_dve, t)
            for k in range(KD):
                i = pe.transpose(g.ps[:, k // 4, (k % 4) * P:(k % 4 + 1) * P], g.xall[:, t, k * P:(k + 1) * P], g.ident[:, :])
            i.then_inc(e.hT_turned, 1)

        def turn_q(t):
            pe.wait_ge(e.rope_done if not first else e.qk_kept, t + 1)
            if t:
                pe.wait_ge(e.qT_kept, t)
            for c in range(c0(t) // P, 4):
                i = pe.transpose(g.ps[:, 7, c * P:(c + 1) * P], qn[:, t % 2, c * P:(c + 1) * P], g.ident[:, :])
            i.then_inc(e.qT_turned, 1)

        if first:
            turn_h(0)
        pe.wait_ge(e.w_loaded, 16 * loads)
        per_v = 2 if first else 1
        for t in range(NT):
            s = t % 2
            if first:
                if t + 1 < NT:
                    turn_h(t + 1)
                pe.wait_ge(e.hT_act, t + 1)
                pe.wait_ge(e.hT_dve, t + 1)
            if t >= 2:
                pe.wait_ge(e.qk_kept, t - 1)
            for k in range(KD):
                i = pe.matmul(g.ps[:, 2 + s, c0(t):], g.hT[:, k, t * P:(t + 1) * P], wq[:, k, c0(t):2 * BW], start=(k == 0), stop=(k == KD - 1))
            i.then_inc(e.qk_done, 1)
            if t >= 1:
                turn_q(t - 1)
                pe.wait_ge(e.v_kept, per_v * t)
            nv = 2 * BW if first and t < NL else BW
            for k in range(KD):
                i = pe.matmul(g.ps[:, 4 + s, 0:nv], g.hT[:, k, t * P:(t + 1) * P], wq[:, k, 2 * BW:2 * BW + nv], start=(k == 0), stop=(k == KD - 1))
            if first:
                for k in range(KD):
                    i = pe.matmul(g.ps[:, 6, 0:16], g.hT[:, k, t * P:(t + 1) * P], wq[:, k, 4 * BW:4 * BW + 16], start=(k == 0), stop=(k == KD - 1))
            i.then_inc(e.v_done, 1)
        turn_q(NT - 1)


def turn_branch(nc, g, e, pe, src):
    for j in range(4):
        for q in range(4):
            i = pe.transpose(g.ps[:, j, q * P:(q + 1) * P], src[:, 4 * (j % 2) + q, (j // 2) * P:(j // 2 + 1) * P], g.ident[:, :])
    i.then_inc(e.br_turned, 1)


def keep_branch(nc, g, e, dve, branch):
    dve.wait_ge(e.br_turned, 1)
    for j in range(4):
        dve.tensor_copy(g.brT[:, 2 * branch + j // 2, (j % 2) * 512:(j % 2 + 1) * 512], g.ps[:, j, :])


def na_first_tile(i):
    return min(max(i - 2, 0), 3)


def phase_na(nc, g, ctx):
    sb = lambda n, s, d=F32: ctx.enter_context(nc.sbuf_tensor("na_" + n, s, d))
    NKL, NK = 640, 896
    bm = sb("bm", [P, 2, H, NKL])
    mask = sb("mask", [P, 2, NKL])
    pr = sb("pr", [P, 2, NK])
    pT = sb("pT", [P, 2, 7, P])
    ya = g.stage
    zt = g.brT[:, 6:8, :].rearrange("p a t -> p (a t)")
    mx = sb("mx", [P, 2])
    nmx = sb("nmx", [P, 2])
    l = sb("l", [P, NL * H])
    e, link = g.na, g.link
    U = [(i, h) for i in range(NL) for h in range(H)]
    block = ctx.enter_context(nc.Block())

    @block.sync
    def _(sp):
        for i in range(NL):
            if i >= 2:
                sp.wait_ge(e.bm_used, H * (i - 1))
            for a in range(2):
                for h in range(H):
                    row = 2 * na_first_tile(i) - (2 * i + a) + RPB_ROW0
                    src = bass.AP(g.rpb_rep.tensor, (h * 20 + row) * GRID_W * P + GRID_W - 1, [[P - 1, GRID_W], [GRID_W * P, 10], [1, GRID_W]])
                    sp.dma_start(bm[a * 64:(a + 1) * 64, i % 2, h, :].rearrange("p (r c) -> p r c", r=10), src).then_inc(e.bm_loaded[i % 2], 16)
            sp.dma_start(mask[:, i % 2], g.k_namask[[0, 1, 2, 2, 2, 2, 3, 4][i]]).then_inc(e.bm_loaded[i % 2], 16)
            if i == 0:
                sp.wait_ge(e.zero_made, 1)
            rows = g.xs.rearrange("(n p r) d -> n p (r d)", p=P, r=2)
            for n in range(i * NBLK_RUN // 2 // NL, (i + 1) * NBLK_RUN // 2 // NL):
                sp.dma_start(rows[n], zt[:, :]).then_inc(e.zeroed, 16)
        sp.wait_ge(e.zeroed, 16 * (NBLK_RUN // 2))

    @block.gpsimd
    def _(pool):
        pool.memset(zt[:, :], 0.0).then_inc(e.zero_made, 1)
        for i in range(NL):
            pool.wait_ge(e.bm_loaded[i % 2], 16 * 9 * (i // 2 + 1))
            for h in range(H):
                pool.tensor_tensor(bm[:, i % 2, h], bm[:, i % 2, h], mask[:, i % 2], ALU.add).then_inc(e.bm_ready, 1)

    @block.tensor
    def _(pe):
        def scores(u):
            i, h = U[u]
            if u >= 2:
                pe.wait_ge(e.exp_done, u - 1)
            b, s = 64 * (h % 2), 2 * (u % 2)
            k0 = na_first_tile(i) * P
            q = g.naQ[b:b + 64, h // 2, i * P:(i + 1) * P]
            for off, src, n in ((0, k0, 512), (512, k0 + 512, 128), (640, S, L)):
                mm = pe.matmul(g.ps[:, s + off // 512, off % 512:off % 512 + n], q, g.naK[b:b + 64, h // 2, src:src + n], start=True, stop=True)
            mm.then_inc(e.s_done, 1)

        def turn(u):
            pe.wait_ge(e.exp_done, u + 1)
            if u:
                pe.wait_ge(e.pt_act, u)
                pe.wait_ge(e.pt_dve, u)
            for k in range(7):
                mm = pe.transpose(g.ps[:, 4 + k // 4, (k % 4) * P:(k % 4 + 1) * P], pr[:, u % 2, k * P:(k + 1) * P], g.ident[:, :])
            mm.then_inc(e.pt_turned, 1)

        def values(u):
            i, h = U[u]
            pe.wait_ge(e.pt_act, u + 1)
            pe.wait_ge(e.pt_dve, u + 1)
            if u >= 2:
                pe.wait_ge(e.o_kept, u - 1)
            for k in range(7):
                kt = na_first_tile(i) + k if k < 5 else NL + k - 5
                mm = pe.matmul(g.ps[:, 6 + u % 2, 0:HD], pT[:, u % 2, k, :], g.naV[:, kt, h * HD:(h + 1) * HD], start=(k == 0), stop=(k == 6))
            mm.then_inc(e.o_done, 1)

        for u in range(len(U) + 2):
            if u < len(U):
                scores(u)
            if 1 <= u <= len(U):
                turn(u - 1)
            if u >= 2:
                values(u - 2)
        pe.wait_ge(e.o_kept, len(U))
        turn_branch(nc, g, e, pe, ya)

    @block.scalar
    def _(act):
        for u in range(len(U) + 1):
            if u < len(U):
                act.wait_ge(e.max_done, u + 1)
                if u >= 2:
                    act.wait_ge(e.pt_turned, u - 1)
                s = g.ps[:, 2 * (u % 2):2 * (u % 2) + 2, :].rearrange("p a b -> p (a b)")
                act.activation(pr[:, u % 2, :], s[:, 0:NK], ACT.Exp, bias=nmx[:, u % 2:u % 2 + 1], accum_out=l[:, u:u + 1]).then_inc(e.exp_done, 1)
            if u:
                act.wait_ge(e.pt_turned, u)
                if u >= 3:
                    act.wait_ge(e.o_done, u - 2)
                act.activation(pT[:, (u - 1) % 2, 0:4, :], g.ps[:, 4, :].rearrange("p (a b) -> p a b", a=4), ACT.Copy).then_inc(e.pt_act, 1)

    @block.vector
    def _(dve):
        for u in range(len(U) + 2):
            if u < len(U):
                i, h = U[u]
                s = g.ps[:, 2 * (u % 2):2 * (u % 2) + 2, :].rearrange("p a b -> p (a b)")
                dve.wait_ge(e.s_done, u + 1)
                dve.wait_ge(e.bm_ready, u + 1)
                dve.tensor_tensor(s[:, 0:NKL], s[:, 0:NKL], bm[:, i % 2, h], ALU.add).then_inc(e.bm_used, 1)
                dve.wait_ge(e.bm_used, u + 1)
                link(dve.tensor_reduce(mx[:, u % 2:u % 2 + 1], s[:, 0:NK], AX.X, ALU.max))
                if u >= 2:
                    dve.wait_ge(e.exp_done, u - 1)
                dve.tensor_scalar(nmx[:, u % 2:u % 2 + 1], mx[:, u % 2:u % 2 + 1], -1.0, None, ALU.mult).then_inc(e.max_done, 1)
            if 1 <= u <= len(U):
                dve.wait_ge(e.pt_turned, u)
                if u >= 3:
                    dve.wait_ge(e.o_done, u - 2)
                dve.tensor_copy(pT[:, (u - 1) % 2, 4:7, :], g.ps[:, 5, 0:384].rearrange("p (a b) -> p a b", a=3)).then_inc(e.pt_dve, 1)
                link(dve.reciprocal(l[:, u - 1:u], l[:, u - 1:u]))
            if u >= 2:
                i, h = U[u - 2]
                dve.wait_ge(e.o_done, u - 1)
                dve.tensor_scalar(ya[:, i, h * HD:(h + 1) * HD], g.ps[:, 6 + u % 2, 0:HD], l[:, u - 2:u - 1], None, ALU.mult).then_inc(e.o_kept, 1)
        keep_branch(nc, g, e, dve, 0)


def phase_da(nc, g, ctx):
    sb = lambda n, s, d=F32: ctx.enter_context(nc.sbuf_tensor("da_" + n, s, d))
    LAM0 = 0.8 - 0.6 * math.exp(0.0)
    p0 = g.brT[:, 4:8, :].rearrange("p a t -> p (a t)")[:, 0:2 * T].rearrange("p (s t) -> p s t", s=2)
    p1 = sb("p1", [P, 2, T])
    pT = g.naV[:, :, :].rearrange("p t c -> p (t c)").rearrange("p (s k i) -> p s k i", s=2, i=P)
    NSET = 3
    qs = [sb(f"qs{j}", [P, S], F32R) for j in range(NSET)]
    ks = [sb(f"ks{j}", [P, T], F32R) for j in range(NSET)]
    N_ = 2 * (S + T)
    high, low = g.attmem[:, 0:N_], g.attmem[:, N_:2 * N_]
    PARTS = [slice(at, at + n) for a in range(2) for at, n in ((a * S, S), (2 * S + a * T, T))]
    yd = g.stage
    sq = p0.rearrange("p s t -> p (s t)")[:, 0:NL * BW].rearrange("p (t c) -> p t c", t=NL)
    gb = sb("gb", [P, HD])
    rr = sb("rr", [P, NL * H])
    lv = sb("lv", [P, 4, DQ])
    lam = sb("lam", [P, 4])
    mx = sb("mx", [P, 2, 2])
    nmx = sb("nmx", [P, 2, 2])
    l = sb("l", [P, 2, 2])
    rl = sb("rl", [P, 4, 2])
    rho = sb("rho", [P, 2])
    e, link = g.da, g.link
    U = [(i, h) for h in range(H) for i in range(NL)]
    NU = len(U)
    block = ctx.enter_context(nc.Block())

    def score_banks(m):
        return g.ps[:, 3 * m:3 * m + 3, :].rearrange("p a b -> p (a b)")[:, 0:T]

    @block.sync
    def _(sp):
        for a, v in enumerate((g.da_lam_q1, g.da_lam_q2, g.da_lam_k1, g.da_lam_k2)):
            sp.dma_start(lv[:, a, :], v.partition_broadcast(P)).then_inc(e.small_loaded, 16)
        sp.dma_start(gb[:, :], g.da_subln_g.partition_broadcast(P)).then_inc(e.small_loaded, 16)
        for c in range(2 * H):
            if c % 4 == 0:
                sp.wait_ge(e.split_done, c // 2 + 2)
            if c >= NSET:
                h, m = (c - NSET) // 2, (c - NSET) % 2
                sp.wait_ge(e.s_done[m], NL * (h + 1))
            rows = slice(DQ * (c % 4), DQ * (c % 4) + DQ)
            for r in range(4):
                for dst, part, off, n in ((qs, (high, low)[r // 2], 0, S), (ks, (high, low)[r % 2], 2 * S, T)):
                    src = part[rows, off + (c // 4) * n:off + (c // 4) * n + n]
                    sp.dma_start(dst[c % NSET][DQ * r:DQ * r + DQ, :].bitcast(F32), src).then_inc(e.set_loaded[c % NSET], 16)

    @block.tensor
    def _(pe):
        def scores(u, m):
            i, h = U[u]
            c = 2 * h + m
            if i == 0:
                pe.wait_ge(e.set_loaded[c % NSET], 128 * (c // NSET + 1))
            if u:
                pe.wait_ge(e.exp_done[m], u)
            for k in range(3):
                n = min(512, T - 512 * k)
                mm = pe.matmul(g.ps[:, 3 * m + k, 0:n], qs[c % NSET][:, i * P:(i + 1) * P], ks[c % NSET][:, 512 * k:512 * k + n], start=True, stop=True)
            mm.then_inc(e.s_done[m], 1)

        def turn(u, j):
            if j == 0:
                pe.wait_ge(e.a_done, u + 1)
            if 3 * u + j:
                pe.wait_ge(e.pt_kept, 3 * u + j)
            for k in range(4 * j, min(4 * j + 4, NT)):
                mm = pe.transpose(g.ps[:, 6, (k % 4) * P:(k % 4 + 1) * P], p1[:, u % 2, k * P:(k + 1) * P], g.ident[:, :])
            mm.then_inc(e.pt_turned, 1)

        def values(u, j):
            i, h = U[u]
            pe.wait_ge(e.pt_kept, 3 * u + j + 1)
            if j == 0 and u:
                pe.wait_ge(e.o_kept, u)
            for k in range(4 * j, min(4 * j + 4, NT)):
                mm = pe.matmul(g.ps[:, 7, 0:HD], pT[:, u % 2, k, :], g.daV[:, k, h * HD:(h + 1) * HD], start=(k == 0), stop=(k == NT - 1))
            if j == 2:
                mm.then_inc(e.o_done, 1)

        for u in range(NU + 1):
            if u < NU:
                scores(u, 0)
            if u:
                turn(u - 1, 0)
            if u < NU:
                scores(u, 1)
            if u:
                turn(u - 1, 1)
                values(u - 1, 0)
                turn(u - 1, 2)
                values(u - 1, 1)
                values(u - 1, 2)
        pe.wait_ge(e.y_done, 1)
        turn_branch(nc, g, e, pe, yd)

    @block.scalar
    def _(act):
        for part in PARTS:
            act.activation(high[:, part].bitcast(F32R), low[:, part], ACT.Copy).then_inc(e.high_done, 1)
        act.wait_ge(e.dots_done, 1)
        act.activation(lam[:, 0:2], lam[:, 0:2], ACT.Exp).then_inc(e.lam_exp, 1)
        for u in range(NU + 1):
            if u < NU:
                for m, p in ((0, p0), (1, p1)):
                    act.wait_ge(e.max_done[m], u + 1)
                    if u >= 2:
                        act.wait_ge(e.pt_turned, 3 * (u - 1))
                    act.activation(p[:, u % 2, :], score_banks(m), ACT.Exp, scale=DQ ** -0.5, bias=nmx[:, u % 2, m:m + 1],
                                   accum_out=l[:, u % 2, m:m + 1]).then_inc(e.exp_done[m], 1)
            if u:
                for j in range(3):
                    k = min(4, NT - 4 * j)
                    act.wait_ge(e.pt_turned, 3 * (u - 1) + j + 1)
                    if u >= 3:
                        act.wait_ge(e.o_done, u - 2)
                    act.activation(pT[:, (u - 1) % 2, 4 * j:4 * j + k, :], g.ps[:, 6, 0:k * P].rearrange("p (a b) -> p a b", a=k), ACT.Copy).then_inc(e.pt_kept, 1)
        act.wait_ge(e.ms_done, 1)
        act.activation(rr[:, :], rr[:, :], ACT.Sqrt).then_inc(e.rms_done, 1)

    @block.vector
    def _(dve):
        for n, part in enumerate(PARTS):
            dve.wait_ge(e.high_done, n + 1)
            dve.tensor_tensor(low[:, part].bitcast(F32R), low[:, part], high[:, part], ALU.subtract).then_inc(e.split_done, 1)
        dve.wait_ge(e.small_loaded, 80)
        link(dve.tensor_tensor(lv[:, 0:2, :], lv[:, 0:2, :], lv[:, 2:4, :], ALU.mult))
        dve.tensor_reduce(lam[:, 0:2], lv[:, 0:2, :], AX.X, ALU.add).then_inc(e.dots_done, 1)
        dve.wait_ge(e.lam_exp, 1)
        link(dve.tensor_tensor(lam[:, 2:3], lam[:, 1:2], lam[:, 0:1], ALU.subtract))
        link(dve.tensor_scalar(lam[:, 2:3], lam[:, 2:3], LAM0, None, ALU.subtract))

        def largest(u, m):
            dve.wait_ge(e.s_done[m], u + 1)
            link(dve.tensor_reduce(mx[:, u % 2, m:m + 1], score_banks(m), AX.X, ALU.max))
            dve.tensor_scalar(nmx[:, u % 2, m:m + 1], mx[:, u % 2, m:m + 1], -DQ ** -0.5, None, ALU.mult).then_inc(e.max_done[m], 1)

        for u in range(NU + 1):
            if u < NU:
                largest(u, 0)
            if u:
                w = (u - 1) % 2
                for m in range(2):
                    dve.wait_ge(e.exp_done[m], u)
                link(dve.reciprocal(rl[:, (u - 1) % 4, :], l[:, w, :]))
                link(dve.scalar_tensor_tensor(rho[:, w:w + 1], l[:, w, 0:1], lam[:, 2:3], rl[:, (u - 1) % 4, 1:2], ALU.mult, ALU.mult))
                dve.scalar_tensor_tensor(p1[:, w, :], p1[:, w, :], rho[:, w:w + 1], p0[:, w, :], ALU.mult, ALU.add).then_inc(e.a_done, 1)
            if u < NU:
                largest(u, 1)
            if u >= 2:
                i, h = U[u - 2]
                dve.wait_ge(e.o_done, u - 1)
                dve.tensor_scalar(yd[:, i, h * HD:(h + 1) * HD], g.ps[:, 7, 0:HD], rl[:, (u - 2) % 4, 0:1], None, ALU.mult).then_inc(e.o_kept, 1)
        dve.wait_ge(e.o_done, NU)
        link(dve.tensor_scalar(yd[:, NL - 1, 3 * HD:], g.ps[:, 7, 0:HD], rl[:, (NU - 1) % 4, 0:1], None, ALU.mult))
        y3 = yd[:, :, :].rearrange("p t (h f) -> p (t h) f", f=HD)
        link(dve.tensor_tensor(sq[:, :, :], yd[:, :, :], yd[:, :, :], ALU.mult))
        link(dve.tensor_reduce(rr[:, :], sq[:, :, :].rearrange("p t (h f) -> p (t h) f", f=HD), AX.X, ALU.add))
        dve.tensor_scalar(rr[:, :], rr[:, :], 1.0 / HD, EPS, ALU.mult, ALU.add).then_inc(e.ms_done, 1)
        dve.wait_ge(e.rms_done, 1)
        link(dve.reciprocal(rr[:, :], rr[:, :]))
        link(dve.tensor_scalar(gb[:, :], gb[:, :], 1.0 - LAM0, None, ALU.mult))
        link(dve.tensor_tensor(y3, y3, bc(rr[:, :], HD), ALU.mult))
        dve.tensor_tensor(y3, y3, gb[:, :].unsqueeze(1).broadcast_to([P, NL * H, HD]), ALU.mult).then_inc(e.y_done, 1)
        keep_branch(nc, g, e, dve, 1)


def phase_gdn_inputs(nc, g, ctx):
    sb = lambda n, s, d=F32: ctx.enter_context(nc.sbuf_tensor("gi_" + n, s, d))
    HALF = CONV // 2
    SEG = S + 2 * HALF
    W = S + L + 2 * HALF
    NS = 6
    wg = sb("wg", [P, 2, KD, P])
    cp = sb("cp", [P, 2, W + 2 * HALF])
    acc = sb("acc", [P, W])
    cw = sb("cw", [P, NS, CONV])
    qkvc = sb("qkvc", [P, NS, T])
    sq = sb("sq", [P, 2 * BW])
    r = sb("r", [P, 2 * H])
    qn = sb("qn", [P, 2, BW])
    e, link = g.gi, g.link
    w_in = g.w_in.rearrange("(k p) n -> p k n", p=P)
    block = ctx.enter_context(nc.Block())

    @block.sync
    def _(sp):
        sp.dma_start(cw[:, :, :], g.conv_cols).then_inc(e.cw_loaded, 16)
        for s in range(NS):
            if s >= 2:
                sp.wait_ge(e.proj_done, s - 1)
            c = COL_GDN + s * P
            sp.dma_start(wg[:, s % 2], w_in[:, :, c:c + P]).then_inc(e.w_loaded[s % 2], 16)

    @block.tensor
    def _(pe):
        for s in range(NS):
            pe.wait_ge(e.w_loaded[s % 2], 16 * (s // 2 + 1))
            if s >= 2:
                pe.wait_ge(e.padded, 3 * (s - 1))
            for j in range(3):
                n = min(512, T - 512 * j)
                for k in range(KD):
                    i = pe.matmul(g.ps[:, 3 * (s % 2) + j, 0:n], wg[:, s % 2, k, :], g.hT[:, k, 512 * j:512 * j + n], start=(k == 0), stop=(k == KD - 1))
            i.then_inc(e.proj_done, 1)

        def turn_back(t):
            pe.wait_ge(e.qk_normed, t + 1)
            if t >= 2:
                pe.wait_ge(e.qkT_kept, t - 1)
            for c in range(2):
                pe.transpose(g.ps[:, t % 2, c * P:(c + 1) * P], qn[:, t % 2, c * P:(c + 1) * P], g.ident[:, :])
            for c in range(2):
                i = pe.transpose(g.ps[:, t % 2, (2 + c) * P:(3 + c) * P], g.gk[:, t, c * P:(c + 1) * P], g.ident[:, :])
            i.then_inc(e.qkT_turned, 1)

        pe.wait_ge(e.silu_done, 2 * NS)
        for t in range(NT):
            if t:
                pe.wait_ge(e.qk_normed, t)
                pe.wait_ge(e.v_kept, t)
            for c in range(NS):
                i = pe.transpose(g.ps[:, 6 + c // 4, (c % 4) * P:(c % 4 + 1) * P], qkvc[:, c, t * P:(t + 1) * P], g.ident[:, :])
            i.then_inc(e.turned, 1)
            if t:
                turn_back(t - 1)
        turn_back(NT - 1)

    @block.scalar
    def _(act):
        act.wait_ge(e.pads_zero, 1)
        for s in range(NS):
            act.wait_ge(e.proj_done, s + 1)
            if s >= 2:
                act.wait_ge(e.conv_done, s - 1)
            for j in range(3):
                n = min(512, T - 512 * j)
                o = HALF + 512 * j if j < 2 else SEG + HALF
                act.activation(cp[:, s % 2, o:o + n], g.ps[:, 3 * (s % 2) + j, 0:n], ACT.Copy).then_inc(e.padded, 1)
            act.wait_ge(e.conv_done, s + 1)
            act.activation(qkvc[:, s, 0:S], acc[:, 0:S], ACT.Silu).then_inc(e.silu_done, 1)
            act.activation(qkvc[:, s, S:T], acc[:, SEG:SEG + L], ACT.Silu).then_inc(e.silu_done, 1)
        for t in range(NT):
            act.wait_ge(e.turned, t + 1)
            if t:
                act.wait_ge(e.ss_done, t)
            act.activation(sq[:, :], g.ps[:, 6, :], ACT.Square).then_inc(e.sq_done, 1)
            act.activation(g.gv[:, t, :], g.ps[:, 7, 0:BW], ACT.Copy).then_inc(e.v_kept, 1)
            act.wait_ge(e.eps_added, t + 1)
            act.activation(r[:, :], r[:, :], ACT.Sqrt).then_inc(e.rms_done, 1)

    @block.gpsimd
    def _(pool):
        pool.memset(g.gkT[:, :, :, :], 0.0).then_inc(e.gkT_zero, 1)

    @block.vector
    def _(dve):
        dve.memset(cp[:, :, :], 0.0).then_inc(e.pads_zero, 1)
        dve.wait_ge(e.gkT_zero, 1)
        dve.wait_ge(e.cw_loaded, 16)
        for s in range(NS):
            dve.wait_ge(e.padded, 3 * (s + 1))
            if s:
                dve.wait_ge(e.silu_done, 2 * s)
            link(dve.tensor_scalar(acc[:, :], cp[:, s % 2, 0:W], cw[:, s, 0:1], None, ALU.mult))
            for i in range(1, CONV):
                ins = dve.scalar_tensor_tensor(acc[:, :], cp[:, s % 2, i:i + W], cw[:, s, i:i + 1], acc[:, :], ALU.mult, ALU.add)
                if i < CONV - 1:
                    link(ins)
            ins.then_inc(e.conv_done, 1)

        def keep_back(t):
            dve.wait_ge(e.qkT_turned, t + 1)
            for c in range(2):
                if t < NL:
                    dve.tensor_copy(g.gqT[:, c, t * P:(t + 1) * P], g.ps[:, t % 2, c * P:(c + 1) * P])
                for b in range(2):
                    q = slice(64 * b, 64 * b + 64)
                    i = dve.tensor_copy(g.gkT[q, b, c, t * P:(t + 1) * P], g.ps[q, t % 2, (2 + c) * P:(3 + c) * P])
            i.then_inc(e.qkT_kept, 1)

        for t in range(NT):
            dve.wait_ge(e.sq_done, t + 1)
            dve.tensor_reduce(r[:, :], sq[:, :].rearrange("p (g f) -> p g f", f=HD), AX.X, ALU.add).then_inc(e.ss_done, 1)
            dve.wait_ge(e.ss_done, t + 1)
            dve.tensor_scalar(r[:, :], r[:, :], EPS, None, ALU.add).then_inc(e.eps_added, 1)
            dve.wait_ge(e.rms_done, t + 1)
            link(dve.reciprocal(r[:, :], r[:, :]))
            link(dve.tensor_scalar(r[:, 0:H], r[:, 0:H], HD ** -0.5, None, ALU.mult))
            if t >= 2:
                dve.wait_ge(e.qkT_turned, t - 1)
            src = g.ps[:, 6, :].rearrange("p (g f) -> p g f", f=HD)
            dve.tensor_tensor(qn[:, t % 2, :].rearrange("p (g f) -> p g f", f=HD), src[:, 0:H], bc(r[:, 0:H], HD), ALU.mult)
            dve.tensor_tensor(g.gk[:, t, :].rearrange("p (g f) -> p g f", f=HD), src[:, H:], bc(r[:, H:], HD), ALU.mult).then_inc(e.qk_normed, 1)
            if t:
                keep_back(t - 1)
        keep_back(NT - 1)


def phase_gdn(nc, g, ctx):
    sb = lambda n, s, d=F32: ctx.enter_context(nc.sbuf_tensor("gd_" + n, s, d))
    lev = sb("lev", [P, 14, P])
    cum = sb("cum", [P, 2, P])
    two = lambda n, s: [sb(f"{n}{d}", s) for d in range(2)]
    E, ET, AT, Dm, DT, PS_ = (two(n, [P, H, P]) for n in ("E", "ET", "AT", "D", "DT", "P"))
    ones = E[0][:, 0, :]
    LT = two("LT", [P, 2, H, P])
    gbig = two("gbig", [P, H, P])
    vb, kbg, kd, vn = (two(n, [P, H, HD]) for n in ("vb", "kbg", "kd", "vn"))
    nwT = two("nwT", [P, 2, P])
    St = two("S", [P, H, HD])
    ot = two("ot", [P, BW])
    al = sb("al", [P, 8])
    dtb = sb("dtb", [P, 8])
    gx = sb("gx", [P, NT, 8])
    g8 = sb("g8", [P, NT, 8])
    be = sb("be", [P, NT, 8])
    G = sb("G", [P, NT, 8])
    eG = sb("eG", [P, NT, 8])
    eL = sb("eL", [P, NT, 8])
    eK = sb("eK", [P, NT, 8])
    beG = sb("beG", [P, NT, 8])
    onb = sb("onb", [P, HD])
    rr = sb("rr", [P, NL * H])
    sq = gbig[0]
    e, link, plink, alink = g.gd, g.link, g.plink, g.alink
    og = g.stage
    order = [[8, 9] + list(range(NL)), [9, 8] + list(range(NL))[::-1]]
    NSTEP, NLEV = NT, 7
    block = ctx.enter_context(nc.Block())

    def heads(ap, t, d):
        return ap[:, t, 4 * d:4 * d + 4]

    @block.sync
    def _(sp):
        sp.dma_start(lev[:, :, :], g.k_lev.rearrange("s p i -> p s i")).then_inc(e.loaded, 16)
        sp.dma_start(cum[:, :, :], g.k_cum.rearrange("s p i -> p s i")).then_inc(e.loaded, 16)
        sp.dma_start(al[:, :], g.gdn_a_log.rearrange("a h -> (a h)").partition_broadcast(P)).then_inc(e.loaded, 16)
        sp.dma_start(dtb[:, :], g.gdn_dt_bias.rearrange("a h -> (a h)").partition_broadcast(P)).then_inc(e.loaded, 16)
        sp.dma_start(onb[:, :], g.gdn_onorm_g.partition_broadcast(P)).then_inc(e.loaded, 16)

    @block.tensor
    def _(pe):
        pe.wait_ge(e.g_ready, 1)
        for d in range(2):
            pe.matmul(g.ps[:, 0, 40 * d:40 * d + 40].rearrange("p (t h) -> p t h", h=4), cum[:, d, :], g8[:, :, 4 * d:4 * d + 4], start=True, stop=True)
        pe.matmul(g.ps[:, 0, 80:160], ones, g8[:, :, :].rearrange("p t h -> p (t h)"), start=True, stop=True).then_inc(e.cum_done, 1)
        pe.wait_ge(e.decays_ready, 1)
        for n in range(NSTEP):
            for d in range(2):
                t = order[d][n]
                B = 3 * d
                pe.wait_ge(e.gbig_ready, 2 * n + d + 1)
                if n:
                    pe.wait_ge(e.s_kept[d], n)
                    if n > 2:
                        pe.wait_ge(e.o_kept[d], n - 2)
                for h in range(H):
                    pe.matmul(g.ps[:, B, h * P:(h + 1) * P], gbig[d][:, h, :], cum[:, d, :], start=True, stop=True)
                for h in range(H):
                    k = g.gkT[:, h % 2, h // 2, t * P:(t + 1) * P]
                    i = pe.matmul(g.ps[:, B + 1, h * P:(h + 1) * P], k, k, start=True, stop=True)
                if t < NL:
                    for h in range(H):
                        i = pe.matmul(g.ps[:, B + 2, h * P:(h + 1) * P], g.gkT[:, h % 2, h // 2, t * P:(t + 1) * P],
                                      g.gqT[:, h // 2, t * P:(t + 1) * P], start=True, stop=True)
                i.then_inc(e.prods[d], 1)
            for d in range(2):
                pe.wait_ge(e.a_ready[d], n + 1)
                for h in range(H):
                    i = pe.transpose(g.ps[:, 3 * d, h * P:(h + 1) * P], E[d][:, h, :], g.ident[:, :])
                i.then_inc(e.a_turned[d], 1)
            for s in range(1, NLEV):
                m = n * (NLEV - 1) + s
                for d in range(2):
                    pe.wait_ge(e.lt_ready[d], m)
                    pe.wait_ge(e.d_ready[d], m)
                    for h in range(H):
                        i = pe.matmul(g.ps[:, 3 * d, h * P:(h + 1) * P], LT[d][:, s % 2, h, :], Dm[d][:, h, :], start=True, stop=True)
                    i.then_inc(e.p_done[d], 1)
                for d in range(2):
                    pe.wait_ge(e.p_kept[d], m)
                    pe.wait_ge(e.dt_ready[d], m)
                    if s < NLEV - 1:
                        for h in range(H):
                            i = pe.matmul(g.ps[:, 3 * d + 1, h * P:(h + 1) * P], DT[d][:, h, :], PS_[d][:, h, :], start=True, stop=True)
                    for h in range(H):
                        i = pe.matmul(g.ps[:, 3 * d + 2, h * P:(h + 1) * P], PS_[d][:, h, :], DT[d][:, h, :], start=True, stop=True)
                    i.then_inc(e.e_done[d], 1)
            for d in range(2):
                pe.wait_ge(e.dt_last[d], n + 1)
                for h in range(H):
                    b = 64 * (h % 2)
                    i = pe.matmul(g.ps[b:b + 64, 3 * d + 1, (h // 2) * P:(h // 2 + 1) * P], kbg[d][:, h, :], DT[d][:, h, :], start=True, stop=True)
                i.then_inc(e.w_done[d], 1)
            for d in range(2):
                t = order[d][n]
                pe.wait_ge(e.w_kept[d], n + 1)
                for h in range(H):
                    o = g.ps[:, 6 + d, h * HD:(h + 1) * HD]
                    pe.matmul(o, DT[d][:, h, :], vb[d][:, h, :], start=True, stop=False)
                    i = pe.matmul(o, nwT[d][:, h // 2, :], St[d][:, h, :], start=False, stop=True)
                i.then_inc(e.v_done[d], 1)
            for d in range(2):
                t = order[d][n]
                if t < NL:
                    for h in range(H):
                        pe.matmul(g.ps[:, 3 * d, h * HD:(h + 1) * HD], g.gqT[:, h // 2, t * P:(t + 1) * P], St[d][:, h, :], start=True, stop=True)
                pe.wait_ge(e.v_kept[d], n + 1)
                if t < NL:
                    for h in range(H):
                        i = pe.matmul(g.ps[:, 3 * d, BW + h * HD:BW + (h + 1) * HD], ET[d][:, h, :], vn[d][:, h, :], start=True, stop=True)
                    i.then_inc(e.o_done[d], 1)
                for h in range(H):
                    b = 64 * (h % 2)
                    i = pe.matmul(g.ps[b:b + 64, 3 * d + 1, (h // 2) * HD:(h // 2 + 1) * HD], kd[d][:, h, :], vn[d][:, h, :], start=True, stop=True)
                i.then_inc(e.s_done[d], 1)
        pe.wait_ge(e.y_done, 1)
        turn_branch(nc, g, e, pe, og)

    @block.scalar
    def _(act):
        act.wait_ge(e.loaded, 80)
        act.wait_ge(e.sp_in, 1)
        alink(act.activation(eG[:, :, :], eG[:, :, :], ACT.Exp))
        alink(act.activation(al[:, :], al[:, :], ACT.Exp))
        act.activation(eG[:, :, :], eG[:, :, :], ACT.Ln, bias=1.0).then_inc(e.ln_done, 1)
        act.activation(be[:, :, :], g.ab[:, :, 8:16], ACT.Sigmoid).then_inc(e.beta_done, 1)
        act.activation(g.z[:, :, :], g.z[:, :, :], ACT.Silu).then_inc(e.z_done, 1)
        act.wait_ge(e.G_kept, 1)
        act.activation(eG[:, :, :], G[:, :, :], ACT.Exp).then_inc(e.exps_done, 1)
        act.activation(eL[:, :, :], eL[:, :, :], ACT.Exp).then_inc(e.exps_done, 1)
        act.activation(eK[:, :, :], eK[:, :, :], ACT.Exp).then_inc(e.exps_done, 1)
        for n in range(NSTEP):
            for d in range(2):
                act.wait_ge(e.x_ready[d], n + 1)
                act.activation(E[d][:, :, :], E[d][:, :, :], ACT.Exp).then_inc(e.exp_done[d], 1)
                act.activation(ET[d][:, :, :], ET[d][:, :, :], ACT.Exp).then_inc(e.exp_done[d], 1)
            for d in range(2):
                act.wait_ge(e.a_turned[d], n + 1)
                act.activation(AT[d][:, :, :].rearrange("p h i -> p (h i)"), g.ps[:, 3 * d, :], ACT.Copy).then_inc(e.at_kept[d], 1)
            for s in range(1, NLEV):
                m = n * (NLEV - 1) + s
                for d in range(2):
                    act.wait_ge(e.p_done[d], m)
                    act.activation(PS_[d][:, :, :].rearrange("p h i -> p (h i)"), g.ps[:, 3 * d, :], ACT.Copy).then_inc(e.p_kept[d], 1)
            for d in range(2):
                act.wait_ge(e.w_done[d], n + 1)
                act.activation(nwT[d][:, :, :].rearrange("p h i -> p (h i)"), g.ps[:, 3 * d + 1, 0:2 * P], ACT.Copy, scale=-1.0).then_inc(e.w_kept[d], 1)
        act.wait_ge(e.ms_done, 1)
        act.activation(rr[:, :], rr[:, :], ACT.Sqrt).then_inc(e.rms_done, 1)

    @block.gpsimd
    def _(pool):
        pool.wait_ge(e.decays_ready, 1)
        for n in range(NSTEP):
            for d in range(2):
                t = order[d][n]
                if n:
                    pool.wait_ge(e.prods[d], n)
                pool.tensor_copy(gbig[d][:, :, :], bc(heads(g8, t, d), P)).then_inc(e.gbig_ready, 1)
            for d in range(2):
                t = order[d][n]
                if n:
                    pool.wait_ge(e.s_done[d], n)
                k3 = g.gk[:, t, :].rearrange("p (h f) -> p h f", f=HD)
                pool.tensor_tensor(vb[d][:, :, :], g.gv[:, t, :].rearrange("p (h f) -> p h f", f=HD), bc(heads(be, t, d), HD), ALU.mult).then_inc(e.ops_ready[d], 1)
                pool.tensor_tensor(kbg[d][:, :, :], k3, bc(heads(beG, t, d), HD), ALU.mult).then_inc(e.ops_ready[d], 1)
                pool.tensor_tensor(kd[d][:, :, :], k3, bc(heads(eK, t, d), HD), ALU.mult).then_inc(e.ops_ready[d], 1)
            for d in range(2):
                pool.wait_ge(e.at_kept[d], n + 1)
                msk = lambda s: lev[:, 7 * (1 - d) + s, :].unsqueeze(1).broadcast_to([P, H, P])
                plink(pool.tensor_tensor(DT[d][:, :, :], AT[d][:, :, :], msk(0), ALU.mult))
                pool.tensor_tensor(DT[d][:, :, :], g.ident[:, :].unsqueeze(1).broadcast_to([P, H, P]), DT[d][:, :, :], ALU.subtract).then_inc(e.dt_first[d], 1)
            for s in range(1, NLEV):
                m = n * (NLEV - 1) + s
                for d in range(2):
                    if m > 2:
                        pool.wait_ge(e.p_done[d], m - 2)
                    pool.tensor_tensor(LT[d][:, s % 2, :, :], AT[d][:, :, :], lev[:, 7 * (1 - d) + s, :].unsqueeze(1).broadcast_to([P, H, P]), ALU.mult).then_inc(e.lt_ready[d], 1)

    @block.vector
    def _(dve):
        dve.memset(ones, 1.0)
        for d in range(2):
            link(dve.memset(St[d][:, :, :], 0.0))
        dve.wait_ge(e.loaded, 80)
        link(dve.tensor_tensor(gx[:, :, :], g.ab[:, :, 0:8], dtb[:, :].unsqueeze(1).broadcast_to([P, NT, 8]), ALU.add))
        link(dve.tensor_scalar(eG[:, :, :], gx[:, :, :], -1.0, None, ALU.mult))
        dve.tensor_tensor(eG[:, :, :], eG[:, :, :], gx[:, :, :], ALU.min).then_inc(e.sp_in, 1)
        dve.wait_ge(e.ln_done, 1)
        link(dve.scalar_tensor_tensor(gx[:, :, :], gx[:, :, :], 0.0, eG[:, :, :], ALU.max, ALU.add))
        link(dve.tensor_scalar(gx[:, :, :], gx[:, :, :], -1.0, None, ALU.mult))
        dve.tensor_tensor(g8[:, :, :], gx[:, :, :], al[:, :].unsqueeze(1).broadcast_to([P, NT, 8]), ALU.mult).then_inc(e.g_ready, 1)
        dve.wait_ge(e.cum_done, 1)
        for d in range(2):
            link(dve.tensor_copy(G[:, :, 4 * d:4 * d + 4], g.ps[:, 0, 40 * d:40 * d + 40].rearrange("p (t h) -> p t h", h=4)))
        link(dve.tensor_copy(eL[:, :, :], g.ps[:, 0, 80:160].rearrange("p (t h) -> p t h", h=8)))
        dve.tensor_tensor(eK[:, :, :], eL[:, :, :], G[:, :, :], ALU.subtract).then_inc(e.G_kept, 1)
        dve.wait_ge(e.exps_done, 3)
        dve.wait_ge(e.beta_done, 1)
        dve.tensor_tensor(beG[:, :, :], be[:, :, :], eG[:, :, :], ALU.mult).then_inc(e.decays_ready, 1)
        hh = lambda ap: ap[:, :, :].rearrange("p h i -> p (h i)")
        idb = g.ident[:, :].unsqueeze(1).broadcast_to([P, H, P])
        for n in range(NSTEP):
            for d in range(2):
                t = order[d][n]
                B = 3 * d
                dve.wait_ge(e.prods[d], n + 1)
                link(dve.tensor_tensor(E[d][:, :, :], bc(heads(G, t, d), P), g.ps[:, B, :].rearrange("p (h i) -> p h i", h=H), ALU.subtract))
                link(dve.tensor_scalar(ET[d][:, :, :], E[d][:, :, :], -1.0, 0.0, ALU.mult, ALU.min))
                dve.tensor_scalar(E[d][:, :, :], E[d][:, :, :], 0.0, None, ALU.min).then_inc(e.x_ready[d], 1)
            for d in range(2):
                t = order[d][n]
                B = 3 * d
                dve.wait_ge(e.exp_done[d], 2 * n + 2)
                link(dve.tensor_tensor(E[d][:, :, :], E[d][:, :, :], bc(heads(be, t, d), P), ALU.mult))
                dve.tensor_tensor(hh(E[d]), g.ps[:, B + 1, :], hh(E[d]), ALU.mult).then_inc(e.a_ready[d], 1)
                if t < NL:
                    link(dve.tensor_tensor(hh(ET[d]), g.ps[:, B + 2, :], hh(ET[d]), ALU.mult))
                    link(dve.tensor_tensor(ET[d][:, :, :], ET[d][:, :, :], cum[:, d, :].unsqueeze(1).broadcast_to([P, H, P]), ALU.mult))
                dve.wait_ge(e.a_ready[d], n + 1)
                link(dve.tensor_tensor(Dm[d][:, :, :], E[d][:, :, :], lev[:, 7 * d, :].unsqueeze(1).broadcast_to([P, H, P]), ALU.mult))
                dve.tensor_tensor(Dm[d][:, :, :], idb, Dm[d][:, :, :], ALU.subtract).then_inc(e.d_ready[d], 1)
            for d in range(2):
                dve.wait_ge(e.dt_first[d], n + 1)
                dve.tensor_copy(DT[d][0:1, 0, 0:1], DT[d][0:1, 0, 0:1]).then_inc(e.dt_ready[d], 1)
            for s in range(1, NLEV):
                m = n * (NLEV - 1) + s
                for d in range(2):
                    dve.wait_ge(e.e_done[d], m)
                    if s < NLEV - 1:
                        dve.tensor_tensor(hh(Dm[d]), hh(Dm[d]), g.ps[:, 3 * d + 1, :], ALU.subtract).then_inc(e.d_ready[d], 1)
                    dve.tensor_tensor(hh(DT[d]), hh(DT[d]), g.ps[:, 3 * d + 2, :], ALU.subtract).then_inc(e.dt_ready[d] if s < NLEV - 1 else e.dt_last[d], 1)
            for d in range(2):
                dve.wait_ge(e.v_done[d], n + 1)
                dve.tensor_copy(vn[d][:, :, :].rearrange("p h f -> p (h f)"), g.ps[:, 6 + d, 0:BW]).then_inc(e.v_kept[d], 1)
            for d in range(2):
                t = order[d][n]
                if t < NL:
                    dve.wait_ge(e.o_done[d], n - 1)
                    link(dve.tensor_tensor(ot[d][:, :].rearrange("p (h f) -> p h f", f=HD), g.ps[:, 3 * d, 0:BW].rearrange("p (h f) -> p h f", f=HD),
                                           bc(heads(eG, t, d), HD), ALU.mult))
                    if n - 2 < NL // 2:
                        i = dve.tensor_tensor(og[:, t, :], ot[d][:, :], g.ps[:, 3 * d, BW:2 * BW], ALU.add)
                    else:
                        link(dve.tensor_tensor(ot[d][:, :], ot[d][:, :], g.ps[:, 3 * d, BW:2 * BW], ALU.add))
                        i = dve.tensor_tensor(og[:, t, :], og[:, t, :], ot[d][:, :], ALU.add)
                    i.then_inc(e.o_kept[d], 1)
                dve.wait_ge(e.s_done[d], n + 1)
                for b in range(2):
                    q = slice(64 * b, 64 * b + 64)
                    link(dve.tensor_tensor(St[d][q, b:H:2, :], St[d][q, b:H:2, :], bc(eL[q, t, 4 * d + b:4 * d + 4:2], HD), ALU.mult))
                for b in range(2):
                    q = slice(64 * b, 64 * b + 64)
                    i = dve.tensor_tensor(St[d][q, b:H:2, :], St[d][q, b:H:2, :], g.ps[q, 3 * d + 1, 0:2 * HD].rearrange("p (a f) -> p a f", f=HD), ALU.add)
                i.then_inc(e.s_kept[d], 1)
        for d in range(2):
            dve.wait_ge(e.o_kept[d], NL)
        y3 = og[:, :, :].rearrange("p t (h f) -> p (t h) f", f=HD)
        for half in range(4):
            v = og[:, 2 * half:2 * half + 2, :].rearrange("p t c -> p (t c)")
            link(dve.tensor_tensor(hh(sq), v, v, ALU.mult))
            link(dve.tensor_reduce(rr[:, 8 * half:8 * half + 8], hh(sq).rearrange("p (a f) -> p a f", f=HD), AX.X, ALU.add))
        dve.tensor_scalar(rr[:, :], rr[:, :], 1.0 / HD, EPS, ALU.mult, ALU.add).then_inc(e.ms_done, 1)
        dve.wait_ge(e.rms_done, 1)
        link(dve.reciprocal(rr[:, :], rr[:, :]))
        link(dve.tensor_tensor(y3, y3, bc(rr[:, :], HD), ALU.mult))
        link(dve.tensor_tensor(y3, y3, onb[:, :].unsqueeze(1).broadcast_to([P, NL * H, HD]), ALU.mult))
        dve.wait_ge(e.z_done, 1)
        dve.tensor_tensor(og[:, :, :], og[:, :, :], g.z[:, :, :], ALU.mult).then_inc(e.y_done, 1)
        keep_branch(nc, g, e, dve, 2)


def phase_fourier(nc, g, ctx):
    sb = lambda n, s, d=F32: ctx.enter_context(nc.sbuf_tensor("fo_" + n, s, d))
    wf = sb("wf", [P, KD, BW])
    fT = sb("fT", [P, 2, S])
    bd = sb("bd", [P, 2, P])
    Z = sb("Z", [P, NL, 2, 2, P])
    dft = sb("dft", [P, 2, 2, S])
    wm = sb("wm", [P, 3, KD, MCH])
    spread = sb("spread", [P, KD, P])
    NM = 3 * D // MCH
    e = g.fo
    block = ctx.enter_context(nc.Block())

    @block.sync
    def _(sp):
        sp.dma_start(wf[:, :, :], g.w_in.rearrange("(k p) n -> p k n", p=P)[:, :, COL_F:COL_F + BW]).then_inc(e.w_loaded, 16)
        sp.dma_start(bd[:, :, :], g.k_bdft.rearrange("a p i -> p a i")).then_inc(e.w_loaded, 16)
        for t in range(NL):
            if t >= 2:
                sp.wait_ge(e.dft_used, t - 1)
            sp.dma_start(dft[:, t % 2], g.k_dft[:, t * P:(t + 1) * P, :].rearrange("a p i -> p a i")).then_inc(e.dft_loaded[t % 2], 16)

    @block.tensor
    def _(pe):
        pe.wait_ge(e.w_loaded, 32)
        for c in range(2):
            for j in range(2):
                for k in range(KD):
                    i = pe.matmul(g.ps[:, 2 * c + j, :], wf[:, k, c * P:(c + 1) * P], g.hT[:, k, 512 * j:512 * j + 512], start=(k == 0), stop=(k == KD - 1))
                i.then_inc(e.f_done, 1)
        pe.wait_ge(e.f_kept, 4)
        for t in range(NL):
            if t >= 2:
                pe.wait_ge(e.z_kept, t - 1)
            for a in range(2):
                for c in range(2):
                    i = pe.matmul(g.ps[:, t % 2, (2 * a + c) * P:(2 * a + c + 1) * P], fT[:, c, t * P:(t + 1) * P], bd[:, a, :], start=True, stop=True)
            i.then_inc(e.z_done, 1)
        for t in range(NL):
            pe.wait_ge(e.z_kept, t + 1)
            pe.wait_ge(e.dft_loaded[t % 2], 16 * (t // 2 + 1))
            for a in range(2):
                for c in range(2):
                    for j in range(2):
                        i = pe.matmul(g.ps[:, 4 + 2 * c + j, :], Z[:, t, a, c, :], dft[:, t % 2, a, 512 * j:512 * j + 512],
                                      start=(t == 0 and a == 0), stop=(t == NL - 1 and a == 1))
            i.then_inc(e.dft_used, 1)
            if t < NM:
                if t == 0:
                    pe.wait_ge(e.spread_done, 1)
                pe.wait_ge(e.mod_loaded[t % 3], 16 * (t // 3 + 1))
                if t >= 2:
                    pe.wait_ge(e.mod_kept, t - 1)
                mod_chunk_product(g, pe, 2 + t % 2, spread, wm[:, t % 3]).then_inc(e.mod_done, 1)

    @block.scalar
    def _(act):
        act.wait_ge(e.w_loaded, 32)
        for j in range(3):
            act.dma_start(wm[:, j], mod_chunk_source(g, MROW + j)).then_inc(e.mod_loaded[j], 16)
        for c in range(4):
            act.wait_ge(e.f_done, c + 1)
            act.activation(fT[:, c // 2, 512 * (c % 2):512 * (c % 2) + 512], g.ps[:, c, :], ACT.Copy).then_inc(e.f_kept, 1)
        for j in range(3, NM):
            act.wait_ge(e.mod_done, j - 2)
            act.dma_start(wm[:, j % 3], mod_chunk_source(g, MROW + j)).then_inc(e.mod_loaded[j % 3], 16)

    @block.vector
    def _(dve):
        dve.tensor_copy(spread[:, :, :], bc(g.scol[:, :, 0], P)).then_inc(e.spread_done, 1)
        for t in range(NL):
            dve.wait_ge(e.z_done, t + 1)
            dve.tensor_copy(Z[:, t].rearrange("p a c i -> p (a c i)"), g.ps[:, t % 2, :]).then_inc(e.z_kept, 1)
        for j in range(NM):
            dve.wait_ge(e.mod_done, j + 1)
            mod_chunk_keep(g, dve, MROW + j, 2 + j % 2).then_inc(e.mod_kept, 1)
        dve.wait_ge(e.dft_used, NL)
        for c in range(2):
            for j in range(2):
                dve.tensor_copy(g.brT[:, 6 + c, 512 * j:512 * j + 512], g.ps[:, 4 + 2 * c + j, :])


def phase_merge(nc, g, ctx):
    sb = lambda n, s, d=F32: ctx.enter_context(nc.sbuf_tensor("me_" + n, s, d))
    RING = 3
    w_raw = sb("w_raw", [P, 2, KD, P])
    w_high = sb("w_high", [P, 2, KD, P], F32R)
    w_low = sb("w_low", [P, 2, KD, P], F32R)
    h_high = sb("h_high", [P, KD, S], F32R)
    h_low = g.h_low[:, :, 0:S]
    wb = sb("wb", [P, RING, 2, P])
    gs = sb("gs", [P, 2, S])
    pt = g.stage.rearrange("p t c -> p (t c)").rearrange("p (a t) -> p a t", a=2)
    e = g.me
    w_in = g.w_in.rearrange("(k p) n -> p k n", p=P)
    U = [(c, b) for c in range(KD) for b in range(4)]
    NU = len(U)
    block = ctx.enter_context(nc.Block())

    @block.sync
    def _(sp):
        for u, (c, b) in enumerate(U):
            o = COL_G + b * D + c * P
            if u >= 2:
                sp.wait_ge(e.w_low_done, u - 1)
            sp.dma_start(w_raw[:, u % 2], w_in[:, :, o:o + P]).then_inc(e.wg_loaded[u % 2], 16)
            if u >= RING:
                sp.wait_ge(e.proj_done, u - RING + 1)
            sp.dma_start(wb[:, u % RING], g.w_branch[b].rearrange("(k p) n -> p k n", p=P)[:, :, c * P:(c + 1) * P]).then_inc(e.wb_loaded[u % RING], 16)

    @block.tensor
    def _(pe):
        for u, (c, b) in enumerate(U):
            s, w = 2 * (u % 2), u % RING
            pe.wait_ge(e.wb_loaded[w], 16 * (u // RING + 1))
            if u >= 2:
                pe.wait_ge(e.mult_done, u - 1)
            for j in range(2):
                for k in range(2):
                    i = pe.matmul(g.ps[:, 4 + s + j, :], wb[:, w, k, :], g.brT[:, 2 * b + k, 512 * j:512 * j + 512], start=(k == 0), stop=(k == 1))
            i.then_inc(e.proj_done, 1)
            if u >= 2:
                pe.wait_ge(e.gate_done, u - 1)
            pe.wait_ge(e.w_low_done, u + 1)
            for j in range(2):
                cols = slice(512 * j, 512 * j + 512)
                for k in range(KD):
                    if u == 0 and j == 0:
                        pe.wait_ge(e.h_low_done, k + 1)
                    wh, wl = w_high[:, u % 2, k, :], w_low[:, u % 2, k, :]
                    pe.matmul(g.ps[:, s + j, :], wh, h_high[:, k, cols], start=(k == 0), stop=False)
                    pe.matmul(g.ps[:, s + j, :], wh, h_low[:, k, cols], start=False, stop=False)
                    i = pe.matmul(g.ps[:, s + j, :], wl, h_high[:, k, cols], start=False, stop=(k == KD - 1))
            i.then_inc(e.gate_in, 1)

    @block.scalar
    def _(act):
        def high(u):
            act.wait_ge(e.wg_loaded[u % 2], 16 * (u // 2 + 1))
            if u >= 2:
                act.wait_ge(e.gate_in, u - 1)
            act.activation(w_high[:, u % 2], w_raw[:, u % 2], ACT.Copy).then_inc(e.w_high_done, 1)

        for k in range(KD):
            act.activation(h_high[:, k, :], g.hT[:, k, 0:S], ACT.Copy).then_inc(e.h_high_done, 1)
            if k == 2:
                high(0)
        high(1)
        for u in range(NU):
            act.wait_ge(e.gate_in, u + 1)
            if u >= 2:
                act.wait_ge(e.mult_done, u - 1)
            act.activation(gs[:, u % 2, :], g.ps[:, 2 * (u % 2):2 * (u % 2) + 2, :].rearrange("p a b -> p (a b)"), ACT.Sigmoid).then_inc(e.gate_done, 1)
            if u + 2 < NU:
                high(u + 2)

    @block.vector
    def _(dve):
        def low(u):
            dve.wait_ge(e.w_high_done, u + 1)
            if u >= 2:
                dve.wait_ge(e.gate_in, u - 1)
            dve.tensor_tensor(w_low[:, u % 2], w_raw[:, u % 2], w_high[:, u % 2].bitcast(F32), ALU.subtract).then_inc(e.w_low_done, 1)

        for k in range(KD):
            dve.wait_ge(e.h_high_done, k + 1)
            dve.tensor_tensor(h_low[:, k, :], g.hT[:, k, 0:S], h_high[:, k, :].bitcast(F32), ALU.subtract).then_inc(e.h_low_done, 1)
            if k == 2:
                low(0)
        low(1)
        for u, (c, b) in enumerate(U):
            dve.wait_ge(e.gate_done, u + 1)
            dve.wait_ge(e.proj_done, u + 1)
            if u >= 2:
                dve.wait_ge(e.added, u - 1)
            dst = g.yT[:, c, :] if b == 0 else pt[:, u % 2, :]
            dve.tensor_tensor(dst, gs[:, u % 2, :], g.ps[:, 4 + 2 * (u % 2):6 + 2 * (u % 2), :].rearrange("p a b -> p (a b)"), ALU.mult).then_inc(e.mult_done, 1)
            if u + 2 < NU:
                low(u + 2)

    @block.gpsimd
    def _(pool):
        for u, (c, b) in enumerate(U):
            pool.wait_ge(e.mult_done, u + 1)
            if u:
                pool.wait_ge(e.added, u)
            if b == 0:
                pool.sem_inc(e.added, 1)
            else:
                pool.tensor_tensor(g.yT[:, c, :], g.yT[:, c, :], pt[:, u % 2, :], ALU.add).then_inc(e.added, 1)


def phase_out(nc, g, ctx):
    sb = lambda n, s, d=F32: ctx.enter_context(nc.sbuf_tensor("ou_" + n, s, d))
    wo = sb("wo", [P, KD, D])
    xt = sb("xt", [P, 2, D])
    junk = sb("junk", [P, D])
    ss = sb("ss", [P, NL])
    a2 = sb("a2", [P, D])
    wr = sb("wr", [P, KD, NEXP])
    hTt = sb("hTt", [P, KD, P])
    e, link = g.ou, g.link
    g1, sh2, sc2 = g.modb[:, 0:D], g.modb[:, D:2 * D], g.modb[:, 2 * D:3 * D]
    h2 = g.h2
    block = ctx.enter_context(nc.Block())

    @block.sync
    def _(sp):
        sp.dma_start(wo[:, :, :], g.w_out.rearrange("(k p) n -> p k n", p=P)).then_inc(e.w_loaded, 16)
        sp.dma_start(a2[:, :], g.norm2_g.partition_broadcast(P)).then_inc(e.w_loaded, 16)
        sp.dma_start(wr[:, :, :], g.w_router.rearrange("(k p) n -> p k n", p=P)).then_inc(e.w_loaded, 16)
        for t in range(NL):
            if t >= 2:
                sp.wait_ge(e.x1_done, t - 1)
            sp.dma_start(xt[:, t % 2], g.x[0, t * P:(t + 1) * P, :]).then_inc(e.x_loaded[t % 2], 16)
        for t in range(NL):
            sp.wait_ge(e.x1_done, t + 1)
            sp.dma_start(g.x1_dram[t * P:(t + 1) * P, :], g.x1[:, t, :]).then_inc(e.x1_stored, 16)
        sp.wait_ge(e.x1_stored, 16 * NL)

    @block.tensor
    def _(pe):
        pe.wait_ge(e.w_loaded, 48)

        def route(t):
            pe.wait_ge(e.h2_done, t + 1)
            if t:
                pe.wait_ge(e.hT_act, t)
                pe.wait_ge(e.hT_dve, t)
            for k in range(KD):
                i = pe.transpose(g.ps[:, 4 + k // 4, (k % 4) * P:(k % 4 + 1) * P], h2[:, t, k * P:(k + 1) * P], g.ident[:, :])
            i.then_inc(e.turned, 1)
            pe.wait_ge(e.hT_act, t + 1)
            pe.wait_ge(e.hT_dve, t + 1)
            if t:
                pe.wait_ge(e.scored, t)
            for k in range(KD):
                i = pe.matmul(g.ps[:, 6, 0:NEXP], hTt[:, k, :], wr[:, k, :], start=(k == 0), stop=(k == KD - 1))
            i.then_inc(e.logits, 1)

        for t in range(NL):
            if t >= 2:
                pe.wait_ge(e.y_read, t - 1)
            for j in range(2):
                for k in range(KD):
                    i = pe.matmul(g.ps[:, 2 * (t % 2) + j, :], g.yT[:, k, t * P:(t + 1) * P], wo[:, k, 512 * j:512 * j + 512], start=(k == 0), stop=(k == KD - 1))
            i.then_inc(e.y_done, 1)
            if t:
                route(t - 1)
        route(NL - 1)

    @block.scalar
    def _(act):
        def keep(t):
            act.wait_ge(e.turned, t + 1)
            if t:
                act.wait_ge(e.logits, t)
            act.activation(hTt[:, 4:8, :].rearrange("p k i -> p (k i)"), g.ps[:, 5, :], ACT.Copy).then_inc(e.hT_act, 1)
            act.wait_ge(e.logits, t + 1)
            act.activation(g.scores[:, t, :], g.ps[:, 6, 0:NEXP], ACT.Sigmoid).then_inc(e.scored, 1)

        for t in range(NL):
            act.wait_ge(e.x1_done, t + 1)
            if t:
                act.wait_ge(e.sq_done, t)
            act.activation(junk[:, :], g.x1[:, t, :], ACT.Square, accum_out=ss[:, t:t + 1]).then_inc(e.sq_done, 1)
            act.wait_ge(e.ms_done, t + 1)
            act.activation(ss[:, t:t + 1], ss[:, t:t + 1], ACT.Sqrt).then_inc(e.rms_done, 1)
            if t:
                keep(t - 1)
        keep(NL - 1)

    @block.vector
    def _(dve):
        dve.wait_ge(e.w_loaded, 48)
        link(dve.scalar_tensor_tensor(a2[:, :], sc2, 1.0, a2[:, :], ALU.add, ALU.mult))

        def keep(t):
            dve.wait_ge(e.turned, t + 1)
            if t:
                dve.wait_ge(e.logits, t)
            dve.tensor_copy(hTt[:, 0:4, :].rearrange("p k i -> p (k i)"), g.ps[:, 4, :]).then_inc(e.hT_dve, 1)

        for t in range(NL):
            dve.wait_ge(e.y_done, t + 1)
            x1 = g.x1[:, t, :]
            dve.tensor_tensor(x1, g.ps[:, 2 * (t % 2):2 * (t % 2) + 2, :].rearrange("p a b -> p (a b)"), g1, ALU.mult).then_inc(e.y_read, 1)
            dve.wait_ge(e.y_read, t + 1)
            dve.wait_ge(e.x_loaded[t % 2], 16 * (t // 2 + 1))
            dve.tensor_tensor(x1, x1, xt[:, t % 2], ALU.add).then_inc(e.x1_done, 1)
            if t:
                keep(t - 1)
            dve.wait_ge(e.sq_done, t + 1)
            dve.tensor_scalar(ss[:, t:t + 1], ss[:, t:t + 1], 1.0 / D, EPS, ALU.mult, ALU.add).then_inc(e.ms_done, 1)
            dve.wait_ge(e.rms_done, t + 1)
            link(dve.reciprocal(ss[:, t:t + 1], ss[:, t:t + 1]))
            link(dve.scalar_tensor_tensor(h2[:, t, :], x1, ss[:, t:t + 1], a2[:, :], ALU.mult, ALU.mult))
            dve.tensor_tensor(h2[:, t, :], h2[:, t, :], sh2, ALU.add).then_inc(e.h2_done, 1)
        keep(NL - 1)


def phase_route(nc, g, ctx):
    sb = lambda n, s, d=F32: ctx.enter_context(nc.sbuf_tensor("ro_" + n, s, d))
    sel = sb("sel", [P, NL, NEXP])
    rb = sb("rb", [P, NEXP])
    pair = sb("pair", [P, 6, NL * NGRP])
    gsc = sb("gsc", [P, NL, NGRP])
    gm = sb("gm", [P, NL])
    one4 = sb("one4", [P, NL, NGRP])
    idx = sb("idx", [P, 2, NEXP])
    t4 = sb("t4", [P, NL, NGRP])
    tE = sb("tE", [P, NL, NEXP])
    m1 = sb("m1", [P, NL])
    oh = sb("oh", [P, 2, NL, NEXP])
    A = sb("A", [P, NL, NEXP])
    tri = sb("tri", [P, 2, P])
    pos = sb("pos", [P, NL, NEXP])
    tot = sb("tot", [P, NL + 1, NEXP])
    nb = sb("nb", [P, NEXP])
    nb2 = sb("nb2", [P, NEXP])
    pe_ = sb("pend", [P, NEXP])
    ps_ = sb("pstart", [P, NEXP])
    cmp3 = sb("cmp3", [P, 8, NEXP])
    blk = sb("blk", [P, 32])
    bcmp = sb("bcmp", [P, 32, NEXP])
    bexp = sb("bexp", [P, 32])
    fresh = sb("fresh", [P, 32])
    run = sb("run", [P, 2, 2, 32])
    dst = sb("dst", [P, 2, NL])
    ws = sb("ws", [P, 3, NL])
    wm = sb("wm", [P, 2, KD, MCH])
    spread = sb("spread", [P, KD, P])
    J0 = 5 * D // MCH
    e, link = g.ro, g.link
    block = ctx.enter_context(nc.Block())
    NEGB = 1e30

    @block.sync
    def _(sp):
        sp.dma_start(rb[:, :], g.router_bias.partition_broadcast(P)).then_inc(e.loaded, 16)
        sp.dma_start(blk[:, :], g.k_blk).then_inc(e.loaded, 16)
        sp.dma_start(tri[:, 0, :], g.k_cum[0]).then_inc(e.loaded, 16)
        for j in range(2):
            sp.dma_start(wm[:, j], mod_chunk_source(g, J0 + j)).then_inc(e.mod_loaded[j], 16)

    @block.gpsimd
    def _(pool):
        pool.wait_ge(e.dst_done, 1)
        for k in range(2):
            for t in range(NL):
                pool.indirect_dma_start(g.xs[:, :], bass.IndirectOffsetOnAxis(ap=g.dsti[:, k * NL + t:k * NL + t + 1], axis=0), g.h2[:, t, :], None).then_inc(e.scattered, 16)
        pool.wait_ge(e.scattered, 32 * NL)

    @block.tensor
    def _(pe):
        pe.wait_ge(e.a_done, 1)
        v = A[:, :, :].rearrange("p t e -> p (t e)")
        pe.matmul(g.ps[:, 0, 0:P], tri[:, 0, :], v, start=True, stop=True)
        pe.matmul(g.ps[:, 0, P:2 * P], tri[:, 1, :], v, start=True, stop=True).then_inc(e.counted, 1)
        pe.wait_ge(e.spread_done, 1)
        for j in range(2):
            pe.wait_ge(e.mod_loaded[j], 16)
            mod_chunk_product(g, pe, 1 + j, spread, wm[:, j]).then_inc(e.mod_done, 1)

    @block.vector
    def _(dve):
        tt, ts, tr = dve.tensor_tensor, dve.tensor_scalar, dve.tensor_reduce
        sc = g.scores
        dve.tensor_copy(spread[:, :, :], bc(g.scol[:, :, 0], P)).then_inc(e.spread_done, 1)
        for i in range(NEXP):
            dve.memset(idx[:, 0, i:i + 1], float(i))
            link(dve.memset(idx[:, 1, i:i + 1], float(NEXP - i)))
        link(dve.memset(tri[:, 1, :], 1.0))
        dve.wait_ge(e.loaded, 48)
        link(tt(sel[:, :, :], sc[:, :, :], rb[:, :].unsqueeze(1).broadcast_to([P, NL, NEXP]), ALU.add))
        s4 = sel[:, :, :].rearrange("p t (g m) -> p (t g) m", m=PERG)
        for n, (a, b) in enumerate(((0, 1), (0, 2), (0, 3), (1, 2), (1, 3), (2, 3))):
            link(tt(pair[:, n, :], s4[:, :, a], s4[:, :, b], ALU.add))
        gf = gsc[:, :, :].rearrange("p t g -> p (t g)")
        link(tr(gf, pair[:, :, :].rearrange("p n x -> p x n"), AX.X, ALU.max))
        link(tr(gm[:, :], gsc[:, :, :], AX.X, ALU.max))

        def first_of(out, val, m, n, tmp):
            w = idx[:, 1, 0:n].unsqueeze(1).broadcast_to([P, NL, n])
            link(tt(tmp, val, bc(m, n), ALU.is_equal))
            link(tt(tmp, tmp, w, ALU.mult))
            link(tr(m, tmp, AX.X, ALU.max))
            link(tt(out, w, bc(m, n), ALU.is_equal))

        first_of(one4[:, :, :], gsc[:, :, :], gm[:, :], NGRP, t4[:, :, :])
        ig = bc(one4[:, :, :].rearrange("p t g -> p (t g)"), PERG)
        link(tt(s4, s4, ig, ALU.mult))
        link(ts(t4[:, :, :], one4[:, :, :], 1.0, NEGB, ALU.subtract, ALU.mult))
        link(tt(s4, s4, bc(t4[:, :, :].rearrange("p t g -> p (t g)"), PERG), ALU.add))
        for k in range(2):
            link(tr(m1[:, :], sel[:, :, :], AX.X, ALU.max))
            first_of(oh[:, k], sel[:, :, :], m1[:, :], NEXP, tE[:, :, :])
            if k == 0:
                link(ts(tE[:, :, :], oh[:, 0], -3.0 * NEGB, None, ALU.mult))
                link(tt(sel[:, :, :], sel[:, :, :], tE[:, :, :], ALU.add))
        link(tt(A[:, :, :], oh[:, 0], oh[:, 1], ALU.add))
        link(tt(tri[:, 0, :], tri[:, 0, :], g.ident[:, :], ALU.subtract))
        dve.tensor_copy(A[:, :, :], A[:, :, :]).then_inc(e.a_done, 1)
        for k in range(2):
            link(tt(tE[:, :, :], oh[:, k], sc[:, :, :], ALU.mult))
            link(tr(ws[:, k, :], tE[:, :, :], AX.X, ALU.add))
        link(tt(ws[:, 2, :], ws[:, 0, :], ws[:, 1, :], ALU.add))
        link(dve.reciprocal(ws[:, 2, :], ws[:, 2, :]))
        for k in range(2):
            link(tt(g.wts[:, k, :], ws[:, k, :], ws[:, 2, :], ALU.mult))
        dve.wait_ge(e.counted, 1)
        link(dve.tensor_copy(pos[:, :, :].rearrange("p t e -> p (t e)"), g.ps[:, 0, 0:P]))
        link(dve.memset(tot[:, 0, :], 0.0))
        for t in range(NL):
            link(tt(tot[:, t + 1, :], g.ps[:, 0, P + t * NEXP:P + (t + 1) * NEXP], tot[:, t, :], ALU.add))
        link(tt(pos[:, :, :], pos[:, :, :], tot[:, 0:NL, :], ALU.add))
        link(tt(cmp3[:, :, :], tot[:, NL, :].unsqueeze(1).broadcast_to([P, 8, NEXP]), bc(g_mult128(g, dve, link, blk), NEXP), ALU.is_gt))
        link(tr(nb[:, :], cmp3[:, :, :].rearrange("p j e -> p e j"), AX.X, ALU.add))
        link(dve.tensor_copy(pe_[:, :], nb[:, :]))
        a, b = pe_, nb2
        for s in (1, 2, 4, 8):
            link(dve.tensor_copy(b[:, 0:s], a[:, 0:s]))
            link(tt(b[:, s:], a[:, s:], a[:, 0:NEXP - s], ALU.add))
            a, b = b, a
        link(tt(ps_[:, :], a[:, :], nb[:, :], ALU.subtract))
        link(ts(ps_[:, :], ps_[:, :], float(P), None, ALU.mult))
        link(ts(a[:, :], a[:, :], float(P), None, ALU.mult))
        link(tt(bcmp[:, :, :], bc(blk[:, :], NEXP), a[:, :].unsqueeze(1).broadcast_to([P, 32, NEXP]), ALU.is_ge))
        link(tr(bexp[:, :], bcmp[:, :, :], AX.X, ALU.add))
        link(ts(bexp[:, :], bexp[:, :], float(NEXP - 1), None, ALU.min))
        link(dve.tensor_copy(g.bexpi[:, EXPERT, :], bexp[0:1, :]))
        link(dve.memset(fresh[:, 0:1], 1.0))
        link(tt(fresh[:, 1:], bexp[:, 0:31], bexp[:, 1:], ALU.is_lt))
        link(dve.tensor_copy(g.bexpi[:, FRESH, :], fresh[0:1, :]))
        link(dve.tensor_copy(run[:, 0, 0, :], fresh[:, :]))
        link(ts(run[:, 0, 1, :], fresh[:, :], -2.0, 1.0, ALU.mult, ALU.add))
        now, then = 0, 1
        for s in (1, 2, 4, 8, 16):
            link(dve.tensor_copy(run[:, then, :, 0:s], run[:, now, :, 0:s]))
            link(tt(run[:, then, 0, s:], run[:, now, 0, s:], run[:, now, 0, 0:32 - s], ALU.add))
            link(tt(run[:, then, 1, s:], run[:, now, 1, s:], run[:, now, 1, 0:32 - s], ALU.mult))
            now, then = then, now
        link(ts(run[:, now, 0, :], run[:, now, 0, :], 16.0, None, ALU.mult))
        link(dve.tensor_copy(g.bexpi[:, SETS16, :], run[0:1, now, 0, :]))
        link(ts(run[:, now, 1, :], run[:, now, 1, :], 0.5, 0.5, ALU.mult, ALU.add))
        link(dve.tensor_copy(g.bexpi[:, SLOT, :], run[0:1, now, 1, :]))
        link(tt(bexp[:, 0:16], blk[:, 0:32:2], a[:, NEXP - 1:NEXP].broadcast_to([P, 16]), ALU.is_lt))
        link(tr(gm[:, 0:1], bexp[:, 0:16], AX.X, ALU.add))
        link(dve.tensor_copy(g.bexpi[:, PAIRS, 0:1], gm[0:1, 0:1]))
        link(tt(pos[:, :, :], pos[:, :, :], ps_[:, :].unsqueeze(1).broadcast_to([P, NL, NEXP]), ALU.add))
        for k in range(2):
            link(tt(tE[:, :, :], oh[:, k], pos[:, :, :], ALU.mult))
            link(tr(dst[:, k, :], tE[:, :, :], AX.X, ALU.add))
        dve.tensor_copy(g.dsti[:, :], dst[:, :, :].rearrange("p k t -> p (k t)")).then_inc(e.dst_done, 1)
        for j in range(2):
            dve.wait_ge(e.mod_done, j + 1)
            mod_chunk_keep(g, dve, J0 + j, 1 + j)


def g_mult128(g, dve, link, blk):
    link(dve.tensor_scalar(blk[:, :], blk[:, :], float(P), None, ALU.mult))
    return blk[:, 0:8]


def phase_experts(nc, g, ctx):
    sb = lambda n, s, d=F32: ctx.enter_context(nc.sbuf_tensor("ex_" + n, s, d))
    two = lambda n, s: [sb(f"{n}{j}", s) for j in range(2)]
    Wg, Wu, Wd = sb("Wg", [P, 2, KD * FF]), sb("Wu", [P, 2, KD * FF]), sb("Wd", [P, 2, FF * D // P])
    xt, xT = two("xt", [P, D]), two("xT", [P, KD, P])
    gs, hh, hT = two("gs", [P, FF]), two("hh", [P, FF]), two("hT", [P, FF // P, P])
    yo = two("yo", [P, D])
    zt = sb("zt", [P, D])
    e = g.ex
    xs = g.xs.rearrange("(n p) d -> n p d", p=P)
    ys = g.ys.rearrange("(n p) d -> n p d", p=P)
    wgv = g.moe_w_gate.rearrange("e (k p) f -> e p k f", p=P)
    wuv = g.moe_w_up.rearrange("e (k p) f -> e p k f", p=P)
    wdv = g.moe_w_down.rearrange("e (k p) f -> e p k f", p=P)
    flat = lambda t: t[:, :, :].rearrange("p k i -> p (k i)")
    DOWN = ((0, 1), (7, 6))
    block = ctx.enter_context(nc.Block())
    N2 = NBLK_RUN // 2

    def pairs(eng):
        return eng.value_load(g.bexpi[0:1, PAIRS, 0:1], min_val=1, max_val=N2)

    def entry(eng, what, i, least, most):
        return eng.value_load(g.bexpi[0:1, what, bass.ds(i, 1)], min_val=least, max_val=most)

    @block.sync
    def _(sp):
        n = pairs(sp)
        one3 = lambda v, i: v[bass.ds(i, 1)].rearrange("o p a -> (o p) a")
        one4 = lambda v, i: v[bass.ds(i, 1)].rearrange("o p k f -> (o p) k f")
        slot_of = lambda W, w, n: W[:, bass.ds(w, 1), :].rearrange("p o (k f) -> p (o k) f", f=n)
        for loaded in (e.g_loaded, e.u_loaded, e.d_loaded):
            sp.sem_inc(loaded, 16)
        with sp.Fori(0, N2) as j:
            with sp.If(j < n):
                for s in range(2):
                    i = 2 * j + s
                    sp.wait_ge(e.x_free[s], j + 1)
                    sp.dma_start(xt[s][:, :], one3(xs, i)).then_inc(e.x_loaded[s], 16)
                    fresh = entry(sp, FRESH, i, 0, 1)
                    with sp.If(fresh > 0):
                        ex = entry(sp, EXPERT, i, 0, NEXP - 1)
                        w = entry(sp, SLOT, i, 0, 1)
                        sets = entry(sp, SETS16, i, 16, 16 * NEXP)
                        for W, v, loaded, free, n_ in ((Wg, wgv, e.g_loaded, e.g_free, FF), (Wu, wuv, e.u_loaded, e.u_free, FF), (Wd, wdv, e.d_loaded, e.d_free, D)):
                            sp.wait_ge(free[s], j + 1)
                            sp.wait_ge(loaded, sets)
                            sp.sem_inc(e.part_asked, 1)
                            sp.dma_start(slot_of(W, w, n_), one4(v, ex)).then_inc(loaded, 16)

    @block.tensor
    def _(pe):
        n = pairs(pe)
        for s in range(2):
            for f in (e.x_free, e.g_free, e.u_free, e.d_free):
                pe.sem_inc(f[s], 1)
        part = lambda W, w, at: W[:, bass.ds(w, 1), at:at + 512].rearrange("p o f -> p (o f)")
        with pe.Fori(0, N2) as j:
            with pe.If(j < n):
                sets = [entry(pe, SETS16, 2 * j + s, 16, 16 * NEXP) for s in range(2)]
                slot = [entry(pe, SLOT, 2 * j + s, 0, 1) for s in range(2)]
                for s in range(2):
                    pe.wait_ge(e.x_loaded[s], 16 * j + 16)
                    if s == 0:
                        pe.wait_ge(e.y_act[0], j + 1)
                        pe.wait_ge(e.y_dve[0], j + 1)
                    else:
                        pe.wait_ge(e.xT_act[0], j + 1)
                        pe.wait_ge(e.xT_dve[0], j + 1)
                    for k in range(KD):
                        i = pe.transpose(g.ps[:, k // 4, (k % 4) * P:(k % 4 + 1) * P], xt[s][:, k * P:(k + 1) * P], g.ident[:, :])
                    i.then_inc(e.x_free[s], 1)

                def gate_up(s):
                    pe.wait_ge(e.xT_act[s], j + 1)
                    pe.wait_ge(e.xT_dve[s], j + 1)
                    for w, W, loaded, free in ((0, Wg, e.g_loaded, e.g_free), (1, Wu, e.u_loaded, e.u_free)):
                        pe.wait_ge(loaded, sets[s] + 16)
                        for k in range(KD):
                            i = pe.matmul(g.ps[:, 2 + 2 * s + w, :], xT[s][:, k, :], part(W, slot[s], k * FF), start=(k == 0), stop=(k == KD - 1))
                        i.then_inc(free[s], 1)

                def turn_h(s):
                    pe.wait_ge(e.h_done[s], j + 1)
                    if s == 0:
                        pe.wait_ge(e.y_dve[1], j + 1)
                    for k in range(FF // P):
                        i = pe.transpose(g.ps[:, 6, k * P:(k + 1) * P], hh[s][:, k * P:(k + 1) * P], g.ident[:, :])
                    i.then_inc(e.h_turned[s], 1)

                def down(s):
                    pe.wait_ge(e.hT_kept[s], j + 1)
                    pe.wait_ge(e.d_loaded, sets[s] + 16)
                    if s == 1:
                        pe.wait_ge(e.y_act[1], j + 1)
                    for m in range(2):
                        for k in range(FF // P):
                            i = pe.matmul(g.ps[:, DOWN[s][m], :], hT[s][:, k, :], part(Wd, slot[s], k * D + 512 * m), start=(k == 0), stop=(k == FF // P - 1))
                    i.then_inc(e.d_free[s], 1)

                gate_up(0)
                gate_up(1)
                turn_h(0)
                down(0)
                turn_h(1)
                down(1)

    @block.scalar
    def _(act):
        n = pairs(act)
        act.wait_ge(e.zero_made, 1)
        for s in range(2):
            act.sem_inc(e.y_free[s], 16)
            act.sem_inc(e.y_act[s], 1)
        with act.Fori(0, N2) as j:
            with act.If(j < n):
                for s in range(2):
                    act.wait_ge(e.x_free[s], j + 2)
                    act.activation(xT[s][:, 4:8, :].rearrange("p k i -> p (k i)"), g.ps[:, 1, :], ACT.Copy).then_inc(e.xT_act[s], 1)

                def silu(s):
                    act.wait_ge(e.g_free[s], j + 2)
                    act.activation(gs[s][:, :], g.ps[:, 2 + 2 * s, :], ACT.Silu).then_inc(e.silu_done[s], 1)

                def finish(s):
                    act.wait_ge(e.d_free[s], j + 2)
                    act.wait_ge(e.y_free[s], 16 * j + 16)
                    act.activation(yo[s][:, 0:512], g.ps[:, DOWN[s][0], :], ACT.Copy).then_inc(e.y_act[s], 1)
                    act.wait_ge(e.y_act[s], j + 2)
                    act.wait_ge(e.y_dve[s], j + 2)
                    act.dma_start(ys[bass.ds(2 * j + s, 1)].rearrange("o p a -> (o p) a"), yo[s][:, :]).then_inc(e.y_free[s], 16)

                def keep_h(s):
                    act.wait_ge(e.h_turned[s], j + 1)
                    act.activation(flat(hT[s]), g.ps[:, 6, :], ACT.Copy).then_inc(e.hT_kept[s], 1)

                silu(0)
                silu(1)
                keep_h(0)
                keep_h(1)
                finish(0)
                finish(1)
            with act.Else():
                for s in range(2):
                    act.dma_start(ys[bass.ds(2 * j + s, 1)].rearrange("o p a -> (o p) a"), zt[:, :]).then_inc(e.y_free[s], 16)
        for s in range(2):
            act.wait_ge(e.y_free[s], 16 * (N2 + 1))

    @block.vector
    def _(dve):
        n = pairs(dve)
        dve.memset(zt[:, :], 0.0).then_inc(e.zero_made, 1)
        for s in range(2):
            dve.sem_inc(e.y_dve[s], 1)
        with dve.Fori(0, N2) as j:
            with dve.If(j < n):
                for s in range(2):
                    dve.wait_ge(e.x_free[s], j + 2)
                    dve.tensor_copy(xT[s][:, 0:4, :].rearrange("p k i -> p (k i)"), g.ps[:, 0, :]).then_inc(e.xT_dve[s], 1)
                for s in range(2):
                    dve.wait_ge(e.silu_done[s], j + 1)
                    dve.wait_ge(e.u_free[s], j + 2)
                    dve.tensor_tensor(hh[s][:, :], gs[s][:, :], g.ps[:, 3 + 2 * s, :], ALU.mult).then_inc(e.h_done[s], 1)
                for s in range(2):
                    dve.wait_ge(e.d_free[s], j + 2)
                    dve.wait_ge(e.y_free[s], 16 * j + 16)
                    dve.tensor_copy(yo[s][:, 512:1024], g.ps[:, DOWN[s][1], :]).then_inc(e.y_dve[s], 1)


def phase_combine(nc, g, ctx):
    sb = lambda n, s, d=F32: ctx.enter_context(nc.sbuf_tensor("co_" + n, s, d))
    ya = sb("ya", [P, 2, 4, D])
    x1 = sb("x1", [P, 4, D])
    g2 = g.modb[:, 3 * D:4 * D]
    e, link = g.co, g.link
    block = ctx.enter_context(nc.Block())

    @block.gpsimd
    def _(pool):
        for t in range(NL):
            if t >= 4:
                pool.wait_ge(e.out_done, t - 3)
            for k in range(2):
                pool.indirect_dma_start(ya[:, k, t % 4, :], None, g.ys[:, :], bass.IndirectOffsetOnAxis(ap=g.dsti[:, k * NL + t:k * NL + t + 1], axis=0)).then_inc(e.y_loaded[t % 4], 16)

    @block.sync
    def _(sp):
        for t in range(NL):
            if t >= 4:
                sp.wait_ge(e.stored[t % 4], 16)
            sp.dma_start(x1[:, t % 4], g.x1_dram[t * P:(t + 1) * P, :]).then_inc(e.x_loaded[t % 4], 16)

    @block.vector
    def _(dve):
        for t in range(NL):
            s = t % 4
            dve.wait_ge(e.y_loaded[s], 32 * (t // 4 + 1))
            link(dve.tensor_scalar(ya[:, 0, s, :], ya[:, 0, s, :], g.wts[:, 0, t:t + 1], None, ALU.mult))
            link(dve.scalar_tensor_tensor(ya[:, 1, s, :], ya[:, 1, s, :], g.wts[:, 1, t:t + 1], ya[:, 0, s, :], ALU.mult, ALU.add))
            link(dve.tensor_tensor(ya[:, 1, s, :], ya[:, 1, s, :], g2, ALU.mult))
            dve.wait_ge(e.x_loaded[s], 16 * (t // 4 + 1))
            dve.tensor_tensor(x1[:, s, :], x1[:, s, :], ya[:, 1, s, :], ALU.add).then_inc(e.out_done, 1)

    @block.scalar
    def _(act):
        for t in range(NL):
            act.wait_ge(e.out_done, t + 1)
            act.dma_start(g.out[0, t * P:(t + 1) * P, :], x1[:, t % 4]).then_inc(e.stored[t % 4], 16)
        for s in range(4):
            act.wait_ge(e.stored[s], 32)


def phase_events(nc, prefix, names):
    made = {}
    for word in names.split():
        name, _, count = word.partition("*")
        sems = [nc.alloc_semaphore(name=f"{prefix}_{name}{j}") for j in range(int(count or 1))]
        made[name] = sems if count else sems[0]
    return named(**made, every=[s for v in made.values() for s in (v if isinstance(v, list) else [v])])


def phase_end(nc, events):
    nc.clear_and_free_semaphores(events.every)
    nc.all_engine_barrier()


def trunk(nc, g):
    top = ExitStack()
    with top:
        sem = lambda n: top.enter_context(nc.semaphore(n))
        g.link = Chain(nc.vector, sem("dve_order"))
        g.alink = Chain(nc.scalar, sem("act_order"))
        g.plink = Chain(nc.gpsimd, sem("pool_order"))
        g.rpb_rep = nc.dram_tensor("rpb_rep", (H, 20, GRID_W, P), F32).ap()
        g.rpb_pad = nc.dram_tensor("rpb_pad", (H, 20, P), F32).ap()
        g.ps = top.enter_context(nc.psum_tensor("ps", [P, 8, 512], F32))
        keep = lambda n, s, d=F32: top.enter_context(nc.sbuf_tensor(n, s, d))
        g.ident = keep("ident", [P, P])
        g.scol = keep("scol", [P, KD, 2])
        g.acol = keep("acol", [P, KD, 2])
        g.bcol = keep("bcol", [P, KD, 2])
        g.modb = keep("modb", [P, 4 * D])
        g.scores = keep("scores", [P, NL, NEXP])
        g.wts = keep("wts", [P, 2, NL])
        g.dsti = keep("dsti", [P, 2 * NL], U32)
        g.bexpi = keep("bexpi", [1, 5, 32], I32)
        g.xs = nc.dram_tensor("xs", (NBLK_RUN * P, D), F32).ap()
        g.ys = nc.dram_tensor("ys", (NBLK_RUN * P, D), F32).ap()
        g.x1_dram = nc.dram_tensor("x1_dram", (S, D), F32).ap()
        mid = ExitStack()
        keep = lambda n, s, d=F32: mid.enter_context(nc.sbuf_tensor(n, s, d))
        g.z = keep("z", [P, NL, BW])
        g.ab = keep("ab", [P, NT, 16])
        region = keep("region", [P, NT * D])
        g.xall = region[:, :].rearrange("p (t d) -> p t d", t=NT)
        g.stage = region[:, 8 * S:].rearrange("p (t c) -> p t c", t=NL)
        g.brT = region[:, 0:8 * S].rearrange("p (b t) -> p b t", b=8)
        tokens_turned = ExitStack()
        g.hT = tokens_turned.enter_context(nc.sbuf_tensor("hT", [P, KD, T], F32))
        with ExitStack() as att:
            a = lambda n, s, d=F32: att.enter_context(nc.sbuf_tensor(n, s, d))
            g.attmem = a("attmem", [P, 4 * S + 8 * T])
            turned = lambda at, n: g.attmem[:, at:at + 2 * n].rearrange("p (a t) -> p a t", a=2)
            tokens = lambda at: g.attmem[:, at:at + NT * BW].rearrange("p (t c) -> p t c", t=NT)
            g.naQ, g.naK = turned(0, S), turned(2 * S, T)
            g.daQ, g.daK = turned(2 * (S + T), S), turned(4 * S + 2 * T, T)
            g.naV, g.daV = tokens(4 * (S + T)), tokens(4 * (S + T) + NT * BW)
            g.mo = phase_events(nc, "mo", "c_loaded x_loaded small_loaded bmod_loaded ident_loaded silu_done sums_done meansq_done rms_done "
                                          "rstd_done xn_done mod_done mod_kept modT_done wmod_loaded*3")
            with ExitStack() as ctx:
                phase_modulation(nc, g, ctx)
            phase_end(nc, g.mo)
            for which in range(2):
                g.qkv = phase_events(nc, f"qkv{which}", "w_loaded hT_turned hT_act hT_dve qk_done ss_done sq_done v_done v_kept ms_done rms_done "
                                                  "qk_kept qT_turned qT_kept rope_done pad_done rep_done")
                with ExitStack() as ctx:
                    phase_qkv(nc, g, ctx, which)
                phase_end(nc, g.qkv)
            g.na = phase_events(nc, "na", "zero_made zeroed bm_ready bm_used s_done exp_done max_done pt_turned pt_act pt_dve o_done o_kept br_turned bm_loaded*2")
            with ExitStack() as ctx:
                phase_na(nc, g, ctx)
            phase_end(nc, g.na)
            g.da = phase_events(nc, "da", "small_loaded high_done split_done dots_done lam_exp s_done*2 exp_done*2 max_done*2 pt_turned pt_kept "
                                          "a_done o_done o_kept ms_done rms_done y_done br_turned set_loaded*3")
            with ExitStack() as ctx:
                phase_da(nc, g, ctx)
            phase_end(nc, g.da)
        with ExitStack() as delta:
            a = lambda n, s, d=F32: delta.enter_context(nc.sbuf_tensor(n, s, d))
            g.gqT = g.brT[:, 6:8, :]
            g.gkT = a("gkT", [P, 2, 2, T])
            g.gk, g.gv = a("gk", [P, NT, BW]), a("gv", [P, NT, BW])
            g.gi = phase_events(nc, "gi", "cw_loaded proj_done padded conv_done pads_zero gkT_zero silu_done turned ss_done sq_done v_kept eps_added rms_done "
                              "qk_normed qkT_turned qkT_kept w_loaded*2")
            with ExitStack() as ctx:
                phase_gdn_inputs(nc, g, ctx)
            phase_end(nc, g.gi)
            g.gd = phase_events(nc, "gd", "loaded g_ready cum_done decays_ready gbig_ready sp_in ln_done beta_done z_done G_kept exps_done ms_done "
                              "rms_done y_done br_turned s_kept*2 o_kept*2 prods*2 a_ready*2 a_turned*2 lt_ready*2 d_ready*2 p_done*2 "
                              "p_kept*2 dt_ready*2 dt_first*2 dt_last*2 e_done*2 w_done*2 w_kept*2 v_done*2 v_kept*2 o_done*2 s_done*2 "
                              "x_ready*2 exp_done*2 at_kept*2 ops_ready*2")
            with ExitStack() as ctx:
                phase_gdn(nc, g, ctx)
            phase_end(nc, g.gd)
        g.fo = phase_events(nc, "fo", "w_loaded dft_used f_done f_kept z_done z_kept mod_loaded*3 spread_done mod_done mod_kept dft_loaded*2")
        with ExitStack() as ctx:
            phase_fourier(nc, g, ctx)
        phase_end(nc, g.fo)
        tokens_turned.close()
        tokens_low = ExitStack()
        g.h_low = tokens_low.enter_context(nc.sbuf_tensor("h_low", [P, KD, T], F32R))
        with ExitStack() as merged:
            g.yT = merged.enter_context(nc.sbuf_tensor("yT", [P, KD, S], F32))
            g.me = phase_events(nc, "me", "proj_done gate_in gate_done mult_done added h_high_done h_low_done w_high_done w_low_done wg_loaded*2 wb_loaded*3")
            with ExitStack() as ctx:
                phase_merge(nc, g, ctx)
            phase_end(nc, g.me)
            g.x1 = region[:, 0:NL * D].rearrange("p (t d) -> p t d", t=NL)
            g.h2 = g.hT[:, :, :].rearrange("p k t -> p (k t)")[:, 0:NL * D].rearrange("p (t d) -> p t d", t=NL)
            g.ou = phase_events(nc, "ou", "w_loaded x1_done x1_stored h2_done hT_act hT_dve turned logits scored y_read y_done sq_done ms_done "
                                    "rms_done x_loaded*2")
            with ExitStack() as ctx:
                phase_out(nc, g, ctx)
            phase_end(nc, g.ou)
        g.ro = phase_events(nc, "ro", "loaded dst_done scattered a_done counted mod_loaded*2 spread_done mod_done")
        with ExitStack() as ctx:
            phase_route(nc, g, ctx)
        phase_end(nc, g.ro)
        tokens_low.close()
        mid.close()
        g.ex = phase_events(nc, "ex", "zero_made x_free*2 g_free*2 u_free*2 d_free*2 xT_act*2 xT_dve*2 h_done*2 h_turned*2 hT_kept*2 silu_done*2 "
                                      "y_act*2 y_dve*2 x_loaded*2 g_loaded u_loaded d_loaded part_asked y_free*2")
        with ExitStack() as ctx:
            phase_experts(nc, g, ctx)
        phase_end(nc, g.ex)
        g.co = phase_events(nc, "co", "out_done y_loaded*4 x_loaded*4 stored*4")
        with ExitStack() as ctx:
            phase_combine(nc, g, ctx)


_INS = ["x", "c", "ctx", "c_ctx", "w_mod", "b_mod", "norm1_g", "norm2_g", "w_in", "na_qn_g", "na_kn_g", "na_rpb", "da_qn_g",
        "da_kn_g", "da_lam_q1", "da_lam_k1", "da_lam_q2", "da_lam_k2", "da_subln_g", "gdn_conv_w", "gdn_a_log",
        "gdn_dt_bias", "gdn_onorm_g", "w_branch", "w_out", "w_router", "router_bias", "moe_w_gate", "moe_w_up", "moe_w_down"]
_DEPTH = {"w_mod", "b_mod", "norm1_g", "norm2_g", "w_in", "na_qn_g", "na_kn_g", "na_rpb", "da_qn_g", "da_kn_g", "da_lam_q1",
          "da_lam_k1", "da_lam_q2", "da_lam_k2", "da_subln_g", "gdn_conv_w", "gdn_a_log", "gdn_dt_bias", "gdn_onorm_g",
          "w_branch", "w_out", "moe_w_gate", "moe_w_up", "moe_w_down"}


def shape_constants():
    f = np.float32
    i = np.arange(P)
    t = np.arange(S)
    k = {"ident": np.eye(P, dtype=f)}
    nf = DQ // 4
    freqs = (10000.0 ** (-np.arange(nf, dtype=f) / f(nf))).astype(f)
    ang = np.stack([(t // GRID_W).astype(f)[:, None] * freqs, (t % GRID_W).astype(f)[:, None] * freqs], axis=1)
    cos, sin = np.cos(ang), np.sin(ang)
    kc, ks = np.ones((T, 2, 2, nf), f), np.zeros((T, 2, 2, nf), f)
    kc[:S] = cos[:, :, None, :]
    ks[:S, :, 0], ks[:S, :, 1] = -sin, sin
    k["cos"], k["sin"] = kc.reshape(T, DQ), ks.reshape(T, DQ)
    m = np.full((NL, P, 10, GRID_W), NEG, f)
    for a in range(NL):
        kt = min(max(a - 2, 0), 3)
        for p in range(P):
            qr, qc = 2 * a + p // GRID_W, p % GRID_W
            r0 = min(max(qr - WIN_H // 2, 0), S // GRID_W - WIN_H)
            w0 = min(max(qc - WIN_W // 2, 0), GRID_W - WIN_W)
            m[a, p, r0 - 2 * kt:r0 - 2 * kt + WIN_H, w0:w0 + WIN_W] = 0
    k["namask"] = m[[0, 1, 2, 6, 7]].reshape(5, P, 640)
    k["cum"] = np.stack([(i[:, None] <= i[None, :]), (i[:, None] >= i[None, :])]).astype(f)
    lev = np.zeros((2, 7, P, P), f)
    for s in range(7):
        b = 1 << s
        same = (i[:, None] // (2 * b)) == (i[None, :] // (2 * b))
        low = (i[:, None] // b) > (i[None, :] // b)
        lev[0, s] = same & low
        lev[1, s] = (same & low).T
    k["lev"] = lev.reshape(14, P, P)
    tk = (t[:, None] * t[None, :]) % S
    k["dft"] = np.stack([np.cos(2 * np.pi * tk / S), np.sin(2 * np.pi * tk / S)]).astype(f)
    w = np.arange(HD)
    wk = (w[:, None] * w[None, :]) % HD
    bd = np.zeros((2, P, P), f)
    for b in range(2):
        q = slice(b * HD, (b + 1) * HD)
        bd[0, q, q] = np.cos(2 * np.pi * wk / HD) / 256
        bd[1, q, q] = -np.sin(2 * np.pi * wk / HD) / 256
    k["bdft"] = bd
    k["blk"] = np.arange(32, dtype=f)[None, :].repeat(P, 0)
    k["zeros"] = np.zeros((4, 24 * 128), f)
    return k


def kernel(**inputs):
    import concourse.bacc as bacc
    from concourse.bass_utils import run_bass_kernel_spmd as run

    nc = bacc.Bacc("TRN2", target_bir_lowering=False, num_devices=1)
    arrays, names = {}, {}
    for name in _INS:
        a = np.ascontiguousarray(inputs[name])
        if name in _DEPTH:
            a = a.reshape(a.shape[1:])
        arrays[name] = a
        names[name] = nc.dram_tensor(name, a.shape, F32, kind="ExternalInput").ap()
    cols = {"c_cols": np.stack([inputs["c"][0], inputs["c_ctx"]]).reshape(2, KD, P).transpose(2, 1, 0),
            "conv_cols": np.asarray(inputs["gdn_conv_w"]).reshape(CONV, 6, P).transpose(2, 1, 0),
            "norm1_cols": np.asarray(inputs["norm1_g"]).reshape(KD, P).T}
    for name, a in cols.items():
        arrays[name] = np.ascontiguousarray(a)
        names[name] = nc.dram_tensor(name, a.shape, F32, kind="ExternalInput").ap()
    for name, a in shape_constants().items():
        arrays["k_" + name] = a
        names["k_" + name] = nc.dram_tensor("k_" + name, a.shape, F32, kind="ExternalInput").ap()
    g = named(**names)
    g.out = nc.dram_tensor("out", (1, S, D), F32, kind="ExternalOutput").ap()
    trunk(nc, g)
    r = run(nc, [arrays], core_ids=[0])
    return r.results[0]["out"]
```
